# Optimizing a Trainium2 kernel written in Bass

```python
import math
import jax
import jax.numpy as jnp
from jax import lax
import numpy as np
import jax, jax.numpy as jnp

D_MODEL = 1024
BATCH = 1
SEQ = 256
DEPTH = 1

GRID_W = 64
CTX_LEN = 256
EPS = 1e-6

RET_HEADS = 4
RET_QK_DIM = 128
RET_V_DIM = 256
RET_QK_WIDTH = RET_HEADS * RET_QK_DIM
RET_V_WIDTH = RET_HEADS * RET_V_DIM
RET_CHUNK = 128
ROPE_BASE = 10000.0

HY_WIDTH = 512
HY_SHORT = 3
HY_POS_DIM = 33
HY_BANDS = (HY_POS_DIM - 1) // 2
HY_FFN = 64
HY_DECAY_TARGET = 1e-2
HY_FAST_PCT = 0.3
HY_SLOW_PCT = 1.5

N_GROUPS = 4
EXPERTS_PER_GROUP = 8
N_EXPERTS = N_GROUPS * EXPERTS_PER_GROUP
TOP_K = 2
EXPERT_HIDDEN = 512
MOE_BLOCK = 128

IN_WIDTH = 2 * RET_QK_WIDTH + 2 * RET_V_WIDTH + 3 * HY_WIDTH + 2 * D_MODEL
IN_SPLITS = (RET_QK_WIDTH, 2 * RET_QK_WIDTH, 2 * RET_QK_WIDTH + RET_V_WIDTH, 2 * RET_QK_WIDTH + 2 * RET_V_WIDTH, 2 * RET_QK_WIDTH + 2 * RET_V_WIDTH + 3 * HY_WIDTH, 2 * RET_QK_WIDTH + 2 * RET_V_WIDTH + 3 * HY_WIDTH + D_MODEL)


def rms_norm(x, gain=None):
    x32 = x.astype(jnp.float32)
    y = x32 * lax.rsqrt(jnp.mean(jnp.square(x32), axis=-1, keepdims=True) + EPS)
    if gain is not None:
        y = y * gain.astype(jnp.float32)
    return y.astype(x.dtype)

def modulate(h, shift, scale):
    return h * (1.0 + scale) + shift

def grid_rope_angles(n_tokens):
    rows = n_tokens // GRID_W
    r, col = jnp.meshgrid(jnp.arange(rows, dtype=jnp.float32), jnp.arange(GRID_W, dtype=jnp.float32), indexing='ij')
    n_freq = RET_QK_DIM // 4
    inv_freq = ROPE_BASE ** (-jnp.arange(n_freq, dtype=jnp.float32) / n_freq)
    return r.reshape(-1)[:, None] * inv_freq, col.reshape(-1)[:, None] * inv_freq

def rope_1d(x, ang):
    n_freq = ang.shape[-1]
    x1, x2 = x[..., :n_freq], x[..., n_freq:]
    cos, sin = jnp.cos(ang), jnp.sin(ang)
    return jnp.concatenate([x1 * cos - x2 * sin, x1 * sin + x2 * cos], axis=-1)

def rope_grid(x, ang_row, ang_col):
    half = RET_QK_DIM // 2
    return jnp.concatenate([rope_1d(x[..., :half], ang_row), rope_1d(x[..., half:], ang_col)], axis=-1)

def split_heads(t, n_heads):
    b, n, _ = t.shape
    return t.reshape(b, n, n_heads, -1).transpose(0, 2, 1, 3)

def retention_scan(q, k, v, log_g, s0, strict):
    b, h, n, _ = q.shape
    dv = v.shape[-1]
    n_chunks = n // RET_CHUNK
    pos = jnp.arange(RET_CHUNK, dtype=jnp.float32)
    diff = pos[:, None] - pos[None, :]
    mask = (diff > 0) if strict else (diff >= 0)
    lg = log_g[:, None, None]
    decay_in = jnp.where(mask[None], jnp.exp(lg * jnp.maximum(diff, 0.0)[None]), 0.0)
    decay_q = jnp.exp(lg * (pos + 1.0)[None, :, None])
    decay_k = jnp.exp(lg * (RET_CHUNK - 1.0 - pos)[None, :, None])
    decay_chunk = jnp.exp(lg * RET_CHUNK)

    def chunks(t):
        return t.reshape(b, h, n_chunks, RET_CHUNK, t.shape[-1]).transpose(2, 0, 1, 3, 4)

    def step(state, qkv):
        qc, kc, vc = qkv
        scores = jnp.einsum('bhid,bhjd->bhij', qc, kc) * decay_in
        out = jnp.einsum('bhij,bhjv->bhiv', scores, vc) + jnp.einsum('bhid,bhdv->bhiv', qc, state) * decay_q
        state = state * decay_chunk + jnp.einsum('bhjd,bhjv->bhdv', kc * decay_k, vc)
        return state, out

    s_final, o = lax.scan(step, s0, (chunks(q), chunks(k), chunks(v)))
    return o.transpose(1, 2, 0, 3, 4).reshape(b, h, n, dv), s_final

def retention_bidir(q, k, v, log_g, s0_fwd, s0_bwd):
    o_f, s_f = retention_scan(q, k, v, log_g[0], s0_fwd, False)
    o_b, s_b = retention_scan(jnp.flip(q, 2), jnp.flip(k, 2), jnp.flip(v, 2), log_g[1], s0_bwd, True)
    return o_f + jnp.flip(o_b, 2), s_f, s_b

def retention_readout(o, g):
    b, h, n, dv = o.shape
    o = rms_norm(o).transpose(0, 2, 1, 3).reshape(b, n, h * dv)
    return jax.nn.silu(g) * o.astype(g.dtype)

def short_conv(u, w, bias):
    n = u.shape[1]
    pad = HY_SHORT // 2
    up = jnp.pad(u, ((0, 0), (pad, pad), (0, 0)))
    return sum(up[:, j:j + n] * w[j] for j in range(HY_SHORT)) + bias

def hyena_filters(n, w1, b1, freq, w2, b2, w3):
    f32 = jnp.float32
    t = jnp.arange(n, dtype=f32) / n
    bands = jnp.linspace(1e-4, HY_BANDS - 1, HY_BANDS, dtype=f32)
    phase = 2.0 * math.pi * t[:, None] * bands[None, :]
    feats = jnp.concatenate([t[:, None], jnp.cos(phase), -jnp.sin(phase)], axis=-1)
    freq = freq.astype(f32)
    hid = jnp.sin(freq * (feats @ w1.astype(f32) + b1.astype(f32)))
    hid = jnp.sin(freq * (hid @ w2.astype(f32) + b2.astype(f32)))
    filt = hid @ w3.astype(f32)
    slow = abs(math.log(HY_DECAY_TARGET)) / HY_SLOW_PCT
    fast = abs(math.log(HY_DECAY_TARGET)) / HY_FAST_PCT
    deltas = jnp.tile(jnp.linspace(slow, fast, HY_WIDTH, dtype=f32), 2)
    filt = filt * jnp.exp(-t[:, None] * deltas[None, :])
    filt = filt / jnp.sum(jnp.abs(filt), axis=0, keepdims=True)
    return filt[:, :HY_WIDTH], filt[:, HY_WIDTH:]

def long_conv_bidir(z, h_fwd, h_bwd):
    n = z.shape[1]
    nfft = 2 * n
    zf = jnp.fft.rfft(z.astype(jnp.float32), n=nfft, axis=1)
    hf = jnp.fft.rfft(h_fwd, n=nfft, axis=0) + jnp.conj(jnp.fft.rfft(h_bwd, n=nfft, axis=0))
    return jnp.fft.irfft(zf * hf[None], n=nfft, axis=1)[:, :n]

def hyena_branch(u, conv_w, conv_b, ffn_w1, ffn_b1, ffn_freq, ffn_w2, ffn_b2, ffn_w3, skip):
    x0, x1, v = jnp.split(short_conv(u, conv_w, conv_b), 3, axis=-1)
    z = x1 * v
    h_fwd, h_bwd = hyena_filters(u.shape[1], ffn_w1, ffn_b1, ffn_freq, ffn_w2, ffn_b2, ffn_w3)
    y = long_conv_bidir(z, h_fwd, h_bwd).astype(u.dtype) + z * skip
    return x0 * y

def merge_branches(ret_gated, hy_out, gate_ret, gate_hy, ret_w_o, hy_w_o, w_out):
    mixed = jax.nn.sigmoid(gate_ret) * (ret_gated @ ret_w_o) + jax.nn.sigmoid(gate_hy) * (hy_out @ hy_w_o)
    return mixed @ w_out

def moe_ffn(u, rg_w, rg_b, re_w, re_b, w1, w3, w2):
    n_tok = u.shape[0]
    f32 = jnp.float32
    group_p = jax.nn.softmax((u @ rg_w).astype(f32) + rg_b.astype(f32), axis=-1)
    p_star, g_star = lax.top_k(group_p, 1)
    expert_logits = ((u @ re_w).astype(f32) + re_b.astype(f32)).reshape(n_tok, N_GROUPS, EXPERTS_PER_GROUP)
    in_group = jnp.take_along_axis(expert_logits, g_star[:, :, None], axis=1)[:, 0]
    w_top, e_top = lax.top_k(jax.nn.softmax(in_group, axis=-1), TOP_K)
    weights = p_star * w_top / jnp.sum(w_top, axis=-1, keepdims=True)
    expert_id = g_star * EXPERTS_PER_GROUP + e_top
    n_assign = n_tok * TOP_K
    flat_e = expert_id.reshape(n_assign)
    flat_tok = jnp.arange(n_assign, dtype=jnp.int32) // TOP_K
    flat_w = weights.reshape(n_assign)
    order = jnp.argsort(flat_e)
    se, stok, sw = flat_e[order], flat_tok[order], flat_w[order]
    counts = jnp.bincount(flat_e, length=N_EXPERTS)
    starts = jnp.cumsum(counts) - counts
    padded = (counts + MOE_BLOCK - 1) // MOE_BLOCK * MOE_BLOCK
    padded_end = jnp.cumsum(padded)
    padded_start = padded_end - padded
    dest = padded_start[se] + jnp.arange(n_assign, dtype=jnp.int32) - starts[se]
    n_blocks = -(-(n_assign + N_EXPERTS * (MOE_BLOCK - 1)) // MOE_BLOCK)
    n_rows = n_blocks * MOE_BLOCK
    row_tok = jnp.zeros((n_rows,), jnp.int32).at[dest].set(stok)
    block_expert = jnp.minimum(jnp.searchsorted(padded_end, jnp.arange(n_blocks, dtype=jnp.int32) * MOE_BLOCK, side='right'), N_EXPERTS - 1)
    xb = u[row_tok].reshape(n_blocks, MOE_BLOCK, u.shape[1])

    def expert_block(args):
        xblk, e = args
        return (jax.nn.silu(xblk @ w1[e]) * (xblk @ w3[e])) @ w2[e]

    yb = lax.map(expert_block, (xb, block_expert)).reshape(n_rows, u.shape[1])
    y = yb[dest] * sw[:, None].astype(u.dtype)
    return jax.ops.segment_sum(y, stok, num_segments=n_tok)

def first_inputs(seed: int = 0) -> dict:
    key = jax.random.key(seed)
    ks = jax.random.split(key, 32)
    f32 = jnp.float32

    def nrm(k, shape, scale):
        return scale * jax.random.normal(k, shape, f32)

    base_logit = np.log(2.0 ** (5 + np.arange(RET_HEADS)) - 1.0).astype(np.float32)
    return {
        'x': nrm(ks[0], (BATCH, SEQ, D_MODEL), 1.0),
        'c': nrm(ks[1], (BATCH, D_MODEL), 1.0),
        'ctx': nrm(ks[2], (BATCH, CTX_LEN, D_MODEL), 1.0),
        'c_ctx': nrm(ks[3], (D_MODEL,), 1.0),
        'ada_w': nrm(ks[4], (DEPTH, D_MODEL, 6 * D_MODEL), 0.5 * D_MODEL ** -0.5),
        'ada_b': nrm(ks[5], (DEPTH, 6 * D_MODEL), 0.02),
        'norm1_g': 1.0 + nrm(ks[6], (DEPTH, D_MODEL), 0.05),
        'norm2_g': 1.0 + nrm(ks[7], (DEPTH, D_MODEL), 0.05),
        'w_in': nrm(ks[8], (DEPTH, D_MODEL, IN_WIDTH), D_MODEL ** -0.5),
        'b_in': nrm(ks[9], (DEPTH, IN_WIDTH), 0.02),
        'ret_decay_logit': jnp.asarray(base_logit)[None, None, :] + nrm(ks[10], (DEPTH, 2, RET_HEADS), 0.1),
        'ret_w_o': nrm(ks[11], (DEPTH, RET_V_WIDTH, D_MODEL), RET_V_WIDTH ** -0.5),
        'hy_conv_w': nrm(ks[12], (DEPTH, HY_SHORT, 3 * HY_WIDTH), HY_SHORT ** -0.5),
        'hy_conv_b': nrm(ks[13], (DEPTH, 3 * HY_WIDTH), 0.02),
        'hy_ffn_w1': nrm(ks[14], (DEPTH, HY_POS_DIM, HY_FFN), HY_POS_DIM ** -0.5),
        'hy_ffn_b1': nrm(ks[15], (DEPTH, HY_FFN), 0.02),
        'hy_ffn_freq': 1.0 + nrm(ks[16], (DEPTH, HY_FFN), 0.05),
        'hy_ffn_w2': nrm(ks[17], (DEPTH, HY_FFN, HY_FFN), HY_FFN ** -0.5),
        'hy_ffn_b2': nrm(ks[18], (DEPTH, HY_FFN), 0.02),
        'hy_ffn_w3': nrm(ks[19], (DEPTH, HY_FFN, 2 * HY_WIDTH), HY_FFN ** -0.5),
        'hy_skip': nrm(ks[20], (DEPTH, HY_WIDTH), 0.5),
        'hy_w_o': nrm(ks[21], (DEPTH, HY_WIDTH, D_MODEL), HY_WIDTH ** -0.5),
        'w_out': nrm(ks[22], (DEPTH, D_MODEL, D_MODEL), D_MODEL ** -0.5),
        'router_group_w': nrm(ks[23], (DEPTH, D_MODEL, N_GROUPS), D_MODEL ** -0.5),
        'router_group_b': nrm(ks[24], (DEPTH, N_GROUPS), 0.01),
        'router_expert_w': nrm(ks[25], (DEPTH, D_MODEL, N_EXPERTS), D_MODEL ** -0.5),
        'router_expert_b': nrm(ks[26], (DEPTH, N_EXPERTS), 0.01),
        'expert_w1': nrm(ks[27], (DEPTH, N_EXPERTS, D_MODEL, EXPERT_HIDDEN), D_MODEL ** -0.5),
        'expert_w3': nrm(ks[28], (DEPTH, N_EXPERTS, D_MODEL, EXPERT_HIDDEN), D_MODEL ** -0.5),
        'expert_w2': nrm(ks[29], (DEPTH, N_EXPERTS, EXPERT_HIDDEN, D_MODEL), EXPERT_HIDDEN ** -0.5),
        'final_norm_g': 1.0 + nrm(ks[30], (D_MODEL,), 0.05),
    }

def first_block(x, c, ctx, c_ctx, ada_w, ada_b, norm1_g, norm2_g, w_in, b_in, ret_decay_logit, ret_w_o, hy_conv_w, hy_conv_b, hy_ffn_w1, hy_ffn_b1, hy_ffn_freq, hy_ffn_w2, hy_ffn_b2, hy_ffn_w3, hy_skip, hy_w_o, w_out, router_group_w, router_group_b, router_expert_w, router_expert_b, expert_w1, expert_w3, expert_w2, final_norm_g):
    f32 = jnp.float32
    batch, n_tokens = x.shape[0], x.shape[1]
    ang_row, ang_col = grid_rope_angles(n_tokens)
    silu_c = jax.nn.silu(c)
    silu_cc = jax.nn.silu(c_ctx)
    k_scale = RET_QK_DIM ** -0.5
    for layer in range(DEPTH):
        last = layer == DEPTH - 1
        sh1, sc1, gt1, sh2, sc2, gt2 = jnp.split((silu_c @ ada_w[layer] + ada_b[layer])[:, None, :], 6, axis=-1)
        csh1, csc1, cgt1, csh2, csc2, cgt2 = jnp.split(silu_cc @ ada_w[layer] + ada_b[layer], 6, axis=-1)
        h = modulate(rms_norm(x, norm1_g[layer]), sh1, sc1)
        hc = modulate(rms_norm(ctx, norm1_g[layer]), csh1, csc1)
        q, k, v, g, hy_u, gate_ret, gate_hy = jnp.split(h @ w_in[layer] + b_in[layer], IN_SPLITS, axis=-1)
        qc, kc, vc, gc, hyc_u, gate_ret_c, gate_hy_c = jnp.split(hc @ w_in[layer] + b_in[layer], IN_SPLITS, axis=-1)
        log_g = jax.nn.log_sigmoid(ret_decay_logit[layer].astype(f32))
        zero_state = jnp.zeros((batch, RET_HEADS, RET_QK_DIM, RET_V_DIM), f32)
        o_ctx, s_fwd, s_bwd = retention_bidir(split_heads(qc, RET_HEADS).astype(f32), split_heads(kc, RET_HEADS).astype(f32) * k_scale, split_heads(vc, RET_HEADS).astype(f32), log_g, zero_state, zero_state)
        q_h = rope_grid(split_heads(q, RET_HEADS).astype(f32), ang_row, ang_col)
        k_h = rope_grid(split_heads(k, RET_HEADS).astype(f32), ang_row, ang_col) * k_scale
        o_lat, _, _ = retention_bidir(q_h, k_h, split_heads(v, RET_HEADS).astype(f32), log_g, s_fwd, s_bwd)
        hy_args = (hy_conv_w[layer], hy_conv_b[layer], hy_ffn_w1[layer], hy_ffn_b1[layer], hy_ffn_freq[layer], hy_ffn_w2[layer], hy_ffn_b2[layer], hy_ffn_w3[layer], hy_skip[layer])
        out_args = (ret_w_o[layer], hy_w_o[layer], w_out[layer])
        moe_args = (router_group_w[layer], router_group_b[layer], router_expert_w[layer], router_expert_b[layer], expert_w1[layer], expert_w3[layer], expert_w2[layer])
        mix = merge_branches(retention_readout(o_lat, g), hyena_branch(hy_u, *hy_args), gate_ret, gate_hy, *out_args)
        x = x + gt1 * mix
        h2 = modulate(rms_norm(x, norm2_g[layer]), sh2, sc2)
        if last:
            x = x + gt2 * moe_ffn(h2.reshape(-1, D_MODEL), *moe_args).reshape(x.shape)
        else:
            mix_c = merge_branches(retention_readout(o_ctx, gc), hyena_branch(hyc_u, *hy_args), gate_ret_c, gate_hy_c, *out_args)
            ctx = ctx + cgt1 * mix_c
            h2c = modulate(rms_norm(ctx, norm2_g[layer]), csh2, csc2)
            y = moe_ffn(jnp.concatenate([h2.reshape(-1, D_MODEL), h2c.reshape(-1, D_MODEL)], axis=0), *moe_args)
            n_lat = batch * n_tokens
            x = x + gt2 * y[:n_lat].reshape(x.shape)
            ctx = ctx + cgt2 * y[n_lat:].reshape(ctx.shape)
    return rms_norm(x, final_norm_g)


DEPTH_2 = 2

GROUP_W = D_MODEL // N_GROUPS
HEAD_DIM = 64
N_HEADS = GROUP_W // HEAD_DIM
NA_WIN_ROWS = 8
NA_WIN_COLS = 16
SGU_CHUNK = 128
DIFF_QK_DIM = HEAD_DIM // 2
D_FF = 4 * D_MODEL
Q_BLOCK = 128
COL_FOURIER = 0
COL_NA = GROUP_W
COL_SGU = 4 * GROUP_W
COL_DIFF = 6 * GROUP_W
D_IN = 9 * GROUP_W


def rms_norm_2(x, g):
    x32 = x.astype(jnp.float32)
    y = x32 * lax.rsqrt(jnp.mean(x32 * x32, axis=-1, keepdims=True) + EPS)
    return (y * g.astype(jnp.float32)).astype(x.dtype)

def layer_norm(x, g, b):
    x32 = x.astype(jnp.float32)
    mu = jnp.mean(x32, axis=-1, keepdims=True)
    var = jnp.mean(jnp.square(x32 - mu), axis=-1, keepdims=True)
    y = (x32 - mu) * lax.rsqrt(var + EPS)
    return (y * g.astype(jnp.float32) + b.astype(jnp.float32)).astype(x.dtype)

def ada_params(cond, w, b):
    m = jax.nn.silu(cond) @ w + b
    return jnp.split(m, 6, axis=-1)

def modulate_2(h, shift, scale):
    return h * (1 + scale) + shift

def heads(t):
    return t.reshape(t.shape[0], t.shape[1], N_HEADS, HEAD_DIM)

def fourier_mix(a):
    bsz, n, _ = a.shape
    a4 = a.astype(jnp.float32).reshape(bsz, n, N_HEADS, GROUP_W // N_HEADS)
    f = jnp.fft.fft2(a4, axes=(1, 3), norm="ortho").real
    return f.reshape(bsz, n, GROUP_W).astype(a.dtype)

def dense_attention(q, k, v):
    s = jnp.einsum('bqhd,bkhd->bhqk', q, k).astype(jnp.float32) * (q.shape[-1] ** -0.5)
    p = jax.nn.softmax(s, axis=-1).astype(v.dtype)
    return jnp.einsum('bhqk,bkhd->bqhd', p, v)

def neighbourhood_attention(q, k, v, k_ctx, v_ctx, rpb, rows):
    bsz, n, h, dh = q.shape
    wr = min(NA_WIN_ROWS, rows)
    qg = q.reshape(bsz, rows, GRID_W, h, dh)
    kg = k.reshape(bsz, rows, GRID_W, h, dh)
    vg = v.reshape(bsz, rows, GRID_W, h, dh)
    r = jnp.arange(rows)
    row_start = jnp.clip(r - wr // 2, 0, rows - wr)
    key_rows = row_start[:, None] + jnp.arange(wr)[None, :]
    k_band = kg[:, key_rows]
    v_band = vg[:, key_rows]
    cidx = jnp.arange(GRID_W)
    col_start = jnp.clip(cidx - NA_WIN_COLS // 2, 0, GRID_W - NA_WIN_COLS)
    in_win = (cidx[None, :] >= col_start[:, None]) & (cidx[None, :] < col_start[:, None] + NA_WIN_COLS)
    dr = key_rows - r[:, None] + NA_WIN_ROWS - 1
    dc = jnp.clip(cidx[None, :] - cidx[:, None], 1 - NA_WIN_COLS, NA_WIN_COLS - 1) + NA_WIN_COLS - 1
    bias = rpb[:, dr[:, None, :, None], dc[None, :, None, :]]
    scale = dh ** -0.5
    s_loc = jnp.einsum('brqhd,brikhd->bhrqik', qg, k_band).astype(jnp.float32) * scale + bias.astype(jnp.float32)
    s_loc = jnp.where(in_win[:, None, :], s_loc, -jnp.inf)
    s_loc = s_loc.reshape(bsz, h, rows, GRID_W, wr * GRID_W)
    s_ctx = jnp.einsum('brqhd,blhd->bhrql', qg, k_ctx).astype(jnp.float32) * scale
    p = jax.nn.softmax(jnp.concatenate([s_loc, s_ctx], axis=-1), axis=-1).astype(v.dtype)
    p_loc = p[..., :wr * GRID_W].reshape(bsz, h, rows, GRID_W, wr, GRID_W)
    p_ctx = p[..., wr * GRID_W:]
    o = jnp.einsum('bhrqik,brikhd->brqhd', p_loc, v_band) + jnp.einsum('bhrql,blhd->brqhd', p_ctx, v_ctx)
    return o.reshape(bsz, n, h * dh)

def spatial_gating(uv, ln_g, ln_b, w_s, b_s):
    bsz, n, _ = uv.shape
    u, v = jnp.split(jax.nn.gelu(uv), 2, axis=-1)
    v = layer_norm(v, ln_g, ln_b)
    vc = v.reshape(bsz, n // SGU_CHUNK, SGU_CHUNK, N_HEADS, GROUP_W // N_HEADS)
    s = jnp.einsum('gpq,bnqgc->bnpgc', w_s, vc) + b_s.T[None, None, :, :, None]
    return u * s.reshape(bsz, n, GROUP_W)

def axial_rope(n):
    t = jnp.arange(n)
    rows = (t // GRID_W).astype(jnp.float32)
    cols = (t % GRID_W).astype(jnp.float32)
    n_freq = DIFF_QK_DIM // 4
    inv = ROPE_BASE ** (-jnp.arange(n_freq, dtype=jnp.float32) / n_freq)
    ang = jnp.concatenate([rows[:, None] * inv, cols[:, None] * inv], axis=-1)
    return jnp.cos(ang), jnp.sin(ang)

def apply_rope(x, cos, sin):
    nf = DIFF_QK_DIM // 4
    xs = x.reshape(x.shape[:-1] + (2, 2, nf))
    x1, x2 = xs[..., 0, :], xs[..., 1, :]
    c = cos.reshape(cos.shape[0], 1, 2, nf).astype(x.dtype)
    s = sin.reshape(sin.shape[0], 1, 2, nf).astype(x.dtype)
    out = jnp.stack([x1 * c - x2 * s, x1 * s + x2 * c], axis=-2)
    return out.reshape(x.shape)

def diff_attend(q1, q2, k1, k2, v, lam):
    scale = DIFF_QK_DIM ** -0.5
    s1 = jnp.einsum('bqhd,bkhd->bhqk', q1, k1).astype(jnp.float32) * scale
    s2 = jnp.einsum('bqhd,bkhd->bhqk', q2, k2).astype(jnp.float32) * scale
    p = jax.nn.softmax(s1, axis=-1) - lam * jax.nn.softmax(s2, axis=-1)
    return jnp.einsum('bhqk,bkhd->bqhd', p.astype(v.dtype), v)

def diff_latent(q, k, v, k_ctx, v_ctx, lam, cos, sin):
    bsz, n, h, _ = q.shape
    q1 = apply_rope(q[..., :DIFF_QK_DIM], cos, sin)
    q2 = apply_rope(q[..., DIFF_QK_DIM:], cos, sin)
    k1 = jnp.concatenate([apply_rope(k[..., :DIFF_QK_DIM], cos, sin), k_ctx[..., :DIFF_QK_DIM]], axis=1)
    k2 = jnp.concatenate([apply_rope(k[..., DIFF_QK_DIM:], cos, sin), k_ctx[..., DIFF_QK_DIM:]], axis=1)
    v_all = jnp.concatenate([v, v_ctx], axis=1)
    nb = n // Q_BLOCK

    def to_blocks(t):
        return t.reshape(bsz, nb, Q_BLOCK, h, DIFF_QK_DIM).swapaxes(0, 1)

    o = lax.map(lambda qb: diff_attend(qb[0], qb[1], k1, k2, v_all, lam), (to_blocks(q1), to_blocks(q2)))
    return o.swapaxes(0, 1).reshape(bsz, n, h, HEAD_DIM)

def diff_post(o, g, lam_init):
    y = rms_norm_2(o, g) * (1 - lam_init)
    return y.reshape(o.shape[0], o.shape[1], GROUP_W)

def sq_relu_mlp(h, w1, w2):
    return jnp.square(jax.nn.relu(h @ w1)) @ w2

def second_inputs(seed: int = 0) -> dict:
    key = jax.random.key(seed)
    ks = jax.random.split(key, 24)
    f32 = jnp.float32

    def nrm(k, shape, s):
        return jax.random.normal(k, shape, f32) * s

    return {
        "x": nrm(ks[0], (BATCH, SEQ, D_MODEL), 1.0),
        "c": nrm(ks[1], (BATCH, D_MODEL), 1.0),
        "ctx": nrm(ks[2], (BATCH, CTX_LEN, D_MODEL), 1.0),
        "c_ctx": nrm(ks[3], (D_MODEL,), 1.0),
        "ada_w": nrm(ks[4], (DEPTH_2, D_MODEL, 6 * D_MODEL), 0.5 * D_MODEL ** -0.5),
        "ada_b": nrm(ks[5], (DEPTH_2, 6 * D_MODEL), 0.01),
        "norm1_g": 1.0 + nrm(ks[6], (DEPTH_2, D_MODEL), 0.02),
        "norm2_g": 1.0 + nrm(ks[7], (DEPTH_2, D_MODEL), 0.02),
        "w_in": nrm(ks[8], (DEPTH_2, D_MODEL, D_IN), D_MODEL ** -0.5),
        "w_out": nrm(ks[9], (DEPTH_2, D_MODEL, D_MODEL), D_MODEL ** -0.5),
        "na_rpb": nrm(ks[10], (DEPTH_2, N_HEADS, 2 * NA_WIN_ROWS - 1, 2 * NA_WIN_COLS - 1), 0.1),
        "sgu_ln_g": 1.0 + nrm(ks[11], (DEPTH_2, GROUP_W), 0.02),
        "sgu_ln_b": nrm(ks[12], (DEPTH_2, GROUP_W), 0.02),
        "sgu_w": nrm(ks[13], (DEPTH_2, N_HEADS, SGU_CHUNK, SGU_CHUNK), SGU_CHUNK ** -0.5),
        "sgu_b": 1.0 + nrm(ks[14], (DEPTH_2, N_HEADS, SGU_CHUNK), 0.02),
        "diff_lq1": nrm(ks[15], (DEPTH_2, DIFF_QK_DIM), 0.1),
        "diff_lk1": nrm(ks[16], (DEPTH_2, DIFF_QK_DIM), 0.1),
        "diff_lq2": nrm(ks[17], (DEPTH_2, DIFF_QK_DIM), 0.1),
        "diff_lk2": nrm(ks[18], (DEPTH_2, DIFF_QK_DIM), 0.1),
        "diff_subln_g": 1.0 + nrm(ks[19], (DEPTH_2, HEAD_DIM), 0.02),
        "w_ff1": nrm(ks[20], (DEPTH_2, D_MODEL, D_FF), D_MODEL ** -0.5),
        "w_ff2": nrm(ks[21], (DEPTH_2, D_FF, D_MODEL), D_FF ** -0.5),
        "final_g": 1.0 + nrm(ks[22], (D_MODEL,), 0.02),
    }

def second_block(x, c, ctx, c_ctx, ada_w, ada_b, norm1_g, norm2_g, w_in, w_out, na_rpb, sgu_ln_g, sgu_ln_b,
              sgu_w, sgu_b, diff_lq1, diff_lk1, diff_lq2, diff_lk2, diff_subln_g, w_ff1, w_ff2, final_g):
    bsz, n, _ = x.shape
    rows = n // GRID_W
    cos, sin = axial_rope(n)
    cx = ctx
    gw = GROUP_W
    for l in range(DEPTH_2):
        last = l == DEPTH_2 - 1
        sh1, sc1, g1, sh2, sc2, g2 = ada_params(c[:, None, :], ada_w[l], ada_b[l])
        csh1, csc1, cg1, csh2, csc2, cg2 = ada_params(c_ctx[None, None, :], ada_w[l], ada_b[l])
        h = modulate_2(rms_norm_2(x, norm1_g[l]), sh1, sc1)
        hc = modulate_2(rms_norm_2(cx, norm1_g[l]), csh1, csc1)
        w = w_in[l]
        p = h @ w
        if last:
            na_kv_c = hc @ w[:, COL_NA + gw:COL_NA + 3 * gw]
            df_kv_c = hc @ w[:, COL_DIFF + gw:COL_DIFF + 3 * gw]
        else:
            pc = hc @ w
            na_kv_c = pc[..., COL_NA + gw:COL_NA + 3 * gw]
            df_kv_c = pc[..., COL_DIFF + gw:COL_DIFF + 3 * gw]
        na_kc, na_vc = heads(na_kv_c[..., :gw]), heads(na_kv_c[..., gw:])
        df_kc, df_vc = heads(df_kv_c[..., :gw]), heads(df_kv_c[..., gw:])
        lam_init = 0.8 - 0.6 * math.exp(-0.3 * l)
        lam = (jnp.exp(jnp.sum(diff_lq1[l].astype(jnp.float32) * diff_lk1[l].astype(jnp.float32)))
               - jnp.exp(jnp.sum(diff_lq2[l].astype(jnp.float32) * diff_lk2[l].astype(jnp.float32))) + lam_init)

        y_a = fourier_mix(p[..., COL_FOURIER:COL_FOURIER + gw])
        y_b = neighbourhood_attention(heads(p[..., COL_NA:COL_NA + gw]), heads(p[..., COL_NA + gw:COL_NA + 2 * gw]),
                                      heads(p[..., COL_NA + 2 * gw:COL_NA + 3 * gw]), na_kc, na_vc, na_rpb[l], rows)
        y_c = spatial_gating(p[..., COL_SGU:COL_SGU + 2 * gw], sgu_ln_g[l], sgu_ln_b[l], sgu_w[l], sgu_b[l])
        o_d = diff_latent(heads(p[..., COL_DIFF:COL_DIFF + gw]), heads(p[..., COL_DIFF + gw:COL_DIFF + 2 * gw]),
                          heads(p[..., COL_DIFF + 2 * gw:COL_DIFF + 3 * gw]), df_kc, df_vc, lam, cos, sin)
        y_d = diff_post(o_d, diff_subln_g[l], lam_init)
        y = jnp.concatenate([y_a, y_b, y_c, y_d], axis=-1) @ w_out[l]

        if not last:
            yc_a = fourier_mix(pc[..., COL_FOURIER:COL_FOURIER + gw])
            yc_b = dense_attention(heads(pc[..., COL_NA:COL_NA + gw]), na_kc, na_vc).reshape(bsz, -1, gw)
            yc_c = spatial_gating(pc[..., COL_SGU:COL_SGU + 2 * gw], sgu_ln_g[l], sgu_ln_b[l], sgu_w[l], sgu_b[l])
            qc = heads(pc[..., COL_DIFF:COL_DIFF + gw])
            oc_d = diff_attend(qc[..., :DIFF_QK_DIM], qc[..., DIFF_QK_DIM:], df_kc[..., :DIFF_QK_DIM],
                               df_kc[..., DIFF_QK_DIM:], df_vc, lam)
            yc_d = diff_post(oc_d, diff_subln_g[l], lam_init)
            yc = jnp.concatenate([yc_a, yc_b, yc_c, yc_d], axis=-1) @ w_out[l]
            cx = cx + cg1 * yc
            hc2 = modulate_2(rms_norm_2(cx, norm2_g[l]), csh2, csc2)
            cx = cx + cg2 * sq_relu_mlp(hc2, w_ff1[l], w_ff2[l])

        x = x + g1 * y
        h2 = modulate_2(rms_norm_2(x, norm2_g[l]), sh2, sc2)
        x = x + g2 * sq_relu_mlp(h2, w_ff1[l], w_ff2[l])
    return rms_norm_2(x, final_g)


def setup_inputs(seed=0):
    out = dict(first_inputs(seed))
    for name, value in second_inputs(seed + 1).items():
        if name != "x":
            out[name + "_2"] = value
    return out


def reference(
    x, c, ctx, c_ctx, ada_w, ada_b, norm1_g, norm2_g, w_in, b_in, ret_decay_logit, ret_w_o,
    hy_conv_w, hy_conv_b, hy_ffn_w1, hy_ffn_b1, hy_ffn_freq, hy_ffn_w2, hy_ffn_b2, hy_ffn_w3,
    hy_skip, hy_w_o, w_out, router_group_w, router_group_b, router_expert_w, router_expert_b,
    expert_w1, expert_w3, expert_w2, final_norm_g, c_2, ctx_2, c_ctx_2, ada_w_2, ada_b_2,
    norm1_g_2, norm2_g_2, w_in_2, w_out_2, na_rpb_2, sgu_ln_g_2, sgu_ln_b_2, sgu_w_2, sgu_b_2,
    diff_lq1_2, diff_lk1_2, diff_lq2_2, diff_lk2_2, diff_subln_g_2, w_ff1_2, w_ff2_2, final_g_2,
):
    x = first_block(
        x, c, ctx, c_ctx, ada_w, ada_b, norm1_g, norm2_g, w_in, b_in, ret_decay_logit, ret_w_o,
        hy_conv_w, hy_conv_b, hy_ffn_w1, hy_ffn_b1, hy_ffn_freq, hy_ffn_w2, hy_ffn_b2,
        hy_ffn_w3, hy_skip, hy_w_o, w_out, router_group_w, router_group_b, router_expert_w,
        router_expert_b, expert_w1, expert_w3, expert_w2, final_norm_g,
    )
    return second_block(
        x, c_2, ctx_2, c_ctx_2, ada_w_2, ada_b_2, norm1_g_2, norm2_g_2, w_in_2, w_out_2,
        na_rpb_2, sgu_ln_g_2, sgu_ln_b_2, sgu_w_2, sgu_b_2, diff_lq1_2, diff_lk1_2, diff_lq2_2,
        diff_lk2_2, diff_subln_g_2, w_ff1_2, w_ff2_2, final_g_2,
    )


_drawn_inputs = setup_inputs


def setup_inputs(seed=0):
    import zlib

    import numpy as np

    out = dict(_drawn_inputs(seed))
    spreads = {}
    factors = {'norm1_g': 3.118,
     'norm2_g': 2.702,
     'b_in': 4.908,
     'hy_conv_b': 6.227,
     'hy_ffn_b1': 8.0,
     'hy_ffn_freq': 7.681,
     'hy_ffn_b2': 8.0,
     'router_group_b': 8.0,
     'router_expert_b': 7.102,
     'norm1_g_2': 8.0,
     'norm2_g_2': 4.669,
     'na_rpb_2': 59.807,
     'sgu_ln_g_2': 8.0,
     'sgu_ln_b_2': 8.0,
     'sgu_b_2': 8.0,
     'diff_lq1_2': 8.0,
     'diff_lk1_2': 8.0,
     'diff_lq2_2': 8.0,
     'diff_lk2_2': 8.0,
     'diff_subln_g_2': 64.0,
     'final_g_2': 9.064}
    for name, (base, spread) in spreads.items():
        noise = np.random.default_rng([zlib.crc32(name.encode()), seed]).standard_normal(out[name].shape)
        drawn = base * np.exp(spread * noise) if base else spread * noise
        out[name] = jnp.asarray(drawn.astype(out[name].dtype))
    for name, factor in factors.items():
        out[name] = (out[name] * factor).astype(out[name].dtype)
    return out
```

```python
import math
from contextlib import ExitStack

import numpy as np

import concourse.bass as bass
from concourse import mybir
from concourse.alu_op_type import AluOpType as ALU

F32 = mybir.dt.float32
I32 = mybir.dt.int32
ACT = mybir.ActivationFunctionType
AX = mybir.AxisListType

EPS = 1e-6
NEG = -1.0e30
NRING = 8


def _rope(n_freq):
    t = np.arange(256)
    inv = (10000.0 ** (-np.arange(n_freq, dtype=np.float32) / np.float32(n_freq))).astype(np.float32)
    row = (t // 64).astype(np.float32)[None, :] * inv[:, None]
    col = (t % 64).astype(np.float32)[None, :] * inv[:, None]
    return np.cos(row), np.sin(row), np.cos(col), np.sin(col)


def _swap(n, width):
    m = np.zeros((n, n), np.float32)
    for b in range(0, n, 2 * width):
        for i in range(width):
            m[b + width + i, b + i] = -1.0
            m[b + i, b + width + i] = 1.0
    return m


def constants():
    f = np.float32
    c = {}
    p = np.arange(128)
    c["k_eye"] = np.stack([np.eye(128), p[:, None] < p[None, :], np.ones((128, 128)), np.eye(128)[::-1]], 1).astype(f)
    small = np.zeros((128, 288), f)
    small[:, 0:32] = np.arange(32)
    small[:, 32] = EPS
    for v in range(4):
        small[32 * v:32 * v + 32, 40 + v] = 32.0 ** -0.5
    for v in range(2):
        small[64 * v:64 * v + 64, 48 + v] = 0.125
    j = (np.arange(2)[None, :] * 128 + p[:, None]).astype(f)
    small[:, 50:52] = 255 - j
    small[:, 52:54] = j
    small[:, 54:56] = j + 1
    small[:, 56:58] = 256 - j
    small[:, 64:288] = np.arange(32, 256)
    c["k_small"] = small
    i = np.arange(256)
    jj = j[:, :, None]
    c["k_ret"] = np.concatenate([np.maximum(i[None, None, :] - jj, 0).reshape(128, 512),
                                 np.maximum(jj - i[None, None, :], 0).reshape(128, 512)], 1).astype(f)
    cr, sr, cc, sc = _rope(32)
    c["k_rope"] = np.concatenate([np.concatenate([cr, cr, cc, cc], 0), np.concatenate([sr, sr, sc, sc], 0), _swap(128, 32)], 1).astype(f)
    cr, sr, cc, sc = _rope(8)
    c["k_rope2"] = np.concatenate([np.tile(np.concatenate([cr, cr, cc, cc], 0), (4, 1)),
                                   np.tile(np.concatenate([sr, sr, sc, sc], 0), (4, 1)), _swap(128, 8)], 1).astype(f)
    t = np.arange(256, dtype=np.float64)
    ang = 2 * np.pi * (np.outer(t, t) % 512) / 512
    co, si = np.cos(ang), np.sin(ang)
    alt = (-1.0) ** t
    si1, co1 = si.copy(), co.copy()
    si1[:, 0] = alt
    co1[:, 0] = alt
    blocks = [co[:, :128], co[:, 128:], si[:, :128], si[:, 128:], si1[:, :128], co1[:, :128]]
    fw = np.stack([b.reshape(2, 128, 128) for b in blocks], 0)
    c["k_dft"] = fw.transpose(2, 0, 1, 3).reshape(128, 1536).astype(f)
    ic, isn = co * 2 / 512, si * 2 / 512
    ic[0] = 1.0 / 512
    isn[0] = alt / 512
    inv = np.concatenate([ic, isn], 0).reshape(4, 128, 256)
    c["k_idft"] = inv.transpose(1, 0, 2).reshape(128, 1024).astype(f)
    tn = (np.arange(256, dtype=f) / f(256)).astype(f)
    bands = np.linspace(1e-4, 15, 16, dtype=f)
    ph = (f(2.0 * math.pi) * tn[:, None] * bands[None, :]).astype(f)
    c["k_feat"] = np.ascontiguousarray(np.concatenate([tn[:, None], np.cos(ph), -np.sin(ph)], 1).T).astype(f)
    slow, fast = abs(math.log(1e-2)) / 1.5, abs(math.log(1e-2)) / 0.3
    deltas = np.tile(np.linspace(slow, fast, 512, dtype=f), 2)
    dec = np.exp((-tn[:, None] * deltas[None, :]).astype(f)).astype(f)
    c["k_decay"] = np.ascontiguousarray(dec.reshape(2, 128, 1024).transpose(1, 0, 2).reshape(128, 2048))
    ang = 2 * np.pi * (np.outer(t, t) % 256) / 256
    cs = np.concatenate([np.cos(ang), np.sin(ang)], 1).reshape(2, 128, 512)
    d = np.arange(64)
    a64 = 2 * np.pi * (np.outer(d, d) % 64) / 64
    bd = np.zeros((2, 128, 128))
    for h in range(2):
        s = slice(64 * h, 64 * h + 64)
        bd[0, s, s] = np.cos(a64) / 128
        bd[1, s, s] = -np.sin(a64) / 128
    c["k_fft"] = np.concatenate([cs.transpose(1, 0, 2).reshape(128, 1024), bd.transpose(1, 0, 2).reshape(128, 256)], 1).astype(f)
    hd = np.zeros((128, 128), f)
    hd[:64, :64] = 1
    hd[64:, 64:] = 1
    c["k_hd"] = hd
    mask = np.zeros((128, 2, 256), f)
    q = np.arange(64)
    start = np.clip(q - 8, 0, 48)
    inw = (q[None, :] >= start[:, None]) & (q[None, :] < start[:, None] + 16)
    m64 = np.where(inw, 0.0, NEG).astype(f)
    full = np.tile(m64, (2, 4))
    mask[:, :, :] = full[::-1][:, None, :]
    c["k_mask"] = mask.reshape(128, 512)
    return {k: np.ascontiguousarray(v, dtype=f) for k, v in c.items()}


class Tok:
    def __init__(self, q, i):
        self.q, self.i = q, i

    def resolve(self):
        return self.q.sem, self.q.count[self.i]


class DTok:

    def __init__(self, owner, val):
        self.owner, self.val = owner, val

    def resolve(self):
        return self.owner.sem, self.owner.n if self.val is None else self.val


def flat(x):
    if x is None:
        return []
    if isinstance(x, (list, tuple)):
        return [t for y in x for t in flat(y)]
    return [x]


class Queue:
    def __init__(self, sem):
        self.sem, self.ops, self.count = sem, [], {}

    def __call__(self, fn, *waits):
        self.ops.append((fn, flat(waits), False))
        return Tok(self, len(self.ops) - 1)

    def raw(self, fn, *waits):
        w = flat(waits)
        self.ops.append((lambda e: fn(e, w), w, True))

    def dma(self, owner, dst, src, *waits):
        self.ops.append((lambda e: e.dma_start(dst, src).then_inc(owner.sem, 16), flat(waits), False))
        owner.n += 16
        return DTok(owner, owner.n)

    def play(self, eng):
        seen = {}
        for i, (fn, waits, raw) in enumerate(self.ops):
            if raw:
                fn(eng)
                continue
            need = {}
            for w in waits:
                sem, val = w.resolve()
                need[sem.name] = (sem, max(val, need.get(sem.name, (sem, 0))[1]))
            for name, (sem, val) in need.items():
                if seen.get(name, 0) < val:
                    eng.wait_ge(sem, val)
                    seen[name] = val
            ins = fn(eng)
            if i in self.count:
                ins.then_inc(self.sem, 1)


def number(queues):
    wanted = {}
    for q in queues:
        for _, waits, _ in q.ops:
            for w in waits:
                if isinstance(w, Tok):
                    wanted.setdefault(id(w.q), set()).add(w.i)
    for q in queues:
        for n, i in enumerate(sorted(wanted.get(id(q), ()))):
            q.count[i] = n + 1


class Loads:

    def __init__(self, sem):
        self.sem, self.n = sem, 0

    @property
    def all(self):
        return DTok(self, None)


class Slot:
    def __init__(self, ap, sem):
        self.ap, self.sem, self.n, self.last = ap, sem, 0, []


class Pool:

    def __init__(self, banks):
        self.free = [(b, []) for b in banks]

    def take(self):
        return self.free.pop(0)

    def give(self, bank, *toks):
        self.free.append((bank, flat(toks)))


class Buf:
    def __init__(self, t, lo, hi, w):
        self.t, self.lo, self.hi, self.w = t, lo, hi, w

    def __getitem__(self, k):
        return self.t[k]


class Mem:

    def __init__(self, nc, lo, hi):
        self.nc, self.free, self.n, self.end, self.low = nc, [(lo, hi, [])], 0, hi, hi - lo
        self.live = {}

    def take(self, name, shape, dtype=F32, parts=128):
        size = 4 * int(np.prod(shape))
        size = (size + 31) // 32 * 32
        for k, (lo, hi, _) in enumerate(self.free):
            end, m = hi, k
            while end - lo < size and m + 1 < len(self.free) and self.free[m + 1][0] == end:
                m += 1
                end = self.free[m][1]
            if end - lo >= size:
                toks = flat([self.free[x][2] for x in range(k, m + 1)])
                tail = self.free[m]
                rest = [(lo + size, tail[1], tail[2])] if lo + size < tail[1] else []
                self.free[k:m + 1] = rest
                self.n += 1
                t = self.nc.alloc_sbuf_tensor_at(f"{name}_{self.n}", [parts, *shape], dtype, offset=lo)
                self.low = min(self.low, sum(b - a for a, b, _ in self.free))
                b = Buf(t, lo, lo + size, toks)
                self.live[name + f"_{self.n}"] = size
                b.key = name + f"_{self.n}"
                return b
        raise MemoryError(f"{name} {size}: free {[(a, b) for a, b, _ in self.free]} live {self.live}")

    def give(self, buf, *toks):
        del self.live[buf.key]
        self.free.append((buf.lo, buf.hi, flat(toks)))
        self.free.sort(key=lambda x: x[0])


class Core:

    def __init__(self, nc, ctx, dram):
        self.nc, self.ctx, self.d = nc, ctx, dram
        self.T, self.V, self.A, self.G, self.S = (Queue(self.sem(n)) for n in ("pe", "dve", "act", "pool", "sp"))
        self.mem = Mem(nc, 16896, 229344)
        self.banks = [ctx.enter_context(nc.psum_tensor(f"bank{i}", [128, 512], F32)) for i in range(8)]
        self.slots = []
        for i in range(NRING):
            self.slots.append(Slot(self.mem.take(f"slot{i}", [2048]).t, self.sem(f"ring{i}")))
        self.outs = Loads(self.sem("stores"))

    def sem(self, name):
        return self.ctx.enter_context(self.nc.semaphore(name))

    def group(self, name):
        return Loads(self.sem(name))

    def load(self, src):
        s = self.slots.pop(0)
        shape = src.shape
        n = int(np.prod(shape[1:]))
        dst = s.ap[:, 0:n]
        if len(shape) == 3:
            dst = dst.rearrange("p (a b) -> p a b", a=shape[1])
        tok = self.S.dma(s, dst, src, s.last)
        return s, dst, tok

    def done(self, slot, *toks):
        slot.last = flat(toks)
        self.slots.append(slot)

    def mm(self, out, lhsT, rhs, start, stop, *w):
        return self.T(lambda e: e.matmul(out, lhsT, rhs, start=start, stop=stop), *w)

    def tr(self, out, in_, *w):
        n = in_.shape[0]
        ident = self.eye[0:n, 0, 0:n]
        return self.T(lambda e: e.transpose(out, in_, ident), *w)

    def tt(self, q, out, a, b, op, *w):
        return q(lambda e: e.tensor_tensor(out, a, b, op), *w)

    def ts(self, q, out, a, s1, s2, op0, op1, *w):
        if op1 is None:
            return q(lambda e: e.tensor_scalar(out, a, s1, None, op0), *w)
        return q(lambda e: e.tensor_scalar(out, a, s1, s2, op0, op1), *w)

    def stt(self, q, out, in0, s, in1, op0, op1, *w):
        return q(lambda e: e.scalar_tensor_tensor(out, in0, s, in1, op0, op1), *w)

    def cp(self, q, out, in_, *w):
        if q is self.A:
            return q(lambda e: e.copy(out, in_), *w)
        return q(lambda e: e.tensor_copy(out, in_), *w)

    def act(self, out, in_, func, *w, bias=None, scale=None, accum=None):
        kw = {}
        if bias is not None:
            kw["bias"] = bias
        if scale is not None:
            kw["scale"] = scale
        if accum is not None:
            kw["accum_out"] = accum
        return self.A(lambda e: e.activation(out, in_, func, **kw), *w)

    def red(self, out, in_, op, *w, negate=False):
        if negate:
            return self.V(lambda e: e.tensor_reduce(out, in_, AX.X, op, negate=True), *w)
        return self.V(lambda e: e.tensor_reduce(out, in_, AX.X, op), *w)

    def recip(self, out, in_, *w):
        return self.V(lambda e: e.reciprocal(out, in_), *w)

    def set(self, q, out, val, *w):
        return q(lambda e: e.memset(out, val), *w)

    def pe_last(self):
        return Tok(self.T, len(self.T.ops) - 1)

    def rstd(self, out, sums, width, *w):
        t = self.act(out, sums, ACT.Sqrt, *w, bias=self.eps[0:out.shape[0]], scale=1.0 / width)
        return self.recip(out, out, t)

    def normed(self, src, name, *w):
        xn = self.mem.take(name, [2, 1024])
        ss = self.mem.take(name + "s", [2])
        a = [self.act(xn[:, t, :], src[:, t, :], ACT.Square, w, xn.w, ss.w, accum=ss[:, t:t + 1]) for t in range(2)]
        r = self.rstd(ss[:, :], ss[:, :], 1024.0, a)
        toks = [self.ts(self.V, xn[:, t, :], src[:, t, :], ss[:, t:t + 1], None, ALU.mult, None, r) for t in range(2)]
        self.mem.give(ss, toks)
        return xn, toks

    def turned(self, xn, toks, scale, shift, out, pool, *w):
        done = []
        for k2 in range(4):
            bank, bw = pool.take()
            for k in range(2):
                for t in range(2):
                    m = self.tr(bank[:, k * 256 + t * 128:k * 256 + t * 128 + 128],
                                xn[:, t, (2 * k2 + k) * 128:(2 * k2 + k + 1) * 128], toks[t], bw, self.eye_t)
            e = []
            for k in range(2):
                kt = 2 * k2 + k
                o, i = out[:, kt, :], bank[:, k * 256:k * 256 + 256]
                if k2 % 2:
                    e.append(self.act(o, i, ACT.Identity, m, w, out.w, scale=scale[:, kt:kt + 1], bias=shift[:, kt:kt + 1]))
                else:
                    e.append(self.ts(self.V, o, i, scale[:, kt:kt + 1], shift[:, kt:kt + 1], ALU.mult, ALU.add, m, w, out.w))
            pool.give(bank, e)
            done += e
        return done

    def cols(self, h, w, c0, n, pool, evac, *wt):
        a, av, at = self.load(w[0:512, c0:c0 + n].rearrange("(k p) c -> p k c", p=128))
        b, bv, bt = self.load(w[512:1024, c0:c0 + n].rearrange("(k p) c -> p k c", p=128))
        for ct in range(n // 128):
            self.col_tile(h, (av, bv), ct, pool, evac, wt, at, bt)
        self.done(a, self.last_mm)
        self.done(b, self.last_mm)

    def col_tile(self, h, views, ct, pool, evac, *wt):
        bank, bw = pool.take()
        for k in range(8):
            m = self.mm(bank[:, 0:256], views[k // 4][:, k % 4, ct * 128:ct * 128 + 128], h[:, k, :], k == 0, k == 7, wt, bw)
        self.last_mm = m
        pool.give(bank, evac(ct, bank[:, 0:256], m))

    def tok_tile(self, h, views, c0, n, t, pool, evac, *wt):
        bank, bw = pool.take()
        for k in range(8):
            m = self.mm(bank[:, 0:n], h[:, k, t * 128:t * 128 + 128], views[k // 4][:, k % 4, c0:c0 + n], k == 0, k == 7, wt, bw)
        self.last_mm = m
        pool.give(bank, evac(t, bank[:, 0:n], m))

    def rows(self, h, w, c0, n, pool, evac, *wt):
        a, av, at = self.load(w[0:512, c0:c0 + n].rearrange("(k p) c -> p k c", p=128))
        b, bv, bt = self.load(w[512:1024, c0:c0 + n].rearrange("(k p) c -> p k c", p=128))
        for t in range(2):
            self.tok_tile(h, (av, bv), 0, n, t, pool, evac, wt, at, bt)
        self.done(a, self.last_mm)
        self.done(b, self.last_mm)

    def ada(self, name, w, bias, cond, pool, tpool, *wt):
        c = self
        m = {"sb": c.mem.take(name + "sb", [3, 512]), "col": [c.mem.take(name + f"c{i}", [48]) for i in range(2)], "t": [None] * 3, "ct": [None] * 3}
        br = c.mem.take(name + "b", [3, 512])
        z = c.set(c.G, br[:, :, :], 0.0, br.w)
        g = c.group(name + "b")
        for i in range(2):
            c.G.dma(g, br[i::32, :, :], bias.rearrange("(q j n) -> j q n", q=3, j=4), z)
        self.mods[name] = m
        for q in range(3):
            bank, bw = pool.take()
            for k in range(8):
                s, v, lt = c.load(w[k * 128:k * 128 + 128, q * 2048:q * 2048 + 2048])
                for j in range(4):
                    t = c.mm(bank[32 * j:32 * j + 32, :], cond[:, k, :], v[:, j * 512:j * 512 + 512], k == 0, k == 7, lt, bw, wt)
                c.done(s, t)
                if k % 2:
                    yield
            m["t"][q] = e = c.tt(c.V, m["sb"][:, q, :], bank[:, :], br[:, q, :], ALU.add, t, g.all, m["sb"].w)
            pool.give(bank, e)
            bank, bw = tpool.take()
            for b in range(4):
                t = c.tr(bank[:, b * 128:b * 128 + 128], m["sb"][:, q, b * 128:b * 128 + 128], e, bw, c.eye_t)
            v = bank[:, :].rearrange("p (b j r) -> p j b r", b=4, j=4)
            e = [c.cp(c.V, m["col"][i][:, q * 16:q * 16 + 16].rearrange("p (j b) -> p j b", j=4), v[:, :, :, i], t, m["col"][i].w) for i in range(2)]
            tpool.give(bank, e)
            m["ct"][q] = e
            yield
        c.mem.give(br, m["t"])

    def gate(self, m, which, seg, pool, dst):
        toks = []
        for h in range(2):
            bank, bw = pool.take()
            r = 32 * ((seg % 2) * 2 + h) + which
            t = self.mm(bank[:, :], self.eye[:, 0, r:r + 1].to_broadcast([128, 128]), m["sb"][:, seg // 2, :], True, True, m["t"][seg // 2], bw, self.eye_t)
            e = self.cp(self.A, dst[:, h * 512:h * 512 + 512], bank[:, :], t, dst.w)
            pool.give(bank, e)
            toks.append(e)
        return toks


def setup(c):
    d, mem, T, V, A, G, S = c.d, c.mem, c.T, c.V, c.A, c.G, c.S
    c.mods = {}
    c.small = mem.take("small", [288])
    c.eye = mem.take("eye", [4, 128])
    c.eps = c.small[:, 32:33]
    c.x = mem.take("x", [2, 1024])
    r0 = mem.take("r0", [128], parts=32)
    g0, g1 = c.group("g0"), c.group("g1")
    A.dma(g0, r0[0:8, :], d["c"].rearrange("o (k p) -> (o k) p", p=128))
    A.dma(g0, r0[8:16, :], d["c_ctx"].rearrange("(k p) -> k p", p=128))
    A.dma(g0, r0[16:24, :], d["c_2"].rearrange("o (k p) -> (o k) p", p=128))
    A.dma(g0, r0[24:32, :], d["c_ctx_2"].rearrange("(k p) -> k p", p=128))
    S.dma(g0, c.eye[:, :, :], d["k_eye"])
    S.dma(g0, c.small[:, :], d["k_small"])
    c.eye_t = g0.all
    S.dma(g1, c.x[:, :, :], d["x"].rearrange("o (t p) n -> p (o t) n", p=128))
    c.x_t = g1.all

    bank, bw = c.pa.take()
    t = c.tr(bank[:, 0:32], r0[:, :], g0.all, bw)
    conds = []
    es = []
    for i in range(2):
        s = mem.take(f"cond{i}", [8, 32])
        z = c.set(V, s[:, :, :], 0.0, s.w)
        e = c.act(s[:, :, 0:2].rearrange("p k w -> p w k"), bank[:, 16 * i:16 * i + 16].rearrange("p (w k) -> p w k", w=2), ACT.Silu, t, z)
        conds.append((s, e))
        es.append(e)
    c.pa.give(bank, es)
    mem.give(r0, t)
    c.conds = conds


def vectors(c):
    d, mem = c.d, c.mem
    r1 = mem.take("r1", [128])
    r2 = mem.take("r2", [128], parts=40)
    g = c.group("vec")
    lay, at = {}, 0
    z = c.set(c.G, r1[:, :], 0.0, r1.w)
    for name, n, src in (("n1", 8, d["norm1_g"]), ("n2", 8, d["norm2_g"]), ("b_in", 52, d["b_in"]), ("cw", 36, d["hy_conv_w"]),
                         ("cb", 12, d["hy_conv_b"]), ("skip", 4, d["hy_skip"])):
        if len(src.shape) == 3:
            src = src.rearrange("o a n -> o (a n)")
        c.G.dma(g, r1[at:at + n, :], src.rearrange("o (k p) -> (o k) p", p=128), z)
        lay[name] = at
        at += n
    lay2, at = {}, 0
    for name, n, src in (("n1_2", 16, d["norm1_g_2"]), ("n2_2", 16, d["norm2_g_2"]), ("sb_2", 8, None)):
        src = src.rearrange("l (k p) -> (l k) p", p=128) if src is not None else d["sgu_b_2"].rearrange("l g p -> (l g) p")
        c.G.dma(g, r2[at:at + n, :], src, r2.w)
        lay2[name] = at
        at += n
    c.vec = mem.take("vec", [168])
    bank, bw = c.pa.take()
    c.tr(bank[:, 0:128], r1[:, :], g.all, bw, c.eye_t)
    t = c.tr(bank[:, 128:168], r2[:, :])
    e = c.cp(c.V, c.vec[:, :], bank[:, 0:168], t, c.vec.w)
    c.pa.give(bank, e)
    mem.give(r1, t)
    mem.give(r2, t)
    c.vec_t = e
    c.col = {k: v for k, v in lay.items()} | {k: v + 128 for k, v in lay2.items()}


def column(c, name, n, at=0):
    b = c.col[name] + at
    return c.vec[:, b:b + n]


def scale_shift(c, m, which, seg_shift, seg_scale, gain, name):
    a = c.mem.take(name, [8])
    t = c.stt(c.V, a[:, :], m["col"][which][:, seg_scale * 8:seg_scale * 8 + 8], 1.0, gain, ALU.add, ALU.mult,
              m["ct"][seg_scale // 2], c.vec_t, a.w)
    return a, m["col"][which][:, seg_shift * 8:seg_shift * 8 + 8], [t, m["ct"][seg_shift // 2]]


def sine(c, arg, n, t, out, *w):
    mem, V = c.mem, c.V
    k = mem.take("sink", [256])
    magic = 12582912.0
    c1 = 6.28125
    c2 = float(np.float32(np.round((2 * math.pi - c1) * 2 ** 22) / 2 ** 22))
    c3 = float(np.float32(2 * math.pi - c1 - c2))
    a, kk = arg[0:n, :], k[0:n, :]
    t = c.ts(V, kk, a, 1 / (2 * math.pi), magic, ALU.mult, ALU.add, t, k.w)
    t = c.ts(V, kk, kk, magic, None, ALU.subtract, None, t)
    for cc in (c1, c2, c3):
        t = c.stt(V, a, kk, -cc, a, ALU.mult, ALU.add, t)
    t = c.ts(V, a, a, 3.1415925, -3.1415925, ALU.min, ALU.max, t)
    mem.give(k, t)
    return c.act(out, a, ACT.Sin, t, w)


def filters(c):
    d, mem, V, A, G = c.d, c.mem, c.V, c.A, c.G
    g = c.group("hyf")
    feat, w1, w2, w3, sc = (mem.take(n, s) for n, s in (("feat", [256]), ("hw1", [64]), ("hw2", [64]), ("hw3", [1024]), ("hsc", [3])))
    for dst, src, b in ((feat[0:33, :], d["k_feat"], feat), (w1[0:33, :], d["hy_ffn_w1"][0], w1), (w2[0:64, :], d["hy_ffn_w2"][0], w2),
                        (w3[0:64, :], d["hy_ffn_w3"][0], w3), (sc[0:64, 0:1], d["hy_ffn_b1"].rearrange("o n -> n o"), sc),
                        (sc[0:64, 1:2], d["hy_ffn_b2"].rearrange("o n -> n o"), sc), (sc[0:64, 2:3], d["hy_ffn_freq"].rearrange("o n -> n o"), sc)):
        G.dma(g, dst, src, b.w)
    dft = c.dft = mem.take("dft", [6, 2, 128])
    G.dma(g, dft[:, :, :, :], d["k_dft"].rearrange("p (b k f) -> p b k f", b=6, k=2), dft.w)
    decay = mem.take("decay", [2, 1024])
    G.dma(g, decay[:, :, :], d["k_decay"].rearrange("p (t n) -> p t n", t=2), decay.w)
    c.dft_t = g.all
    yield
    arg = mem.take("harg", [256])
    hid = mem.take("hid", [256])
    t = None
    for w, b, rhs, kk in ((w1, 0, feat, 33), (w2, 1, hid, 64)):
        bank, bw = c.pa.take()
        t = c.mm(bank[0:64, 0:256], w[0:kk, :], rhs[0:kk, :], True, True, g.all, bw, t)
        e = c.ts(V, arg[0:64, :], bank[0:64, 0:256], sc[0:64, b:b + 1], sc[0:64, 2:3], ALU.add, ALU.mult, t, arg.w)
        c.pa.give(bank, e)
        t = sine(c, arg, 64, e, hid[0:64, :], hid.w)
        yield
    filt = mem.take("filt", [2, 1024])
    ab = mem.take("fabs", [2, 1024])
    es, ea = [], []
    for tt in range(2):
        for h in range(2):
            bank, bw = c.pa.take()
            m = c.mm(bank[:, :], hid[0:64, tt * 128:tt * 128 + 128], w3[0:64, h * 512:h * 512 + 512], True, True, t, bw)
            o = filt[:, tt, h * 512:h * 512 + 512]
            e = c.tt(V, o, bank[:, :], decay[:, tt, h * 512:h * 512 + 512], ALU.mult, m, filt.w)
            c.pa.give(bank, e)
            es.append(e)
            ea.append(c.act(ab[:, tt, h * 512:h * 512 + 512], o, ACT.Abs, e, ab.w))
            yield
    mem.give(feat, t); mem.give(w1, t); mem.give(w2, t); mem.give(w3, m); mem.give(sc, es); mem.give(arg, t); mem.give(hid, m)
    mem.give(decay, es)
    inv = mem.take("finv", [2, 512])
    er = []
    for h in range(2):
        bank, bw = c.pa.take()
        for tt in range(2):
            m = c.mm(bank[:, :], c.eye[:, 2, :], ab[:, tt, h * 512:h * 512 + 512], tt == 0, tt == 1, ea, bw)
        e = c.recip(inv[:, h, :], bank[:, :], m, inv.w)
        c.pa.give(bank, e)
        er.append(e)
        yield
    mem.give(ab, m)
    fn = []
    for h in range(2):
        for tt in range(2):
            o = filt[:, tt, h * 512:h * 512 + 512]
            fn.append(c.tt(G, o, o, inv[:, h, :], ALU.mult, er[h], es))
    mem.give(inv, fn)
    yield
    sm = mem.take("fsum", [2, 2, 512])
    hs = [c.tt(G, sm[:, i, :, :], filt[:, :, 0:512], filt[:, :, 512:1024], op, fn, sm.w) for i, op in enumerate((ALU.add, ALU.subtract))]
    mem.give(filt, hs)
    c.hf = mem.take("hf", [5, 512])
    c.hf_t = []
    for i, (blk, s) in enumerate(((0, 0), (1, 0), (2, 1), (3, 1), (5, 0))):
        bank, bw = c.pa.take()
        for k in range(2):
            m = c.mm(bank[:, :], dft[:, blk, k, :], sm[:, s, k, :], k == 0, k == 1, hs, bw)
        e = c.cp(A, c.hf[:, i, :], bank[:, :], m, c.hf.w)
        c.pa.give(bank, e)
        c.hf_t.append(e)
        yield
    mem.give(sm, m)


def hyena(c, u, ut, out):
    d, mem, V, A, G = c.d, c.mem, c.V, c.A, c.G
    cv = mem.take("conv", [12, 256])
    ct = []
    for k in range(12):
        o = cv[:, k, :]
        w = lambda j: column(c, "cw", 1, 12 * j + k)
        t = c.ts(V, o, u[:, k, 1:257], w(1), column(c, "cb", 1, k), ALU.mult, ALU.add, ut[k], cv.w, c.vec_t)
        t = c.stt(V, o, u[:, k, 0:256], w(0), o, ALU.mult, ALU.add, t)
        t = c.stt(V, o, u[:, k, 2:258], w(2), o, ALU.mult, ALU.add, t)
        ct.append(t)
        if k % 4 == 3:
            yield
    mem.give(u, ct)
    z = cv[:, 4:8, :]
    zt = c.tt(V, z, z, cv[:, 8:12, :], ALU.mult, ct)
    ztok = mem.take("ztok", [2, 512])
    e = []
    for t in range(2):
        bank, bw = c.pa.take()
        for k in range(4):
            m = c.tr(bank[:, k * 128:k * 128 + 128], cv[:, 4 + k, t * 128:t * 128 + 128], zt, bw)
        e.append(c.cp(A, ztok[:, t, :], bank[:, :], m, ztok.w))
        c.pa.give(bank, e[-1])
        yield
    while not c.hf_t or len(c.hf_t) < 5:
        yield
    zf = mem.take("zf", [4, 512])
    ez = []
    for i, blk in enumerate((0, 1, 4, 3)):
        bank, bw = c.pa.take()
        for k in range(2):
            m = c.mm(bank[:, :], c.dft[:, blk, k, :], ztok[:, k, :], k == 0, k == 1, e, bw, c.dft_t)
        ez.append(c.cp(A, zf[:, i, :], bank[:, :], m, zf.w))
        c.pa.give(bank, ez[-1])
        yield
    mem.give(ztok, m)
    mem.give(c.dft, m)
    yf = mem.take("yf", [4, 512])
    tmp = mem.take("yt", [2, 512])
    hr, hi = c.hf[:, 0:2, :], c.hf[:, 2:4, :]
    zc, zs = zf[:, 0:2, :], zf[:, 2:4, :]
    a = c.tt(V, yf[:, 0:2, :], zc, hr, ALU.mult, ez, c.hf_t, yf.w)
    b = c.tt(G, tmp[:, :, :], zs, hi, ALU.mult, ez, c.hf_t, tmp.w)
    y1 = c.tt(V, yf[:, 0:2, :], yf[:, 0:2, :], tmp[:, :, :], ALU.subtract, a, b)
    b = c.tt(G, tmp[:, :, :], zc, hi, ALU.mult, ez, c.hf_t, y1)
    a0 = c.tt(V, yf[:, 2, :], zf[:, 2, :], c.hf[:, 4, :], ALU.mult, ez, c.hf_t, yf.w)
    a1 = c.tt(V, yf[:, 3, :], zf[:, 3, :], c.hf[:, 1, :], ALU.mult, ez, c.hf_t, yf.w)
    y2 = c.tt(V, yf[:, 2:4, :], yf[:, 2:4, :], tmp[:, :, :], ALU.add, a0, a1, b)
    mem.give(zf, y1, y2)
    mem.give(c.hf, y1, y2)
    mem.give(tmp, y1, y2)
    yield
    idft = mem.take("idft", [4, 256])
    g = c.group("idft")
    G.dma(g, idft[:, :, :], d["k_idft"].rearrange("p (b t) -> p b t", b=4), idft.w)
    yield
    done = []
    for k in range(4):
        bank, bw = c.pa.take()
        for i in range(4):
            m = c.mm(bank[:, 0:256], yf[:, i, k * 128:k * 128 + 128], idft[:, i, :], i == 0, i == 3, y1, y2, bw, g.all)
        o = out[:, k, :]
        e = c.stt(V, o, cv[:, 4 + k, :], column(c, "skip", 1, k), bank[:, 0:256], ALU.mult, ALU.add, m, out.w)
        c.pa.give(bank, e)
        done.append(c.tt(V, o, o, cv[:, k, :], ALU.mult, e))
        yield
    mem.give(yf, m)
    mem.give(idft, m)
    mem.give(cv, done)
    c.hy_t = done


def decays(c):
    d, mem, V, A, G = c.d, c.mem, c.V, c.A, c.G
    g = c.group("decay")
    lg = mem.take("lg", [8])
    w = mem.take("lgw", [5, 8])
    ret = mem.take("kret", [1024])
    G.dma(g, lg[:, :], d["ret_decay_logit"].rearrange("o a h -> o (a h)").to_broadcast([128, 8]), lg.w)
    G.dma(g, ret[:, :], d["k_ret"], ret.w)
    e, u, dd, z, s = (w[:, i, :] for i in range(5))
    t = c.act(e, lg[:, :], ACT.Abs, g.all, w.w)
    t = c.act(e, e, ACT.Exp, t, scale=-1.0)
    t = c.ts(V, u, e, 1.0, None, ALU.add, None, t, w.w)
    t1 = c.act(s, u, ACT.Ln, t, w.w)
    t = c.ts(V, dd, u, -1.0, None, ALU.add, None, t, w.w)
    tz = c.ts(V, z, dd, 0.0, None, ALU.is_equal, None, t, w.w)
    t = c.tt(V, dd, dd, z, ALU.add, tz)
    t = c.recip(dd, dd, t)
    t = c.tt(V, dd, dd, s, ALU.mult, t, t1)
    t = c.tt(V, dd, dd, z, ALU.add, t)
    t = c.tt(V, dd, dd, e, ALU.mult, t)
    t = c.stt(V, lg[:, :], lg[:, :], 0.0, dd, ALU.min, ALU.subtract, t)
    mem.give(w, t)
    yield
    c.dk = mem.take("dk", [2, 4, 2])
    c.dq = mem.take("dq", [2, 4, 2])
    c.dm = mem.take("dm", [4, 512])
    c.dk_t, c.dq_t, c.dm_t = [], [], []
    for i in range(2):
        for h in range(4):
            l = lg[:, i * 4 + h:i * 4 + h + 1]
            c.dk_t.append(c.act(c.dk[:, i, h, :], c.small[:, 50 + 2 * i:52 + 2 * i], ACT.Exp, t, c.dk.w, scale=l))
            c.dq_t.append(c.act(c.dq[:, i, h, :], c.small[:, 54 + 2 * i:56 + 2 * i], ACT.Exp, t, c.dq.w, scale=l))
    c.dk_t = [c.ts(V, c.dk[:, :, :, :], c.dk[:, :, :, :], 128.0 ** -0.5, None, ALU.mult, None, c.dk_t)]
    yield
    last = []
    for h in range(4):
        o = c.dm[:, h, :]
        t1 = c.ts(V, o, ret[:, 0:512], lg[:, h:h + 1], None, ALU.mult, None, t, c.dm.w)
        t1 = c.stt(V, o, ret[:, 512:1024], lg[:, 4 + h:5 + h], o, ALU.mult, ALU.add, t1)
        last.append(t1)
        c.dm_t.append(c.act(o, o, ACT.Exp, t1))
        yield
    mem.give(ret, last)
    mem.give(lg, last, c.dq_t, c.dk_t)


def states(c, kc, kct, vc, vct):
    mem, V, A, G = c.mem, c.V, c.A, c.G
    c.st = mem.take("st", [4, 2, 256])
    c.st_t = []
    kd = mem.take("kd", [2, 2, 2, 128])
    last = [[], []]
    for h in range(4):
        b = h % 2
        kt = []
        for i in range(2):
            for t in range(2):
                kt.append(c.ts(V, kd[:, b, i, t, :], kc[:, t, h * 128:h * 128 + 128], c.dk[:, i, h, t:t + 1], None, ALU.mult, None,
                               kct, c.dk_t, kd.w, last[b]))
        bank, bw = c.pa.take()
        for i in range(2):
            for t in range(2):
                m = c.mm(bank[:, i * 256:i * 256 + 256], kd[:, b, i, t, :], vc[:, t, h * 256:h * 256 + 256], t == 0, t == 1, kt, vct, bw)
        last[b] = m
        e = c.cp(A, c.st[:, h, :, :], bank[:, :].rearrange("p (i v) -> p i v", i=2), m, c.st.w)
        c.pa.give(bank, e)
        c.st_t.append(e)
        yield
    mem.give(kd, last)
    mem.give(kc, kt)
    mem.give(vc, m)
    mem.give(c.dk, kt)


def turn_heads(c, x, xt, rope, rt, out):
    V, G = c.V, c.G
    toks = []
    for p in range(2):
        bank, bw = c.pa.take()
        for h in range(2):
            m = c.mm(bank[:, h * 256:h * 256 + 256], rope[:, 512:640], x[:, 2 * p + h, :], True, True, xt[2 * p + h], rt, bw)
        o, i = out[:, 2 * p:2 * p + 2, :], x[:, 2 * p:2 * p + 2, :]
        sin = rope[:, 256:512].unsqueeze(1).to_broadcast([128, 2, 256])
        cos = rope[:, 0:256].unsqueeze(1).to_broadcast([128, 2, 256])
        e = c.tt(V, o, bank[:, :].rearrange("p (h t) -> p h t", h=2), sin, ALU.mult, m, rt, out.w)
        c.pa.give(bank, e)
        f = c.tt(V, i, i, cos, ALU.mult, xt[2 * p:2 * p + 2], rt, m)
        toks.append(c.tt(V, o, o, i, ALU.add, e, f))
        yield
    c.turned_t = toks


def retention(c, q, qt, k, kt, v, vt, o):
    d, mem, V, A, G = c.d, c.mem, c.V, c.A, c.G
    rope = mem.take("rope", [640])
    g = c.group("rope")
    G.dma(g, rope[:, :], d["k_rope"], rope.w)
    qr = mem.take("qr", [4, 256])
    kr = mem.take("kr", [4, 256])
    yield
    yield from turn_heads(c, k, kt, rope, g.all, kr)
    krt = c.turned_t
    mem.give(k, krt)
    yield from turn_heads(c, q, qt, rope, g.all, qr)
    qrt = c.turned_t
    mem.give(q, qrt)
    mem.give(rope, qrt)
    while not vt or not c.st_t or len(c.st_t) < 4 or len(c.dm_t) < 4:
        yield
    sc = mem.take("rsc", [2, 512])
    c.oss = mem.take("oss", [8])
    junk = mem.take("ojunk", [2, 256])
    c.o_t, c.oss_t = [], []
    last = [[], []]
    js = [[], []]
    for h in range(4):
        b = h % 2
        bank, bw = c.pa.take()
        for j in range(2):
            m = c.mm(bank[:, j * 256:j * 256 + 256], kr[:, h, j * 128:j * 128 + 128], qr[:, h, :], True, True, krt, qrt, bw)
        e = c.stt(V, sc[:, b, :], bank[:, :], 128.0 ** -0.5, c.dm[:, h, :], ALU.mult, ALU.mult, m, c.dm_t[h], sc.w, last[b])
        c.pa.give(bank, e)
        yield
        bank, bw = c.pa.take()
        for t in range(2):
            out = bank[:, t * 256:t * 256 + 256]
            for j in range(2):
                m = c.mm(out, sc[:, b, j * 256 + t * 128:j * 256 + t * 128 + 128], v[:, j, h * 256:h * 256 + 256], j == 0, j == 1, e, vt, bw)
        ci = c.cp(A, o[:, :, h * 256:h * 256 + 256], bank[:, :].rearrange("p (t v) -> p t v", t=2), m, o.w)
        c.pa.give(bank, ci)
        last[b] = m
        yield
        es = []
        for t in range(2):
            bank, bw = c.pa.take()
            m = c.mm(bank[:, :], qr[:, h, t * 128:t * 128 + 128], c.st[:, h, :, :], True, True, c.st_t[h], bw)
            x, y = o[:, t, h * 256:h * 256 + 256], ci
            for i in range(2):
                y = c.stt(V, x, bank[:, i * 256:i * 256 + 256], c.dq[:, i, h, t:t + 1], x, ALU.mult, ALU.add, m, y, c.dq_t)
            c.pa.give(bank, y)
            es.append(y)
            a = c.act(junk[:, t, :], x, ACT.Square, y, junk.w, c.oss.w, js[t], accum=c.oss[:, t * 4 + h:t * 4 + h + 1])
            js[t] = [a]
            c.oss_t.append(a)
        c.o_t += es
        yield
    mem.give(junk, c.oss_t)
    mem.give(sc, m)
    mem.give(qr, m)
    mem.give(kr, m)
    mem.give(v, m)
    mem.give(c.st, m)
    mem.give(c.dq, es)
    mem.give(c.dm, e)


def first_mix(c):
    d, mem, V, A, G, S = c.d, c.mem, c.V, c.A, c.G, c.S
    w, b_in = d["w_in"][0], d["b_in"]
    xn, xt = c.normed(c.x, "xn", c.x_t)
    ctx = mem.take("ctx", [2, 1024])
    g = c.group("ctx")
    S.dma(g, ctx[:, :, :], d["ctx"].rearrange("o (t p) n -> p (o t) n", p=128), ctx.w)
    cond, ct = c.conds[0]
    a1 = c.ada("m1", d["ada_w"][0], d["ada_b"][0], cond, c.pa, c.pb, ct)
    pre = [filters(c), decays(c)]
    while not c.mods.get("m1") or c.mods["m1"]["ct"][0] is None:
        next(a1)
        for j in list(pre):
            if next(j, "end") == "end":
                pre.remove(j)
    run(pre)
    m = c.mods["m1"]
    cn, cnt = c.normed(ctx, "cn", g.all)
    mem.give(ctx, cnt)
    ax, shx, st = scale_shift(c, m, 0, 0, 1, column(c, "n1", 8), "ax")
    h = mem.take("h", [8, 256])
    ht = c.turned(xn, xt, ax, shx, h, c.pb, st)
    mem.give(xn, c.pe_last())
    ac, shc, sct = scale_shift(c, m, 1, 0, 1, column(c, "n1", 8), "ac")
    hc = mem.take("hc", [8, 256])
    hct = c.turned(cn, cnt, ac, shc, hc, c.pb, sct)
    mem.give(cn, c.pe_last())
    mem.give(ax, ht)
    mem.give(ac, hct)

    jobs = [a1]

    def step(n=1):
        for _ in range(n):
            for j in list(jobs):
                if next(j, "end") == "end":
                    jobs.remove(j)

    u = mem.take("u", [12, 258])
    uz = c.set(G, u[:, :, 0:258:257], 0.0, u.w)
    ut = [None] * 12

    def to_u(base):
        def evac(i, ps, t):
            k = base + i
            ut[k] = [c.act(u[:, k, 1:257], ps, ACT.Identity, t, u.w, uz, c.vec_t, bias=column(c, "b_in", 1, 24 + k))]
            return ut[k]
        return evac
    for n in range(3):
        c.cols(h, w, 3072 + n * 512, 512, c.pb, to_u(4 * n), ht)
        step()
    hy = mem.take("hy", [4, 256])
    jobs.append(hyena(c, u, ut, hy))
    step(3)

    def to_heads(dst, toks, base):
        def evac(i, ps, t):
            e = c.act(dst[:, i, :], ps, ACT.Identity, t, dst.w, c.vec_t, bias=column(c, "b_in", 1, base + i))
            toks.append(e)
            return e
        return evac
    kT = mem.take("kT", [4, 256])
    kc = mem.take("kc", [2, 512])
    bias = mem.take("bias", [1536])
    gb = c.group("bias")
    G.dma(gb, bias[:, :], b_in[0:1, 512:2048].to_broadcast([128, 1536]), bias.w)
    kt, qt, kct, vct, vt = [], [], [], [], []

    def to_tok(dst, toks, base, boff):
        def evac(t, ps, tok):
            n = ps.shape[1]
            e = c.tt(V, dst[:, t, base:base + n], ps, bias[:, boff:boff + n], ALU.add, tok, gb.all, dst.w)
            toks.append(e)
            return e
        return evac
    a, av, at = c.load(w[0:512, 512:1024].rearrange("(k p) c -> p k c", p=128))
    b, bv, bt = c.load(w[512:1024, 512:1024].rearrange("(k p) c -> p k c", p=128))
    for i in range(4):
        c.col_tile(h, (av, bv), i, c.pb, to_heads(kT, kt, 4), ht, at, bt)
    for t in range(2):
        c.tok_tile(hc, (av, bv), 0, 512, t, c.pb, to_tok(kc, kct, 0, 0), hct)
    c.done(a, c.last_mm)
    c.done(b, c.last_mm)
    step(5)
    qT = mem.take("qT", [4, 256])
    c.cols(h, w, 0, 512, c.pb, to_heads(qT, qt, 0), ht)
    step(5)
    vc = mem.take("vc", [2, 1024])
    v = mem.take("v", [2, 1024])
    o = mem.take("o", [2, 1024])
    jobs.append(retention(c, qT, qt, kT, kt, v, vt, o))
    for n in range(2):
        c0 = 1024 + 512 * n
        a, av, at = c.load(w[0:512, c0:c0 + 512].rearrange("(k p) c -> p k c", p=128))
        b, bv, bt = c.load(w[512:1024, c0:c0 + 512].rearrange("(k p) c -> p k c", p=128))
        tx = []
        for t in range(2):
            c.tok_tile(hc, (av, bv), 0, 512, t, c.pb, to_tok(vc, vct, n * 512, 512 + n * 512), hct, at, bt)
            step()
        for t in range(2):
            c.tok_tile(h, (av, bv), 0, 512, t, c.pb, to_tok(v, tx, n * 512, 512 + n * 512), ht)
            step()
        c.done(a, c.last_mm)
        c.done(b, c.last_mm)
        if n:
            vt.extend(tx0 + tx)
        tx0 = tx
    mem.give(hc, c.last_mm)
    mem.give(bias, vt, vct, kct)
    jobs.append(states(c, kc, kct, vc, vct))
    sg = mem.take("sg", [2, 1024])
    bias2 = mem.take("bias2", [1024])
    gb2 = c.group("bias2")
    G.dma(gb2, bias2[:, :], b_in[0:1, 2048:3072].to_broadcast([128, 1024]), bias2.w)
    sgt, sga = [], []

    def to_sg(n):
        def evac(t, ps, tok):
            o_ = sg[:, t, n * 512:n * 512 + 512]
            e = c.tt(V, o_, ps, bias2[:, n * 512:n * 512 + 512], ALU.add, tok, gb2.all, sg.w)
            sga.append(e)
            sgt.append(c.act(o_, o_, ACT.Silu, e))
            return e
        return evac
    for n in range(2):
        c.rows(h, w, 2048 + n * 512, 512, c.pb, to_sg(n), ht)
        step(3)
    mem.give(bias2, sga)
    gr = mem.take("gr", [2, 8, 256])
    grt = [[None] * 8, [None] * 8]

    def to_gate(i, base):
        def evac(k, ps, t):
            grt[i][base + k] = c.act(gr[:, i, base + k, :], ps, ACT.Sigmoid, t, gr.w, c.vec_t, bias=column(c, "b_in", 1, 36 + 8 * i + base + k))
            return grt[i][base + k]
        return evac
    for n in range(4):
        c.cols(h, w, 4608 + n * 512, 512, c.pb, to_gate(n // 2, 4 * (n % 2)), ht)
        step(3)
    mem.give(h, c.last_mm)
    while jobs:
        step()
    r = c.rstd(c.oss[:, :], c.oss[:, :], 256.0, c.oss_t)
    og = []
    for t in range(2):
        for hh in range(4):
            s = slice(hh * 256, hh * 256 + 256)
            og.append(c.stt(V, o[:, t, s], o[:, t, s], c.oss[:, t * 4 + hh:t * 4 + hh + 1], sg[:, t, s], ALU.mult, ALU.mult, r, sgt, c.o_t))
    mem.give(c.oss, og)
    mem.give(sg, og)
    ogT = mem.take("ogT", [8, 256])
    et = []
    for k2 in range(4):
        bank, bw = c.pa.take()
        for k in range(2):
            for t in range(2):
                kk = (2 * k2 + k) * 128
                mt = c.tr(bank[:, k * 256 + t * 128:k * 256 + t * 128 + 128], o[:, t, kk:kk + 128], og[4 * t + k2], bw)
        et.append(c.cp(A if k2 % 2 else V, ogT[:, 2 * k2:2 * k2 + 2, :], bank[:, :].rearrange("p (k t) -> p k t", k=2), mt, ogT.w))
        c.pa.give(bank, et[-1])
    mem.give(o, mt)
    hw = d["hy_w_o"][0]
    rw = d["ret_w_o"][0]
    mx = [None] * 8
    for n in range(2):
        c0 = n * 512
        sl, hv, lt = c.load(hw[:, c0:c0 + 512].rearrange("(k p) c -> p k c", p=128))
        mh = []
        for k in range(4):
            bank, bw = c.pb.take()
            for kk in range(4):
                mt = c.mm(bank[:, 0:256], hv[:, kk, k * 128:k * 128 + 128], hy[:, kk, :], kk == 0, kk == 3, lt, bw, c.hy_t)
            o_ = gr[:, 1, 4 * n + k, :]
            e = c.tt(V, o_, bank[:, 0:256], o_, ALU.mult, mt, grt[1][4 * n + k])
            c.pb.give(bank, e)
            mh.append(e)
        c.done(sl, mt)

        def to_mix(k, ps, t):
            kk = 4 * n + k
            o_ = gr[:, 0, kk, :]
            e = c.tt(V, o_, ps, o_, ALU.mult, t, grt[0][kk])
            mx[kk] = c.tt(V, o_, o_, gr[:, 1, kk, :], ALU.add, e, mh[k])
            return e
        c.cols(ogT, rw, c0, 512, c.pb, to_mix, et)
    mem.give(hy, mt)
    mem.give(ogT, c.last_mm)
    gt = mem.take("gt1", [1024])
    gtt = c.gate(m, 0, 2, c.pa, gt)
    x_t = [[], []]
    wo = d["w_out"][0]
    tmp = mem.take("xtmp", [2, 512])
    last = [[], []]
    for n in range(2):
        def to_x(t, ps, tok):
            s = slice(n * 512, n * 512 + 512)
            e = c.tt(V, tmp[:, t, :], ps, gt[:, s], ALU.mult, tok, gtt, tmp.w, last[t])
            last[t] = [c.tt(V, c.x[:, t, s], c.x[:, t, s], tmp[:, t, :], ALU.add, e, c.x_t)]
            x_t[t].append(last[t][0])
            return e
        c.rows(Buf(gr[:, 0, :, :], 0, 0, []), wo, n * 512, 512, c.pb, to_x, mx)
    mem.give(gr, c.last_mm)
    mem.give(gt, x_t)
    mem.give(tmp, x_t)
    c.x_t = flat(x_t)


def first_hot(c, eq, n, base, out, t):
    mem, V = c.mem, c.V
    cand = mem.take("cand", [2, n])
    mn = mem.take("cmin", [2])
    t = c.stt(V, cand[:, :, :], eq, -64.0, base.unsqueeze(1).to_broadcast([128, 2, n]), ALU.mult, ALU.add, t, cand.w, c.eye_t)
    t = c.red(mn[:, :], cand[:, :, :], ALU.min, t, mn.w)
    t = c.tt(V, out, cand[:, :, :], mn[:, :].unsqueeze(2).to_broadcast([128, 2, n]), ALU.is_equal, t)
    mem.give(cand, t)
    mem.give(mn, t)
    return t


def route(c, h2, h2t):
    d, mem, V, A, G = c.d, c.mem, c.V, c.A, c.G
    rw, rb, rt = c.rw, c.rb, c.rw_t
    L = mem.take("logits", [2, 36])
    bank, bw = c.pa.take()
    for t in range(2):
        for k in range(8):
            m = c.mm(bank[:, t * 64:t * 64 + 36], h2[:, k, t * 128:t * 128 + 128], rw[:, k, :], k == 0, k == 7, h2t, rt, bw)
    lt = [c.tt(V, L[:, t, :], bank[:, t * 64:t * 64 + 36], rb[:, :], ALU.add, m, L.w, rt) for t in range(2)]
    c.pa.give(bank, lt)
    mem.give(rw, m)
    mem.give(rb, lt)
    gl, el = L[:, :, 0:4], L[:, :, 4:36].rearrange("p t (g e) -> p t e g", g=4)
    w = mem.take("rtw", [2, 96])
    iota = c.small[:, 0:32]
    gx, eq, oh = w[:, :, 0:4], w[:, :, 4:8], w[:, :, 8:12]
    one = lambda i: w[:, :, 12 + i]
    bc = lambda a, n: a.unsqueeze(2).to_broadcast([128, 2, n])
    gm, ps, m1, m2, e2, w1, w2, sm = (one(i) for i in range(8))
    t = c.red(gm, gl, ALU.max, lt, w.w)
    t1 = c.tt(V, gx, gl, bc(gm, 4), ALU.subtract, t)
    t2 = c.tt(V, eq, gl, bc(gm, 4), ALU.is_equal, t)
    ex = c.act(gx, gx, ACT.Exp, t1)
    to = first_hot(c, eq, 4, iota[:, 0:4], oh, t2)
    t = c.red(ps, gx, ALU.add, ex)
    tp = c.recip(ps, ps, t)
    pr = mem.take("prod", [2, 8, 4])
    t = c.tt(V, pr[:, :, :, :], el, oh.unsqueeze(2).to_broadcast([128, 2, 8, 4]), ALU.mult, to, pr.w, lt)
    ing, eq1, oh1, oh2 = (w[:, :, 24 + 8 * i:32 + 8 * i] for i in range(4))
    t = c.red(ing, pr[:, :, :, :], ALU.add, t)
    mem.give(pr, t)
    mem.give(L, t)
    t = c.red(m1, ing, ALU.max, t)
    t = c.tt(V, eq1, ing, bc(m1, 8), ALU.is_equal, t)
    to1 = first_hot(c, eq1, 8, iota[:, 0:8], oh1, t)
    t = c.stt(V, ing, oh1, NEG, ing, ALU.mult, ALU.add, to1)
    t = c.red(m2, ing, ALU.max, t)
    t2 = c.tt(V, e2, m2, m1, ALU.subtract, t)
    x2 = c.act(e2, e2, ACT.Exp, t2)
    t = c.tt(V, eq1, ing, bc(m2, 8), ALU.is_equal, t)
    to2 = first_hot(c, eq1, 8, iota[:, 0:8], oh2, t)
    t = c.ts(V, sm, e2, 1.0, None, ALU.add, None, x2)
    t = c.recip(sm, sm, t)
    tw1 = c.tt(V, w1, ps, sm, ALU.mult, t, tp)
    tw2 = c.tt(V, w2, w1, e2, ALU.mult, tw1)
    ab = mem.take("assign", [3, 2, 32])
    a1, a2, al = (ab[:, i, :, :] for i in range(3))
    c.wt = mem.take("wt", [2, 32])
    c.rk = mem.take("rk", [2, 32])
    as3 = lambda a, t: a[:, t, :].rearrange("p (g e) -> p g e", g=4)
    ta, tw = [], []
    for i in range(2):
        o4 = oh[:, i, :].unsqueeze(2).to_broadcast([128, 4, 8])
        s1 = c.tt(V, as3(a1, i), o4, oh1[:, i, :].unsqueeze(1).to_broadcast([128, 4, 8]), ALU.mult, to, to1, ab.w)
        s2 = c.tt(V, as3(a2, i), o4, oh2[:, i, :].unsqueeze(1).to_broadcast([128, 4, 8]), ALU.mult, to2, ab.w)
        ta.append(c.tt(V, al[:, i, :], a1[:, i, :], a2[:, i, :], ALU.add, s1, s2))
        s = c.ts(V, c.wt[:, i, :], a1[:, i, :], w1[:, i:i + 1], None, ALU.mult, None, s1, tw2, c.wt.w)
        tw.append(c.stt(V, c.wt[:, i, :], a2[:, i, :], w2[:, i:i + 1], c.wt[:, i, :], ALU.mult, ALU.add, s))
    bank, bw = c.pa.take()
    c.mm(bank[:, 0:32], c.eye[:, 1, :], al[:, 0, :], True, True, ta, bw)
    c.mm(bank[:, 32:64], c.eye[:, 2, :], al[:, 0, :], True, False)
    c.mm(bank[:, 32:64], c.eye[:, 1, :], al[:, 1, :], False, True)
    c.mm(bank[:, 64:96], c.eye[:, 2, :], al[:, 0, :], True, False)
    m = c.mm(bank[:, 64:96], c.eye[:, 2, :], al[:, 1, :], False, True)
    t = c.stt(V, c.rk[:, :, :], bank[:, 0:64].rearrange("p (t e) -> p t e", t=2), 1.0, al, ALU.add, ALU.mult, m, c.rk.w)
    c.rk_t = c.ts(V, c.rk[:, :, :], c.rk[:, :, :], -1.0, None, ALU.add, None, t)
    c.cnt = mem.take("cnt", [33])
    tc = c.cp(V, c.cnt[:, 0:32], bank[:, 64:96], m, c.cnt.w)
    t_ = c.red(c.cnt[:, 32:33], c.cnt[:, 0:32], ALU.max, tc)
    c.cnti = mem.take("cnti", [1], I32)
    c.cnt_t = c.cp(V, c.cnti[:, :], c.cnt[:, 32:33], t_, c.cnti.w)
    c.pa.give(bank, t, tc)
    mem.give(ab, c.rk_t, tw)
    mem.give(w, tw)
    c.wt_t = tw


def experts(c, xn, xnt, ax, shx, axt, gt, gtt):
    d, mem, V, A, G = c.d, c.mem, c.V, c.A, c.G
    w1, w3, w2 = (d[n][0] for n in ("expert_w1", "expert_w3", "expert_w2"))
    iota = c.small[:, 0:32].unsqueeze(1).to_broadcast([128, 4, 32])
    P = mem.take("P", [2, 2, 128])
    xg = [mem.take("xg", [8, 128]) for _ in range(2)]
    pw = [mem.take("pw", [256]) for _ in range(2)]
    last_x, last_pw, last_P = [[], []], [[], []], []

    def prepare(g):
        nonlocal last_P
        b = g % 2
        pt, ws = [], []
        for t in range(2):
            sel, wgt = (P[:, i, t, :].rearrange("p (e s) -> p e s", e=4) for i in range(2))
            e = c.tt(V, sel, c.rk[:, t, 4 * g:4 * g + 4].unsqueeze(2).to_broadcast([128, 4, 32]), iota, ALU.is_equal, c.rk_t, P.w, last_P)
            pt.append(e)
            ws.append(c.tt(V, wgt, sel, c.wt[:, t, 4 * g:4 * g + 4].unsqueeze(2).to_broadcast([128, 4, 32]), ALU.mult, e, c.wt_t))
        es = []
        for k4 in range(2):
            bank, bw = c.pa.take()
            for k in range(4):
                o = bank[:, k * 128:k * 128 + 128]
                kk = k4 * 4 + k
                for t in range(2):
                    m = c.mm(o, xn[:, t, kk * 128:kk * 128 + 128], P[:, 0, t, :], t == 0, t == 1, xnt, pt, bw)
            ev = []
            for k in range(4):
                o, kk = bank[:, k * 128:k * 128 + 128], k4 * 4 + k
                if k4:
                    ev.append(c.act(xg[b][:, kk, :], o, ACT.Identity, m, axt, xg[b].w, last_x[b], scale=ax[:, kk:kk + 1], bias=shx[:, kk:kk + 1]))
                else:
                    ev.append(c.ts(V, xg[b][:, kk, :], o, ax[:, kk:kk + 1], shx[:, kk:kk + 1], ALU.mult, ALU.add, m, axt, xg[b].w, last_x[b]))
            c.pa.give(bank, ev)
            es += ev
        bank, bw = c.pa.take()
        for t in range(2):
            m = c.tr(bank[:, t * 128:t * 128 + 128], P[:, 1, t, :], ws[t], bw)
        e = c.cp(A, pw[b][:, :], bank[:, 0:256], m, pw[b].w, last_pw[b])
        c.pa.give(bank, e)
        last_P = [m]
        return es, e
    ready = prepare(0)
    yield
    xt = {(t, h): c.x_t for t in range(2) for h in range(2)}
    sl = mem.take("mh", [2, 512])
    hT = mem.take("mhT", [4, 128])
    y = mem.take("my", [2, 512])
    hl, hTl, yl = [], [], [[], []]
    for g in range(8):
        (xe, pwt), xb = ready, xg[g % 2]
        b1, w1w = c.pa.take()
        b3, w3w = c.pa.take()
        for k in range(8):
            for w, bank, bw in ((w1, b1, w1w), (w3, b3, w3w)):
                s, v, lt = c.load(w[4 * g:4 * g + 4, k * 128:k * 128 + 128, :].rearrange("e p f -> p e f"))
                for j in range(4):
                    m = c.mm(bank[32 * j:32 * j + 32, :], xb[:, k, 32 * j:32 * j + 32], v[:, j, :], k == 0, k == 7, lt, xe, bw)
                c.done(s, m)
            yield
        last_x[g % 2] = [m]
        e1 = c.act(sl[:, 0, :], b1[:, :], ACT.Silu, m, sl.w, hl)
        e3 = c.tt(V, sl[:, 1, :], sl[:, 0, :], b3[:, :], ALU.mult, e1, m)
        c.pa.give(b1, e1)
        c.pa.give(b3, e3)
        if g < 7:
            ready = prepare(g + 1)
        yield
        bank, bw = c.pa.take()
        for k in range(4):
            m = c.tr(bank[:, k * 128:k * 128 + 128], sl[:, 1, k * 128:k * 128 + 128], e3, bw)
        hl = [m]
        e = c.cp(A, hT[:, :, :], bank[:, :].rearrange("p (k s) -> p k s", k=4), m, hT.w, hTl)
        c.pa.give(bank, e)
        yield
        for h in range(2):
            bank, bw = c.pa.take()
            for k in range(4):
                s, v, lt = c.load(w2[4 * g:4 * g + 4, k * 128:k * 128 + 128, h * 512:h * 512 + 512].rearrange("e p f -> p e f"))
                for j in range(4):
                    m = c.mm(bank[32 * j:32 * j + 32, :], hT[:, k, 32 * j:32 * j + 32], v[:, j, :], k == 0, k == 3, lt, e, bw)
                c.done(s, m)
                if k % 2:
                    yield
            hTl = [m]
            ey = c.tt(V, y[:, h, :], bank[:, :], gt[:, h * 512:h * 512 + 512], ALU.mult, m, gtt, y.w, yl[h])
            c.pa.give(bank, ey)
            for t in range(2):
                bank, bw = c.pa.take()
                m = c.mm(bank[:, :], pw[g % 2][:, t * 128:t * 128 + 128], y[:, h, :], True, True, ey, pwt, bw)
                o = c.x[:, t, h * 512:h * 512 + 512]
                xt[t, h] = c.tt(V, o, o, bank[:, :], ALU.add, m, xt[t, h])
                c.pa.give(bank, xt[t, h])
            yl[h] = [m]
            yield
        last_pw[g % 2] = [m]
    c.x_t = list(xt.values())
    mem.give(P, last_P)
    for i in range(2):
        mem.give(xg[i], last_x[i])
        mem.give(pw[i], m)
    mem.give(sl, hl)
    mem.give(hT, hTl)
    mem.give(y, yl)


def crowded(c):
    c.most = {}
    for q in (c.T, c.V, c.A, c.S):
        def fn(e, w, q=q):
            for t in w:
                e.wait_ge(*t.resolve())
            c.most[id(q)] = e.value_load(c.cnti[0:1, 0:1], min_val=0, max_val=256)
        q.raw(fn, c.cnt_t)


def beyond(c, xn, ax, shx, gt):
    d, mem, nc = c.d, c.mem, c.nc
    w1, w3, w2 = (d[n][0] for n in ("expert_w1", "expert_w3", "expert_w2"))
    N = 224
    P, XT, wa, wb, hh, pwT, y, tmp = (mem.take("o" + n, s) for n, s in (
        ("P", [2, 2, N]), ("XT", [8, N]), ("wa", [8, 512]), ("wb", [8, 512]), ("hh", [2, 4, N]),
        ("pwT", [2, 256]), ("y", [2, 1024]), ("tmp", [2, 2, 32])))
    bufs = (P, XT, wa, wb, hh, pwT, y, tmp)
    wc = wa[:, :, :].rearrange("p (k h) n -> p k (h n)", h=2)
    before = flat([b.w for b in bufs]) + [Tok(q, len(q.ops) - 1) for q in (c.T, c.V, c.A)]
    sv, sp, sa, sd = (c.sem("over_" + n) for n in "vpad")
    bk = c.banks
    slots = ((0, 128), (128, 96))
    iota = c.small[:, 64:288]

    def enter(e, w):
        for t in w:
            e.wait_ge(*t.resolve())

    def leave(e):
        e.wait_ge(sv, 32 * 7 + 1)

    def vec(e, w):
        with e.If(c.most[id(c.V)] > 32):
            enter(e, w)
            e.sem_inc(sv, 1)
            with e.Fori(0, 32) as i:
                e.wait_ge(sv, i * 7 + 1)
                for t in range(2):
                    e.tensor_scalar(P[:, 0, t, :], iota, c.rk[:, t, 0:1], None, ALU.is_equal)
                    m = e.tensor_scalar(P[:, 1, t, :], iota, c.rk[:, t, 0:1], c.wt[:, t, 0:1], ALU.is_equal, ALU.mult)
                m.then_inc(sv, 1)
                e.wait_ge(sp, i * 4 + 2)
                for k in range(8):
                    e.tensor_scalar(XT[:, k, :], bk[k // 2][:, (k % 2) * N:(k % 2) * N + N], ax[:, k:k + 1], shx[:, k:k + 1], ALU.mult, ALU.add)
                e.tensor_copy(pwT[:, 0, :], bk[4][:, 0:256])
                e.tensor_copy(pwT[0:96, 1, :], bk[4][0:96, 256:512]).then_inc(sv, 1)
                e.wait_ge(sa, i + 1)
                for h in range(2):
                    m = e.tensor_tensor(hh[:, 1, 2 * h:2 * h + 2, :], hh[:, 0, 2 * h:2 * h + 2, :],
                                        bk[(7 + h) % 8][:, 0:2 * N].rearrange("p (f s) -> p f s", f=2), ALU.mult)
                m.then_inc(sv, 1)
                e.wait_ge(sp, i * 4 + 4)
                for s, (_, n) in enumerate(slots):
                    for h in range(2):
                        m = e.tensor_tensor(y[0:n, s, h * 512:h * 512 + 512], bk[1 + 2 * s + h][0:n, :], gt[0:n, h * 512:h * 512 + 512], ALU.mult)
                m.then_inc(sv, 1)
                e.wait_ge(sp, i * 4 + 5)
                for t in range(2):
                    for h in range(2):
                        o = c.x[:, t, h * 512:h * 512 + 512]
                        m = e.tensor_tensor(o, o, bk[(5 + 2 * t + h) % 8][:, :], ALU.add)
                m.then_inc(sv, 1)
                e.tensor_copy(tmp[:, 0, :, 0:31], c.rk[:, :, 1:32])
                e.tensor_copy(tmp[:, 1, :, 0:31], c.wt[:, :, 1:32]).then_inc(sv, 1)
                e.wait_ge(sv, i * 7 + 7)
                e.tensor_copy(c.rk[:, :, 0:31], tmp[:, 0, :, 0:31])
                e.tensor_copy(c.wt[:, :, 0:31], tmp[:, 1, :, 0:31]).then_inc(sv, 1)
            leave(e)

    def pe(e, w):
        with e.If(c.most[id(c.T)] > 32):
            enter(e, w)
            e.sem_inc(sp, 1)
            with e.Fori(0, 32) as i:
                e.wait_ge(sv, i * 7 + 2)
                for k in range(8):
                    for t in range(2):
                        e.matmul(bk[k // 2][:, (k % 2) * N:(k % 2) * N + N], xn[:, t, k * 128:k * 128 + 128], P[:, 0, t, :], start=t == 0, stop=t == 1)
                for s, (s0, n) in enumerate(slots):
                    for t in range(2):
                        m = e.transpose(bk[4][0:n, s * 256 + t * 128:s * 256 + t * 128 + 128], P[:, 1, t, s0:s0 + n], c.eye[:, 0, :])
                m.then_inc(sp, 1)
                e.wait_ge(sv, i * 7 + 3)
                e.wait_ge(sd, i * 48 + 32)
                for b, wt in ((5, wa), (7, wb)):
                    for f in range(4):
                        for k in range(8):
                            m = e.matmul(bk[(b + f // 2) % 8][:, (f % 2) * N:(f % 2) * N + N], wt[:, k, f * 128:f * 128 + 128], XT[:, k, :], start=k == 0, stop=k == 7)
                m.then_inc(sp, 1)
                e.wait_ge(sv, i * 7 + 4)
                e.wait_ge(sd, i * 48 + 48)
                for s, (s0, n) in enumerate(slots):
                    for h in range(2):
                        for f in range(4):
                            m = e.matmul(bk[1 + 2 * s + h][0:n, :], hh[:, 1, f, s0:s0 + n], wc[:, f, h * 512:h * 512 + 512], start=f == 0, stop=f == 3)
                m.then_inc(sp, 1)
                e.wait_ge(sv, i * 7 + 5)
                for t in range(2):
                    for h in range(2):
                        for s, (_, n) in enumerate(slots):
                            m = e.matmul(bk[(5 + 2 * t + h) % 8][:, :], pwT[0:n, s, t * 128:t * 128 + 128], y[0:n, s, h * 512:h * 512 + 512], start=s == 0, stop=s == 1)
                m.then_inc(sp, 1)
            leave(e)

    def act(e, w):
        with e.If(c.most[id(c.A)] > 32):
            enter(e, w)
            with e.Fori(0, 32) as i:
                e.wait_ge(sp, i * 4 + 3)
                for h in range(2):
                    m = e.activation(hh[:, 0, 2 * h:2 * h + 2, :], bk[5 + h][:, 0:2 * N].rearrange("p (f s) -> p f s", f=2), ACT.Silu)
                m.then_inc(sa, 1)
            leave(e)

    def sp_(e, w):
        with e.If(c.most[id(c.S)] > 32):
            enter(e, w)
            with e.Fori(0, 32) as i:
                e.wait_ge(sp, i * 4 + 1)
                for dst, src in ((wa[:, :, :], w1), (wb[:, :, :], w3), (wc, w2)):
                    if src is w2:
                        e.wait_ge(sp, i * 4 + 3)
                    e.dma_start(dst, src[bass.ds(i, 1), :, :].rearrange("o (k p) n -> p (o k) n", p=128)).then_inc(sd, 16)
            leave(e)
    for q, fn in ((c.T, pe), (c.V, vec), (c.A, act), (c.S, sp_)):
        q.raw(fn, before)
    done = c.V(lambda e: e.drain())
    for b in bufs:
        mem.give(b, done)
    return done


def second_consts(c):
    d, mem, V, A, G = c.d, c.mem, c.V, c.A, c.G
    g = c.group("second")
    c.fft = mem.take("fft", [1280])
    c.rope2 = mem.take("rope2", [640])
    c.hd = mem.take("hd", [128])
    for b, n in ((c.fft, "k_fft"), (c.rope2, "k_rope2"), (c.hd, "k_hd")):
        G.dma(g, b[:, :], d[n], b.w)
    dl = mem.take("dl", [2, 4, 32])
    for i, n in enumerate(("diff_lq1_2", "diff_lk1_2", "diff_lq2_2", "diff_lk2_2")):
        G.dma(g, dl[:, :, i, :], d[n].rearrange("(o l) n -> o l n", o=1).to_broadcast([128, 2, 32]), dl.w)
    c.lam = mem.take("lam", [2, 2])
    c.subg = mem.take("subg", [2])
    for l in range(2):
        for i in range(2):
            G.dma(g, c.subg[64 * i:64 * i + 64, l:l + 1], d["diff_subln_g_2"][l:l + 1, :].rearrange("o n -> n o"), c.subg.w)
    c.second_t = g.all
    yield
    t = [c.tt(V, dl[:, :, 2 * i, :], dl[:, :, 2 * i, :], dl[:, :, 2 * i + 1, :], ALU.mult, g.all) for i in range(2)]
    t = [c.red(c.lam[:, i, :], dl[:, :, 2 * i, :], ALU.add, t[i], c.lam.w) for i in range(2)]
    mem.give(dl, t)
    t = c.act(c.lam[:, :, :], c.lam[:, :, :], ACT.Exp, t)
    init = [0.8 - 0.6 * math.exp(-0.3 * l) for l in range(2)]
    t = c.tt(V, c.lam[:, 0, :], c.lam[:, 1, :], c.lam[:, 0, :], ALU.subtract, t)
    c.lam_t, c.subg_t = [], []
    for l in range(2):
        c.lam_t.append(c.ts(V, c.lam[:, 0, l:l + 1], c.lam[:, 0, l:l + 1], -init[l], None, ALU.add, None, t))
        c.subg_t.append(c.ts(V, c.subg[:, l:l + 1], c.subg[:, l:l + 1], 1.0 - init[l], None, ALU.mult, None, g.all))
    yield


def attend(c, q, qt, nb, keys, vals, bias, lam, pool, evac):
    mem, V, A = c.mem, c.V, c.A
    nk = 256 * len(keys)
    P = [mem.take("ap", [nk]) for _ in range(2 * nb)]
    pt = [mem.take("apt", [nk // 128, 256]) for _ in range(2)]
    st = [mem.take("ast", [2 * nb]) for _ in range(2)]
    last_p, last_t, last_s = [[] for _ in range(2 * nb)], [[], []], [[], []]
    n = 0
    for pair in range(2):
        ob, ow = pool.take()
        for hh in range(2):
            h = 2 * pair + hh
            es = []
            for t in range(2):
                s = st[t]
                pe = []
                nm = []
                banks = []
                for b in range(nb):
                    bank, bw = pool.take()
                    for i, (kb, kt) in enumerate(keys):
                        with_bias = bias is not None and i == 0
                        o = bank[:, i * 256:i * 256 + 256]
                        m = c.mm(o, q[:, pair, hh * nb + b, t * 128:t * 128 + 128], kb[:, pair, :], True, not with_bias, qt, kt, bw)
                        if with_bias:
                            m = c.mm(o, c.eye[:, 3, :], bias[0][:, h, t, :], False, True, bias[1])
                    banks.append(bank)
                    x = c.red(s[:, b:b + 1], bank[:, 0:nk], ALU.max, m, st[t].w, last_s[t], negate=True)
                    nm.append(x)
                    k = t * nb + b
                    e = c.act(P[k][:, :], bank[:, 0:nk], ACT.Exp, x, P[k].w, last_p[k], bias=s[:, b:b + 1], accum=s[:, nb + b:nb + b + 1])
                    pool.give(bank, e)
                    pe.append(e)
                yield
                r = c.recip(s[:, nb:2 * nb], s[:, nb:2 * nb], pe)
                k = t * nb
                e = c.ts(V, P[k][:, :], P[k][:, :], s[:, nb:nb + 1], None, ALU.mult, None, r)
                if nb == 2:
                    r = c.tt(V, s[:, nb + 1:nb + 2], s[:, nb + 1:nb + 2], lam[0], ALU.mult, r, lam[1])
                    e = c.stt(V, P[k][:, :], P[k + 1][:, :], s[:, nb + 1:nb + 2], P[k][:, :], ALU.mult, ALU.add, e, r)
                    last_p[k + 1] = [e]
                last_s[t] = [e]
                bank, bw = pool.take()
                for i in range(nk // 128):
                    m = c.tr(bank[:, i * 128:i * 128 + 128], P[k][:, i * 128:i * 128 + 128], e, bw)
                last_p[k] = [m]
                e = c.cp(A, pt[hh][:, :, t * 128:t * 128 + 128], bank[:, 0:nk].rearrange("p (k q) -> p k q", q=128), m, pt[hh].w, last_t[hh])
                pool.give(bank, e)
                es.append(e)
                yield
            for i in range(nk // 128):
                vb, vt = vals[i // 2]
                m = c.mm(ob[64 * hh:64 * hh + 64, 0:256], vb[:, i % 2, h * 64:h * 64 + 64], pt[hh][:, i, :], i == 0, i == nk // 128 - 1, es, vt, ow)
            last_t[hh] = [m]
            yield
        pool.give(ob, evac(pair, ob[:, 0:256], m))
    for k in range(2 * nb):
        mem.give(P[k], last_p[k])
    for i in range(2):
        mem.give(pt[i], last_t[i])
        mem.give(st[i], last_s[i])


def masked(c, qm, q, qt, n, base, pool):
    toks = []
    for pair in range(2):
        for v in range(n):
            toks.append(c.ts(c.V, qm[:, pair, v, :], q(pair), c.small[:, base + v:base + v + 1], None, ALU.mult, None, qt(pair), qm.w, c.eye_t))
    return toks


def mixers(c, l, h, ht, own, kv, pool, jpool, y, name):
    d, mem, V, A, G = c.d, c.mem, c.V, c.A, c.G
    w = d["w_in_2"][l]
    y_t = y.toks = []
    jobs = []

    def step(n=1):
        for _ in range(n):
            if jobs and next(jobs[0], "end") == "end":
                jobs.pop(0)

    def pair_load(c0, n):
        a = c.load(w[0:512, c0:c0 + n].rearrange("(k p) c -> p k c", p=128))
        b = c.load(w[512:1024, c0:c0 + n].rearrange("(k p) c -> p k c", p=128))
        return a, b, (a[1], b[1]), [a[2], b[2]]

    def free(a, b):
        c.done(a[0], c.last_mm)
        c.done(b[0], c.last_mm)

    def new(n, shape):
        b = mem.take(name + n, shape)
        b.toks = []
        return b

    def keep(b, q=None):
        def evac(i, ps, t):
            e = c.cp(q or (A if i % 2 else V), b[:, i, :], ps, t, b.w)
            b.toks.append(e)
            return e
        return evac
    if not own:
        rp = d["na_rpb_2"]
        bias = new("bias", [4, 2, 256])
        mask = new("mask", [256])
        gb = c.group(name + "bias")
        for hh in range(4):
            for t in range(2):
                for r in range(2):
                    off = ((l * 4 + hh) * 15 + 6 - 2 * t + r) * 31 - 48
                    G.dma(gb, bias[64 * r:64 * r + 64, hh, t, :].rearrange("p (i k) -> p i k", i=4),
                          bass.AP(tensor=rp.tensor, offset=off, ap=[[1, 64], [31, 4], [1, 64]]), bias.w)
        G.dma(gb, mask[:, :], d["k_mask"][:, 0:256], mask.w)
        bt = c.tt(G, bias[:, :, :, :].rearrange("p h t k -> p (h t) k"), bias[:, :, :, :].rearrange("p h t k -> p (h t) k"),
                  mask[:, :].unsqueeze(1).to_broadcast([128, 8, 256]), ALU.add, gb.all)
        mem.give(mask, bt)
    ln = new("ln", [2, 256])
    ws = new("ws", [4, 128])
    gl = c.group(name + "ln")
    G.dma(gl, ln[:, 0, :], d["sgu_ln_g_2"][l:l + 1, :].to_broadcast([128, 256]), ln.w)
    G.dma(gl, ln[:, 1, :], d["sgu_ln_b_2"][l:l + 1, :].to_broadcast([128, 256]), ln.w)
    G.dma(gl, ws[:, :, :], d["sgu_w_2"][l].rearrange("g p q -> p g q"), ws.w)

    nk, nv, a_ = new("nk", [2, 256]), new("nv", [2, 256]), new("fa", [2, 256])
    qm = new("nq", [2, 2, 256])
    a, b, v, lt = pair_load(512, 512)
    for i in range(2):
        c.col_tile(h, v, i, pool, keep(nk), ht, lt)
    for t in range(2):
        c.tok_tile(h, v, 256, 256, t, pool, keep(nv), lt)
    free(a, b)
    yield
    a, b, v, lt = pair_load(0, 512)

    def to_qm(i, ps, t):
        e = [c.ts(V, qm[:, i - 2, u, :], ps, c.small[:, 48 + u:49 + u], None, ALU.mult, None, t, qm.w) for u in range(2)]
        qm.toks.extend(e)
        return e
    for i in range(2, 4):
        c.col_tile(h, v, i, pool, to_qm, ht, lt)
    for t in range(2):
        c.tok_tile(h, v, 0, 256, t, pool, keep(a_), lt)
    free(a, b)

    def window():
        def out(pair, ps, t):
            e = c.cp(A, y[:, 2 + pair, :], ps, t, y.w)
            y_t.append(e)
            return e
        if own:
            keys, vals = [(nk, nk.toks)], [(nv, nv.toks)]
        else:
            keys, vals = [(nk, nk.toks), (kv["nk"], kv["nk"].toks)], [(nv, nv.toks), (kv["nv"], kv["nv"].toks)]
        yield from attend(c, qm, qm.toks, 1, keys, vals, None if own else (bias, bt), None, jpool, out)
        e = c.pe_last()
        mem.give(qm, e)
        if not own:
            for b_ in (bias, nk, nv, kv["nk"], kv["nv"]):
                mem.give(b_, e)

    def fourier():
        f = new("ff", [2, 512])
        for i in range(2):
            bank, bw = jpool.take()
            for k in range(2):
                m = c.mm(bank[:, :], a_[:, k, i * 128:i * 128 + 128], c.fft[:, k * 512:k * 512 + 512], k == 0, k == 1, a_.toks, c.second_t, bw)
            e = c.cp(A, f[:, i, :], bank[:, :], m, f.w)
            jpool.give(bank, e)
            f.toks.append(e)
            yield
        mem.give(a_, m)
        bank, bw = jpool.take()
        for i in range(2):
            for k in range(2):
                m = c.mm(bank[:, i * 256:i * 256 + 256], c.fft[:, 1024 + k * 128:1152 + k * 128], f[:, i, k * 256:k * 256 + 256], k == 0, k == 1, f.toks, bw)
        e = c.cp(A, y[:, 0:2, :], bank[:, :].rearrange("p (i t) -> p i t", i=2), m, y.w)
        jpool.give(bank, e)
        mem.give(f, m)
        y_t.append(e)
        yield
    jobs += [window(), fourier()]
    yield
    step()
    dq, dk, dv = new("dq", [2, 256]), new("dk", [2, 256]), new("dv", [2, 256])
    dm = new("dm", [2, 4, 256])
    a, b, v, lt = pair_load(1536, 512)

    def to_dm(i, ps, t):
        e = [c.ts(V, dm[:, i, u, :], ps, c.small[:, 40 + u:41 + u], None, ALU.mult, None, t, dm.w) for u in range(4)]
        dm.toks.extend(e)
        return e
    kd = keep(dk)
    for i in range(4):
        if i < 2:
            c.col_tile(h, v, i, pool, to_dm if own else keep(dq), ht, lt)
        else:
            c.col_tile(h, v, i, pool, lambda i_, ps, t: kd(i_ - 2, ps, t), ht, lt)
        step()
        yield
    free(a, b)
    a, b, v, lt = pair_load(2048, 256)
    for t in range(2):
        c.tok_tile(h, v, 0, 256, t, pool, keep(dv), lt)
        step()
        yield
    free(a, b)

    def spin(x, out):
        bank, bw = jpool.take()
        for i in range(2):
            m = c.mm(bank[:, i * 256:i * 256 + 256], c.rope2[:, 512:640], x[:, i, :], True, True, x.toks, c.second_t, bw)
        cos = c.rope2[:, 0:256].unsqueeze(1).to_broadcast([128, 2, 256])
        sin = c.rope2[:, 256:512].unsqueeze(1).to_broadcast([128, 2, 256])
        e = c.tt(V, out[:, :, :], bank[:, :].rearrange("p (i t) -> p i t", i=2), sin, ALU.mult, m, out.w)
        jpool.give(bank, e)
        f = c.tt(V, x[:, :, :], x[:, :, :], cos, ALU.mult, m)
        out.toks.append(c.tt(V, out[:, :, :], out[:, :, :], x[:, :, :], ALU.add, e, f))
        mem.give(x, out.toks)

    def differential():
        k_ = dk
        if not own:
            qr, k_ = new("dqr", [2, 256]), new("dkr", [2, 256])
            spin(dq, qr)
            yield
            spin(dk, k_)
            dm.toks += masked(c, dm, lambda p: qr[:, p, :], lambda p: qr.toks, 4, 40, jpool)
            mem.give(qr, dm.toks)
            yield
        else:
            mem.give(dq)
        od = new("od", [2, 256])
        sq = new("osq", [2, 256])

        def out(pair, ps, t):
            e = c.cp(A, od[:, pair, :], ps, t, od.w)
            sq.toks.append(c.act(sq[:, pair, :], od[:, pair, :], ACT.Square, e, sq.w))
            od.toks.append(e)
            return e
        if own:
            keys, vals = [(dk, dk.toks)], [(dv, dv.toks)]
        else:
            keys, vals = [(k_, k_.toks), (kv["dk"], kv["dk"].toks)], [(dv, dv.toks), (kv["dv"], kv["dv"].toks)]
        yield from attend(c, dm, dm.toks, 2, keys, vals, None, (c.lam[:, 0, l:l + 1], c.lam_t[l]), jpool, out)
        e = c.pe_last()
        mem.give(dm, e)
        if not own:
            for b_ in (k_, dv, kv["dk"], kv["dv"]):
                mem.give(b_, e)
        bank, bw = jpool.take()
        for i in range(2):
            m = c.mm(bank[:, i * 256:i * 256 + 256], c.hd[:, :], sq[:, i, :], True, True, sq.toks, bw, c.second_t)
        t = c.act(sq[:, :, :], bank[:, :].rearrange("p (i t) -> p i t", i=2), ACT.Sqrt, m, bias=c.eps, scale=1.0 / 64)
        jpool.give(bank, t)
        yield
        t = c.recip(sq[:, :, :], sq[:, :, :], t)
        e = c.stt(V, y[:, 6:8, :], od[:, :, :], c.subg[:, l:l + 1], sq[:, :, :], ALU.mult, ALU.mult, t, od.toks, c.subg_t[l], y.w)
        y_t.append(e)
        mem.give(od, e)
        mem.give(sq, e)
        yield
    jobs.append(differential())
    uv = new("uv", [2, 512])

    def to_uv(t, ps, tok):
        e = c.act(uv[:, t, :], ps, ACT.Gelu_apprx_tanh, tok, uv.w)
        uv.toks.append(e)
        return e
    a, b, v, lt = pair_load(1024, 512)
    for t in range(2):
        c.tok_tile(h, v, 0, 512, t, pool, to_uv, ht, lt)
        step(2)
        yield
    free(a, b)
    y.h_free = c.last_mm

    def gating():
        st = new("lst", [4])
        t0 = []
        vc = uv[:, :, 256:512]
        t = c.red(st[:, 0:2], vc, ALU.add, uv.toks, st.w)
        t = c.ts(V, st[:, 0:2], st[:, 0:2], -1.0 / 256, None, ALU.mult, None, t)
        sqb = new("lsq", [2, 256])
        for i in range(2):
            e = c.ts(V, uv[:, i, 256:512], uv[:, i, 256:512], st[:, i:i + 1], None, ALU.add, None, t)
            t0.append(c.act(sqb[:, i, :], uv[:, i, 256:512], ACT.Square, e, sqb.w, st.w, accum=st[:, 2 + i:3 + i]))
        r = c.rstd(st[:, 2:4], st[:, 2:4], 256.0, t0)
        mem.give(sqb, t0)
        et = []
        for i in range(2):
            o = uv[:, i, 256:512]
            e = c.stt(V, o, o, st[:, 2 + i:3 + i], ln[:, 0, :], ALU.mult, ALU.mult, r, gl.all)
            et.append(c.tt(V, o, o, ln[:, 1, :], ALU.add, e))
        mem.give(st, et)
        mem.give(ln, et)
        yield
        wT = new("wsT", [4, 128])
        bank, bw = jpool.take()
        for g_ in range(4):
            m = c.tr(bank[:, g_ * 128:g_ * 128 + 128], ws[:, g_, :], gl.all, bw)
        e = c.cp(A, wT[:, :, :], bank[:, :].rearrange("p (g q) -> p g q", g=4), m, wT.w)
        jpool.give(bank, e)
        mem.give(ws, m)
        yield
        bank, bw = jpool.take()
        for g_ in range(4):
            m = c.mm(bank[:, g_ * 128:g_ * 128 + 128], wT[:, g_, :], uv[:, :, 256 + g_ * 64:320 + g_ * 64], True, True, e, et, bw)
        mem.give(wT, m)
        es = []
        for g_ in range(4):
            u_ = uv[:, :, g_ * 64:g_ * 64 + 64]
            es.append(c.stt(V, u_, bank[:, g_ * 128:g_ * 128 + 128].rearrange("p (t n) -> p t n", t=2), column(c, "sb_2", 1, l * 4 + g_), u_, ALU.add, ALU.mult, m, c.vec_t))
        jpool.give(bank, es)
        yield
        bank, bw = jpool.take()
        for i in range(2):
            for t_ in range(2):
                m = c.tr(bank[:, i * 256 + t_ * 128:i * 256 + t_ * 128 + 128], uv[:, t_, i * 128:i * 128 + 128], es, bw)
        e = c.cp(A, y[:, 4:6, :], bank[:, :].rearrange("p (i t) -> p i t", i=2), m, y.w)
        jpool.give(bank, e)
        mem.give(uv, m)
        y_t.append(e)
        yield
    jobs.append(gating())
    while jobs:
        step()
        yield
    if own:
        kv.update(nk=nk, nv=nv, dk=dk, dv=dv)


def last_keys(c, l, h, ht, kv, pool, name):
    mem, V, A = c.mem, c.V, c.A
    w = c.d["w_in_2"][l]
    for c0, k, v_ in ((512, "nk", "nv"), (1792, "dk", "dv")):
        bufs = [mem.take(name + n, [2, 256]) for n in (k, v_)]
        for b in bufs:
            b.toks = []
        a, av, at = c.load(w[0:512, c0:c0 + 512].rearrange("(k p) c -> p k c", p=128))
        b, bv, bt = c.load(w[512:1024, c0:c0 + 512].rearrange("(k p) c -> p k c", p=128))

        def keep(buf):
            def evac(i, ps, t):
                e = c.cp(A if i % 2 else V, buf[:, i, :], ps, t, buf.w)
                buf.toks.append(e)
                return e
            return evac
        for i in range(2):
            c.col_tile(h, (av, bv), i, pool, keep(bufs[0]), ht, at, bt)
        for t in range(2):
            c.tok_tile(h, (av, bv), 256, 256, t, pool, keep(bufs[1]), ht, at, bt)
        c.done(a, c.last_mm)
        c.done(b, c.last_mm)
        kv[k], kv[v_] = bufs
        yield


def add_gated(c, x, xt, gate, gt, tmp, last, n):
    def evac(t, ps, tok):
        s = slice(n * 512, n * 512 + 512)
        e = c.tt(c.V, tmp[:, t, :], ps, gate[:, s], ALU.mult, tok, gt, tmp.w, last[t])
        last[t] = [c.tt(c.V, x[:, t, s], x[:, t, s], tmp[:, t, :], ALU.add, e, xt)]
        x.new.append(last[t][0])
        return e
    return evac


def ffn(c, l, h, ht, x, xt, gate, gt, pool, acc_pool, name):
    d, mem, V, A = c.d, c.mem, c.V, c.A
    w1, w2 = d["w_ff1_2"][l], d["w_ff2_2"][l]
    acc = [[acc_pool.take() for _ in range(2)] for _ in range(2)]
    hid = [mem.take(name + "hid", [8, 256]) for _ in range(2)]
    rl = [mem.take(name + "relu", [256]) for _ in range(2)]
    last_h, last_r = [[], []], [[], []]
    for blk in range(4):
        b = blk % 2
        et = [None] * 8
        for n in range(2):
            def relu2(i, ps, t):
                k = n * 4 + i
                r = k % 2
                e = c.act(rl[r][:, :], ps, ACT.Relu, t, rl[r].w, last_r[r])
                et[k] = c.tt(V, hid[b][:, k, :], rl[r][:, :], rl[r][:, :], ALU.mult, e, hid[b].w, last_h[b])
                last_r[r] = [et[k]]
                return e
            c.cols(h, w1, blk * 1024 + n * 512, 512, pool, relu2, ht)
            yield
        for k2 in range(4):
            r0 = blk * 1024 + k2 * 256
            s, v, lt = c.load(w2[r0:r0 + 256, :].rearrange("(k p) n -> p k n", p=128))
            for kk in range(2):
                k = k2 * 2 + kk
                first, final = blk == 0 and k == 0, blk == 3 and k == 7
                for t in range(2):
                    for n in range(2):
                        m = c.mm(acc[t][n][0][:, :], hid[b][:, k, t * 128:t * 128 + 128], v[:, kk, n * 512:n * 512 + 512], first, final, et[k], lt, acc[t][n][1])
            c.done(s, m)
            yield
        last_h[b] = [m]
    for i in range(2):
        mem.give(hid[i], m)
        mem.give(rl[i], last_r[i])
    x.new = []
    tmp = mem.take(name + "tmp", [2, 512])
    last = [[], []]
    for n in range(2):
        ev = add_gated(c, x, xt, gate, gt, tmp, last, n)
        for t in range(2):
            acc_pool.give(acc[t][n][0], ev(t, acc[t][n][0][:, :], m))
    mem.give(tmp, x.new)
    yield


def layer(c, l, x, xt, m, which, kv, pool, jpool, fpool, apool, name):
    mem = c.mem
    own = which == 1
    xn, xnt = c.normed(x, name + "xn", xt)
    a, sh, at = scale_shift(c, m, which, 0, 1, column(c, "n1_2", 8, 8 * l), name + "a")
    h = mem.take(name + "h", [8, 256])
    ht = c.turned(xn, xnt, a, sh, h, pool, at)
    mem.give(xn, c.pe_last())
    mem.give(a, ht)
    yield
    y = mem.take(name + "y", [8, 256])
    yield from mixers(c, l, h, ht, own, kv, pool, jpool, y, name)
    mem.give(h, y.h_free)
    gate = mem.take(name + "g", [1024])
    gt = c.gate(m, which, 2, jpool, gate)
    tmp = mem.take(name + "t", [2, 512])
    x.new, last = [], [[], []]
    for n in range(2):
        c.rows(y, c.d["w_out_2"][l], n * 512, 512, pool, add_gated(c, x, xt, gate, gt, tmp, last, n), y.toks)
        yield
    mem.give(y, c.last_mm)
    mem.give(tmp, x.new)
    mem.give(gate, x.new)
    xt = x.new
    xn, xnt = c.normed(x, name + "xn", xt)
    a, sh, at = scale_shift(c, m, which, 3, 4, column(c, "n2_2", 8, 8 * l), name + "a")
    h = mem.take(name + "h", [8, 256])
    ht = c.turned(xn, xnt, a, sh, h, pool, at)
    mem.give(xn, c.pe_last())
    mem.give(a, ht)
    gate = mem.take(name + "g", [1024])
    gt = c.gate(m, which, 5, jpool, gate)
    yield
    yield from ffn(c, l, h, ht, x, xt, gate, gt, fpool, apool, name)
    mem.give(h, c.last_mm)
    mem.give(gate, x.new)
    x.toks = x.new


def context_path(c, pool):
    yield from layer(c, 0, c.cx, c.cx_t, c.mods["m2"], 1, c.kv[0], pool, pool, pool, pool, "c0")


def context_keys(c, pool):
    mem = c.mem
    xn, xnt = c.normed(c.cx, "c1xn", c.cx.toks)
    mem.give(c.cx, xnt)
    m = c.mods["m3"]
    a, sh, at = scale_shift(c, m, 1, 0, 1, column(c, "n1_2", 8, 8), "c1a")
    h = mem.take("c1h", [8, 256])
    ht = c.turned(xn, xnt, a, sh, h, pool, at)
    mem.give(xn, c.pe_last())
    mem.give(a, ht)
    yield
    yield from last_keys(c, 1, h, ht, c.kv[1], pool, "c1")
    mem.give(h, c.last_mm)


def normed_by(c, x, xt, gain, gt, out):
    mem, V = c.mem, c.V
    xn, t = c.normed(x, "fin", xt)
    toks = [c.tt(V, out[:, i, :], xn[:, i, :], gain[:, :], ALU.mult, t, gt) for i in range(2)]
    mem.give(xn, toks)
    return toks


def run(gens):
    gens = list(gens)
    while gens:
        for g in list(gens):
            if next(g, "end") == "end":
                gens.remove(g)


def program(nc, d, out):
    with ExitStack() as ctx:
        c = Core(nc, ctx, d)
        mem = c.mem
        c.pa, c.pb = Pool(c.banks[0:3]), Pool(c.banks[3:8])
        c.hf_t, c.st_t, c.dm_t = [], [], []
        c.kv = [{}, {}]
        setup(c)
        vectors(c)
        first_mix(c)

        m1 = c.mods["m1"]
        xn, xt = c.normed(c.x, "xn2", c.x_t)
        ax, sh, at = scale_shift(c, m1, 0, 3, 4, column(c, "n2", 8), "ax2")
        c.rw, c.rb = mem.take("rw", [8, 36]), mem.take("rb", [36])
        g = c.group("router")
        c.G.dma(g, c.rw[:, :, 0:4], d["router_group_w"][0].rearrange("(k p) n -> p k n", p=128), c.rw.w)
        c.G.dma(g, c.rw[:, :, 4:36], d["router_expert_w"][0].rearrange("(k p) n -> p k n", p=128), c.rw.w)
        c.G.dma(g, c.rb[:, 0:4], d["router_group_b"].to_broadcast([128, 4]), c.rb.w)
        c.G.dma(g, c.rb[:, 4:36], d["router_expert_b"].to_broadcast([128, 32]), c.rb.w)
        c.rw_t = g.all
        h2 = mem.take("h2", [8, 256])
        h2t = c.turned(xn, xt, ax, sh, h2, c.pb, at)
        route(c, h2, h2t)
        mem.give(h2, c.pe_last())
        gate = mem.take("gt2", [1024])
        gtt = c.gate(m1, 0, 5, c.pa, gate)
        mem.give(m1["sb"], c.pe_last())

        c.cx = mem.take("cx", [2, 1024])
        g = c.group("cx")
        c.S.dma(g, c.cx[:, :, :], d["ctx_2"].rearrange("o (t p) n -> p (o t) n", p=128), c.cx.w)
        c.cx_t = g.all
        for _ in second_consts(c):
            pass
        cond, ct = c.conds[1]
        run([c.ada("m2", d["ada_w_2"][0], d["ada_b_2"][0], cond, c.pb, c.pa, ct)])

        crowded(c)
        run([experts(c, xn, xt, ax, sh, at, gate, gtt), context_path(c, c.pb)])
        c.x_t = [beyond(c, xn, ax, sh, gate)]
        for b in (xn, gate, c.rk, c.wt, c.cnt, c.cnti, ax, m1["col"][0], m1["col"][1]):
            mem.give(b, c.x_t)
        gain = mem.take("gain", [1024])
        g = c.group("gain")
        c.S.dma(g, gain[:, :], d["final_norm_g"].rearrange("(o n) -> o n", o=1).to_broadcast([128, 1024]), gain.w)
        x_t = normed_by(c, c.x, c.x_t, gain, g.all, c.x)
        mem.give(gain, x_t)
        run([layer(c, 0, c.x, x_t, c.mods["m2"], 0, c.kv[0], c.pb, c.pa, c.pa, c.pb, "x0"),
             c.ada("m3", d["ada_w_2"][1], d["ada_b_2"][1], cond, c.pb, c.pa, ct)])
        run([context_keys(c, c.pb)])
        run([layer(c, 1, c.x, c.x.toks, c.mods["m3"], 0, c.kv[1], c.pb, c.pa, c.pa, c.pb, "x1")])
        gain = mem.take("gain2", [1024])
        g = c.group("gain2")
        c.S.dma(g, gain[:, :], d["final_g_2"].rearrange("(o n) -> o n", o=1).to_broadcast([128, 1024]), gain.w)
        x_t = normed_by(c, c.x, c.x.toks, gain, g.all, c.x)
        c.S.dma(c.outs, out.rearrange("o (t p) n -> p (o t) n", p=128), c.x[:, :, :], x_t)

        number([c.T, c.V, c.A, c.G, c.S])
        with nc.Block() as block:
            @block.tensor
            def _(e):
                c.T.play(e)

            @block.vector
            def _(e):
                c.V.play(e)

            @block.scalar
            def _(e):
                c.A.play(e)

            @block.gpsimd
            def _(e):
                c.G.play(e)

            @block.sync
            def _(e):
                c.S.play(e)
                e.wait_ge(c.outs.sem, c.outs.n)
    return c


_INS = ['x', 'c', 'ctx', 'c_ctx', 'ada_w', 'ada_b', 'norm1_g', 'norm2_g', 'w_in', 'b_in', 'ret_decay_logit', 'ret_w_o',
        'hy_conv_w', 'hy_conv_b', 'hy_ffn_w1', 'hy_ffn_b1', 'hy_ffn_freq', 'hy_ffn_w2', 'hy_ffn_b2', 'hy_ffn_w3', 'hy_skip',
        'hy_w_o', 'w_out', 'router_group_w', 'router_group_b', 'router_expert_w', 'router_expert_b', 'expert_w1', 'expert_w3',
        'expert_w2', 'final_norm_g', 'c_2', 'ctx_2', 'c_ctx_2', 'ada_w_2', 'ada_b_2', 'norm1_g_2', 'norm2_g_2', 'w_in_2',
        'w_out_2', 'na_rpb_2', 'sgu_ln_g_2', 'sgu_ln_b_2', 'sgu_w_2', 'sgu_b_2', 'diff_lq1_2', 'diff_lk1_2', 'diff_lq2_2',
        'diff_lk2_2', 'diff_subln_g_2', 'w_ff1_2', 'w_ff2_2', 'final_g_2']


def kernel(**inputs):
    import numpy as _np
    import concourse.bacc as _bacc
    from concourse import mybir as _mybir
    from concourse.bass_utils import run_bass_kernel_spmd as _run

    nc = _bacc.Bacc("TRN2", target_bir_lowering=False, num_devices=1)
    arrays, d = {}, {}
    named = [(n, _np.ascontiguousarray(inputs[n])) for n in _INS] + list(constants().items())
    for name, a in named:
        arrays[f"in_{name}_dram"] = a
        d[name] = nc.dram_tensor(f"in_{name}_dram", a.shape, _mybir.dt.from_np(a.dtype), kind="ExternalInput").ap()
    out = nc.dram_tensor("out_0_dram", (1, 256, 1024), _mybir.dt.float32, kind="ExternalOutput").ap()
    program(nc, d, out)
    r = _run(nc, [arrays], core_ids=[0])
    return r.results[0]["out_0_dram"]
```

```python
import math
from contextlib import ExitStack

import numpy as np

import concourse.bass as bass
from concourse import mybir
from concourse.alu_op_type import AluOpType as ALU

F32 = mybir.dt.float32
F32R = mybir.dt.float32r
I32 = mybir.dt.int32
ACT = mybir.ActivationFunctionType
AX = mybir.AxisListType

EPS = 1e-6
NEG = -1.0e30


def _rope(n_freq):
    t = np.arange(256)
    inv = (10000.0 ** (-np.arange(n_freq, dtype=np.float32) / np.float32(n_freq))).astype(np.float32)
    row = (t // 64).astype(np.float32)[None, :] * inv[:, None]
    col = (t % 64).astype(np.float32)[None, :] * inv[:, None]
    return np.cos(row), np.sin(row), np.cos(col), np.sin(col)


def _swap(n, width):
    m = np.zeros((n, n), np.float32)
    for b in range(0, n, 2 * width):
        for i in range(width):
            m[b + width + i, b + i] = -1.0
            m[b + i, b + width + i] = 1.0
    return m


def constants():
    f = np.float32
    c = {}
    p = np.arange(128)
    c["k_eye"] = np.stack([np.eye(128), p[:, None] < p[None, :], np.ones((128, 128)), np.eye(128)[::-1]], 1).astype(f)
    small = np.zeros((128, 288), f)
    small[:, 0:32] = np.arange(32)
    small[:, 32] = EPS
    for v in range(4):
        small[32 * v:32 * v + 32, 40 + v] = 32.0 ** -0.5
    for v in range(2):
        small[64 * v:64 * v + 64, 48 + v] = 0.125
    j = (np.arange(2)[None, :] * 128 + p[:, None]).astype(f)
    small[:, 50:52] = 255 - j
    small[:, 52:54] = j
    small[:, 54:56] = j + 1
    small[:, 56:58] = 256 - j
    small[:, 64:288] = np.arange(32, 256)
    c["k_small"] = small
    i = np.arange(256)
    jj = j[:, :, None]
    c["k_ret"] = np.concatenate([np.maximum(i[None, None, :] - jj, 0).reshape(128, 512),
                                 np.maximum(jj - i[None, None, :], 0).reshape(128, 512)], 1).astype(f)
    cr, sr, cc, sc = _rope(32)
    c["k_rope"] = np.concatenate([np.concatenate([cr, cr, cc, cc], 0), np.concatenate([sr, sr, sc, sc], 0), _swap(128, 32)], 1).astype(f)
    cr, sr, cc, sc = _rope(8)
    c["k_rope2"] = np.concatenate([np.tile(np.concatenate([cr, cr, cc, cc], 0), (4, 1)),
                                   np.tile(np.concatenate([sr, sr, sc, sc], 0), (4, 1)), _swap(128, 8)], 1).astype(f)
    t = np.arange(256, dtype=np.float64)
    ang = 2 * np.pi * (np.outer(t, t) % 512) / 512
    co, si = np.cos(ang), np.sin(ang)
    alt = (-1.0) ** t
    si1, co1 = si.copy(), co.copy()
    si1[:, 0] = alt
    co1[:, 0] = alt
    blocks = [co[:, :128], co[:, 128:], si[:, :128], si[:, 128:], si1[:, :128], co1[:, :128]]
    fw = np.stack([b.reshape(2, 128, 128) for b in blocks], 0)
    c["k_dft"] = fw.transpose(2, 0, 1, 3).reshape(128, 1536).astype(f)
    ic, isn = co * 2 / 512, si * 2 / 512
    ic[0] = 1.0 / 512
    isn[0] = alt / 512
    inv = np.concatenate([ic, isn], 0).reshape(4, 128, 256)
    c["k_idft"] = inv.transpose(1, 0, 2).reshape(128, 1024).astype(f)
    tn = (np.arange(256, dtype=f) / f(256)).astype(f)
    bands = np.linspace(1e-4, 15, 16, dtype=f)
    ph = (f(2.0 * math.pi) * tn[:, None] * bands[None, :]).astype(f)
    c["k_feat"] = np.ascontiguousarray(np.concatenate([tn[:, None], np.cos(ph), -np.sin(ph)], 1).T).astype(f)
    slow, fast = abs(math.log(1e-2)) / 1.5, abs(math.log(1e-2)) / 0.3
    deltas = np.tile(np.linspace(slow, fast, 512, dtype=f), 2)
    dec = np.exp((-tn[:, None] * deltas[None, :]).astype(f)).astype(f)
    c["k_decay"] = np.ascontiguousarray(dec.reshape(2, 128, 1024).transpose(1, 0, 2).reshape(128, 2048))
    ang = 2 * np.pi * (np.outer(t, t) % 256) / 256
    cs = np.concatenate([np.cos(ang), np.sin(ang)], 1).reshape(2, 128, 512)
    d = np.arange(64)
    a64 = 2 * np.pi * (np.outer(d, d) % 64) / 64
    bd = np.zeros((2, 128, 128))
    for h in range(2):
        s = slice(64 * h, 64 * h + 64)
        bd[0, s, s] = np.cos(a64) / 128
        bd[1, s, s] = -np.sin(a64) / 128
    c["k_fft"] = np.concatenate([cs.transpose(1, 0, 2).reshape(128, 1024), bd.transpose(1, 0, 2).reshape(128, 256)], 1).astype(f)
    hd = np.zeros((128, 128), f)
    hd[:64, :64] = 1
    hd[64:, 64:] = 1
    c["k_hd"] = hd
    mask = np.zeros((128, 2, 256), f)
    q = np.arange(64)
    start = np.clip(q - 8, 0, 48)
    inw = (q[None, :] >= start[:, None]) & (q[None, :] < start[:, None] + 16)
    m64 = np.where(inw, 0.0, NEG).astype(f)
    full = np.tile(m64, (2, 4))
    mask[:, :, :] = full[::-1][:, None, :]
    c["k_mask"] = mask.reshape(128, 512)
    return {k: np.ascontiguousarray(v, dtype=f) for k, v in c.items()}


class Tok:
    def __init__(self, q, i):
        self.q, self.i = q, i

    def resolve(self):
        return self.q.sem, self.q.count[self.i]


class DTok:

    def __init__(self, owner, val):
        self.owner, self.val = owner, val

    def resolve(self):
        return self.owner.sem, self.owner.n if self.val is None else self.val


def flat(x):
    if x is None:
        return []
    if isinstance(x, (list, tuple)):
        return [t for y in x for t in flat(y)]
    return [x]


class Queue:
    def __init__(self, sem):
        self.sem, self.ops, self.count = sem, [], {}

    def __call__(self, fn, *waits):
        self.ops.append((fn, flat(waits), False))
        return Tok(self, len(self.ops) - 1)

    def raw(self, fn, *waits):
        w = flat(waits)
        self.ops.append((lambda e: fn(e, w), w, True))

    def dma(self, owner, dst, src, *waits):
        self.ops.append((lambda e: e.dma_start(dst, src).then_inc(owner.sem, 16), flat(waits), False))
        owner.n += 16
        return DTok(owner, owner.n)

    def play(self, eng):
        seen = {}
        for i, (fn, waits, raw) in enumerate(self.ops):
            if raw:
                fn(eng)
                continue
            need = {}
            for w in waits:
                sem, val = w.resolve()
                need[sem.name] = (sem, max(val, need.get(sem.name, (sem, 0))[1]))
            for name, (sem, val) in need.items():
                if seen.get(name, 0) < val:
                    eng.wait_ge(sem, val)
                    seen[name] = val
            ins = fn(eng)
            if i in self.count:
                ins.then_inc(self.sem, 1)


def number(queues):
    wanted = {}
    for q in queues:
        for _, waits, _ in q.ops:
            for w in waits:
                if isinstance(w, Tok):
                    wanted.setdefault(id(w.q), set()).add(w.i)
    for q in queues:
        for n, i in enumerate(sorted(wanted.get(id(q), ()))):
            q.count[i] = n + 1


class Loads:

    def __init__(self, sem):
        self.sem, self.n = sem, 0

    @property
    def all(self):
        return DTok(self, None)


class Slot:
    def __init__(self, ap, sem):
        self.ap, self.sem, self.n, self.last = ap, sem, 0, []


class Pool:

    def __init__(self, banks):
        self.free = [(b, []) for b in banks]

    def take(self):
        return self.free.pop(0)

    def give(self, bank, *toks):
        self.free.append((bank, flat(toks)))


class Buf:
    def __init__(self, t, lo, hi, w):
        self.t, self.lo, self.hi, self.w = t, lo, hi, w

    def __getitem__(self, k):
        return self.t[k]


class Mem:

    def __init__(self, nc, lo, hi):
        self.nc, self.free, self.n, self.end, self.low = nc, [(lo, hi, [])], 0, hi, hi - lo
        self.live = {}

    def take(self, name, shape, dtype=F32, parts=128, top=False):
        size = (4 * int(np.prod(shape)) + 31) // 32 * 32
        spans = []
        for lo, hi, toks in self.free:
            if spans and spans[-1][1] == lo:
                spans[-1] = (spans[-1][0], hi)
            else:
                spans.append((lo, hi))
        spans = [x for x in spans if x[1] - x[0] >= size]
        if not spans:
            raise MemoryError(f"{name} {size}: free {[(a, b) for a, b, _ in self.free]} live {self.live}")
        lo = spans[-1][1] - size if top else spans[0][0]
        toks, rest = [], []
        for a, b, t in self.free:
            if b <= lo or a >= lo + size:
                rest.append((a, b, t))
                continue
            toks += t
            if a < lo:
                rest.append((a, lo, t))
            if b > lo + size:
                rest.append((lo + size, b, t))
        self.free = rest
        self.n += 1
        t = self.nc.alloc_sbuf_tensor_at(f"{name}_{self.n}", [parts, *shape], dtype, offset=lo)
        self.low = min(self.low, sum(b - a for a, b, _ in self.free))
        buf = Buf(t, lo, lo + size, toks)
        buf.key = name + f"_{self.n}"
        self.live[buf.key] = size
        return buf

    def give(self, buf, *toks):
        del self.live[buf.key]
        self.free.append((buf.lo, buf.hi, flat(toks)))
        self.free.sort(key=lambda x: x[0])


class Op:

    def __init__(self, raw=None, hi=None, lo=None, toks=None):
        self.raw, self.hi, self.lo, self.toks = raw, hi, lo, toks if toks is not None else []


class Stream:

    def __init__(self, c, items, split, ahead):
        self.c, self.split, self.ahead = c, split, ahead
        self.todo = [(src, v, k, len(vs)) for src, vs in items for k, v in enumerate(vs)]
        self.ready, self.at, self.slot = [], 0, None

    def issue(self):
        c = self.c
        src, view, k, n = self.todo[self.at]
        if k == 0:
            if not c.slots:
                return False
        if self.split and not c.pairs:
            return False
        if k == 0:
            self.slot = c.load(src)
        self.at += 1
        s, v, lt = self.slot
        w = view(v)
        if not self.split:
            self.ready.append((Op(raw=w, toks=[lt]), s, k == n - 1))
            return True
        hi, lo, free = c.pairs.pop(0)
        a, b = w.shape[1:]
        hv, lv = (x[:, 0:a * b].rearrange("p (a b) -> p a b", a=a) for x in (hi, lo))
        t = c.cp(c.A, hv, w, lt, free)
        t = c.tt(c.V, lv, w, hv.bitcast(F32), ALU.subtract, lt, t, free)
        if k == n - 1:
            c.done(s, t)
        self.ready.append((Op(hi=hv, lo=lv, toks=[t]), (hi, lo), None))
        return True

    def get(self):
        while len(self.ready) <= self.ahead and self.at < len(self.todo):
            if not self.issue():
                break
        self.part = self.ready.pop(0)
        return self.part[0]

    def done(self, *toks):
        _, owner, last = self.part
        if self.split:
            self.c.pairs.append((*owner, flat(toks)))
        elif last:
            self.c.done(owner, *toks)


def by_cols(w, c0, n=256):
    return w[:, c0:c0 + n].rearrange("(k p) c -> p k c", p=128), [lambda v: v[:, 0:4, :], lambda v: v[:, 4:8, :]]


class Core:

    def __init__(self, nc, ctx, dram):
        self.nc, self.ctx, self.d = nc, ctx, dram
        self.T, self.V, self.A, self.G, self.S = (Queue(self.sem(n)) for n in ("pe", "dve", "act", "pool", "sp"))
        self.mem = Mem(nc, 16896, 229344)
        self.banks = [ctx.enter_context(nc.psum_tensor(f"bank{i}", [128, 512], F32)) for i in range(8)]
        self.p = Pool(self.banks)
        self.slots, self.pairs, self.nslot = [], [], 0
        self.slot_bufs, self.pair_bufs, self.slot_sems = {}, {}, []
        self.fillers = []
        self.outs = Loads(self.sem("stores"))

    def sem(self, name):
        return self.ctx.enter_context(self.nc.semaphore(name))

    def group(self, name):
        return Loads(self.sem(name))

    def more_slots(self, n):
        for _ in range(n):
            b = self.mem.take("slot", [2048])
            s = self.slot_sems.pop() if self.slot_sems else Slot(None, self.sem(f"ring{self.nslot}"))
            self.nslot += 1
            s.ap, s.last, s.buf = b.t, b.w, b
            self.slots.append(s)

    def less_slots(self, n):
        for _ in range(n):
            s = self.slots.pop(0)
            self.mem.give(s.buf, s.last)
            self.slot_sems.append(s)

    def more_pairs(self, n):
        for _ in range(n):
            hi, lo = (self.mem.take(x, [1024], F32R) for x in ("whi", "wlo"))
            self.pair_bufs[id(hi)] = (hi, lo)
            self.pairs.append((hi, lo, hi.w + lo.w))

    def less_pairs(self, n):
        for _ in range(n):
            hi, lo, toks = self.pairs.pop(0)
            self.mem.give(hi, toks)
            self.mem.give(lo, toks)

    def load(self, src):
        s = self.slots.pop(0)
        shape = src.shape
        n = int(np.prod(shape[1:]))
        dst = s.ap[:, 0:n]
        if len(shape) == 3:
            dst = dst.rearrange("p (a b) -> p a b", a=shape[1])
        tok = self.S.dma(s, dst, src, s.last)
        return s, dst, tok

    def done(self, slot, *toks):
        slot.last = flat(toks)
        self.slots.append(slot)

    def fill(self, n):
        while n > 0 and self.fillers:
            if next(self.fillers[0], "end") == "end":
                self.fillers.pop(0)
            else:
                n -= 1

    def pe_last(self):
        return Tok(self.T, len(self.T.ops) - 1)

    def mm(self, out, lhsT, rhs, start, stop, *w):
        return self.T(lambda e: e.matmul(out, lhsT, rhs, start=start, stop=stop), *w)

    def tr(self, out, in_, *w):
        n = in_.shape[0]
        ident = self.eye[0:n, 0, 0:n]
        return self.T(lambda e: e.transpose(out, in_, ident), *w)

    def tt(self, q, out, a, b, op, *w):
        return q(lambda e: e.tensor_tensor(out, a, b, op), *w)

    def ts(self, q, out, a, s1, s2, op0, op1, *w):
        if op1 is None:
            return q(lambda e: e.tensor_scalar(out, a, s1, None, op0), *w)
        return q(lambda e: e.tensor_scalar(out, a, s1, s2, op0, op1), *w)

    def stt(self, q, out, in0, s, in1, op0, op1, *w):
        return q(lambda e: e.scalar_tensor_tensor(out, in0, s, in1, op0, op1), *w)

    def cp(self, q, out, in_, *w):
        if q is self.A:
            return q(lambda e: e.copy(out, in_), *w)
        return q(lambda e: e.tensor_copy(out, in_), *w)

    def act(self, out, in_, func, *w, bias=None, scale=None, accum=None):
        kw = {}
        if bias is not None:
            kw["bias"] = bias
        if scale is not None:
            kw["scale"] = scale
        if accum is not None:
            kw["accum_out"] = accum
        return self.A(lambda e: e.activation(out, in_, func, **kw), *w)

    def red(self, out, in_, op, *w, negate=False):
        if negate:
            return self.V(lambda e: e.tensor_reduce(out, in_, AX.X, op, negate=True), *w)
        return self.V(lambda e: e.tensor_reduce(out, in_, AX.X, op), *w)

    def recip(self, out, in_, *w):
        return self.V(lambda e: e.reciprocal(out, in_), *w)

    def set(self, q, out, val, *w):
        return q(lambda e: e.memset(out, val), *w)

    def rstd(self, out, sums, width, *w):
        t = self.act(out, sums, ACT.Sqrt, *w, bias=self.eps[0:out.shape[0]], scale=1.0 / width)
        return self.recip(out, out, t)

    def normed(self, src, name, *w):
        xn = self.mem.take(name, [2, 1024])
        ss = self.mem.take(name + "s", [2])
        a = [self.act(xn[:, t, :], src[:, t, :], ACT.Square, w, xn.w, ss.w, accum=ss[:, t:t + 1]) for t in range(2)]
        r = self.rstd(ss[:, :], ss[:, :], 1024.0, a)
        toks = [self.ts(self.V, xn[:, t, :], src[:, t, :], ss[:, t:t + 1], None, ALU.mult, None, r) for t in range(2)]
        self.mem.give(ss, toks)
        return xn, toks

    def operand(self, name, shape, split, top=False):
        if split:
            return Op(hi=self.mem.take(name + "h", shape, F32R, top=top), lo=self.mem.take(name + "l", shape, F32R, top=top))
        return Op(raw=self.mem.take(name, shape, top=top))

    def drop(self, op, *toks):
        for b in (op.raw, op.hi, op.lo):
            if b is not None:
                self.mem.give(b, *toks)

    def part(self, op, k, src, *w):
        hi, lo = op.hi[:, k], op.lo[:, k]
        t = self.cp(self.A, hi, src, w, op.hi.w)
        t = self.tt(self.V, lo, src, hi.bitcast(F32), ALU.subtract, t, w, op.lo.w)
        op.toks.append(t)
        return t

    def turned(self, xn, toks, scale, shift, op, *w):
        tmp, last = None, [[], []]
        if op.hi is not None:
            tmp = [self.mem.take("turn", [2, 256], top=True) for _ in range(2)]
        for k2 in range(4):
            bank, bw = self.p.take()
            for k in range(2):
                for t in range(2):
                    m = self.tr(bank[:, k * 256 + t * 128:k * 256 + t * 128 + 128],
                                xn[:, t, (2 * k2 + k) * 128:(2 * k2 + k + 1) * 128], toks[t], bw, self.eye_t)
            b = k2 % 2
            out = tmp[b] if tmp else op.raw
            e = []
            for k in range(2):
                kt = 2 * k2 + k
                o, i = out[:, k if tmp else kt, :], bank[:, k * 256:k * 256 + 256]
                if b:
                    e.append(self.act(o, i, ACT.Identity, m, w, out.w, last[b], scale=scale[:, kt:kt + 1], bias=shift[:, kt:kt + 1]))
                else:
                    e.append(self.ts(self.V, o, i, scale[:, kt:kt + 1], shift[:, kt:kt + 1], ALU.mult, ALU.add, m, w, out.w, last[b]))
            self.p.give(bank, e)
            if tmp:
                last[b] = [self.part(op, slice(2 * k2, 2 * k2 + 2), tmp[b][:, :, :], e)]
            else:
                op.toks += e
        if tmp:
            for b in range(2):
                self.mem.give(tmp[b], last[b])

    def passes(self, a, b):
        if a.raw is not None:
            return ((a.raw, b.raw),)
        return (a.hi, b.hi), (a.hi, b.lo), (a.lo, b.hi)

    def unit(self, stream, nparts, consumers, kpart=4):
        groups = [(kind, h, evac, i, *self.p.take()) for kind, h, evac in consumers for i in range(2)]
        last = [None] * len(groups)
        for part in range(nparts):
            u = stream.get()
            for n, (kind, h, _, i, bank, bw) in enumerate(groups):
                s = slice(i * 128, i * 128 + 128)
                for k in range(kpart):
                    kk = part * kpart + k
                    if kind == "cols":
                        ops = [(a[:, k, s], b[:, kk, :]) for a, b in self.passes(u, h)]
                    else:
                        ops = [(b[:, kk, s], a[:, k, :]) for b, a in self.passes(h, u)]
                    for j, (a, b) in enumerate(ops):
                        last[n] = self.mm(bank[:, 0:256], a, b, kk == 0 and j == 0, kk == nparts * kpart - 1 and j == len(ops) - 1,
                                          u.toks, h.toks, bw)
            stream.done(last[-1])
        self.last_mm = last[-1]
        for n, (kind, h, evac, i, bank, bw) in enumerate(groups):
            self.p.give(bank, evac(i, bank[:, 0:256], last[n]))

    def ada(self, name, w, bias, cond, ct):
        c = self
        m = {"sb": c.mem.take(name + "sb", [3, 512]), "col": [c.mem.take(name + f"c{i}", [48]) for i in range(2)], "t": [None] * 3, "ct": [None] * 3}
        self.mods[name] = m
        for q in range(3):
            br = c.mem.take(name + "b", [512], top=True)
            z = c.set(c.G, br[:, :], 0.0, br.w)
            g = c.group(f"{name}b{q}")
            for i in range(2):
                c.G.dma(g, br[i::32, :], bias[q * 2048:q * 2048 + 2048].rearrange("(j n) -> j n", j=4), z)
            bank, bw = self.p.take()
            for k in range(8):
                s, v, lt = c.load(w[k * 128:k * 128 + 128, q * 2048:q * 2048 + 2048])
                for j in range(4):
                    t = c.mm(bank[32 * j:32 * j + 32, :], cond[:, k, :], v[:, j * 512:j * 512 + 512], k == 0, k == 7, lt, bw, ct)
                c.done(s, t)
                if k < 7:
                    yield
            m["t"][q] = e = c.tt(c.V, m["sb"][:, q, :], bank[:, :], br[:, :], ALU.add, t, g.all, m["sb"].w)
            self.p.give(bank, e)
            c.mem.give(br, e)
            yield
            bank, bw = self.p.take()
            for b in range(4):
                t = c.tr(bank[:, b * 128:b * 128 + 128], m["sb"][:, q, b * 128:b * 128 + 128], e, bw, c.eye_t)
            v = bank[:, :].rearrange("p (b j r) -> p j b r", b=4, j=4)
            e = [c.cp(c.V, m["col"][i][:, q * 16:q * 16 + 16].rearrange("p (j b) -> p j b", j=4), v[:, :, :, i], t, m["col"][i].w) for i in range(2)]
            self.p.give(bank, e)
            m["ct"][q] = e
            if q < 2:
                yield

    def gate(self, m, which, seg, dst):
        toks = []
        for h in range(2):
            r = 32 * ((seg % 2) * 2 + h) + which
            o, i, t = dst[:, h * 512:h * 512 + 512], m["sb"], m["t"][seg // 2]
            if which == 0:
                src = i[r:r + 1, seg // 2, :]
                toks.append(self.G(lambda e, o=o, src=src: e.partition_broadcast(o, src), t, dst.w))
                continue
            bank, bw = self.p.take()
            t = self.mm(bank[:, :], self.eye[:, 0, r:r + 1].to_broadcast([128, 128]), i[:, seg // 2, :], True, True, t, bw, self.eye_t)
            e = self.cp(self.A, o, bank[:, :], t, dst.w)
            self.p.give(bank, e)
            toks.append(e)
        return toks


def setup(c):
    d, mem, T, V, A, G, S = c.d, c.mem, c.T, c.V, c.A, c.G, c.S
    c.mods = {}
    c.small = mem.take("small", [288])
    c.eye = mem.take("eye", [4, 128])
    c.eps = c.small[:, 32:33]
    c.x = mem.take("x", [2, 1024])
    r0 = mem.take("r0", [128], parts=32)
    g0, g1, g2 = c.group("g0"), c.group("g1"), c.group("ctx")
    A.dma(g0, r0[0:8, :], d["c"].rearrange("o (k p) -> (o k) p", p=128))
    A.dma(g0, r0[8:16, :], d["c_ctx"].rearrange("(k p) -> k p", p=128))
    A.dma(g0, r0[16:24, :], d["c_2"].rearrange("o (k p) -> (o k) p", p=128))
    A.dma(g0, r0[24:32, :], d["c_ctx_2"].rearrange("(k p) -> k p", p=128))
    S.dma(g0, c.eye[:, :, :], d["k_eye"])
    S.dma(g0, c.small[:, :], d["k_small"])
    c.eye_t = g0.all

    r1 = mem.take("r1", [128])
    r2 = mem.take("r2", [128], parts=40)
    g = c.group("vec")
    lay, at = {}, 0
    z = c.set(V, r1[:, :], 0.0, r1.w)
    for name, n, src in (("n1", 8, d["norm1_g"]), ("n2", 8, d["norm2_g"]), ("b_in", 52, d["b_in"]), ("cw", 36, d["hy_conv_w"]),
                         ("cb", 12, d["hy_conv_b"]), ("skip", 4, d["hy_skip"])):
        if len(src.shape) == 3:
            src = src.rearrange("o a n -> o (a n)")
        A.dma(g, r1[at:at + n, :], src.rearrange("o (k p) -> (o k) p", p=128), z)
        lay[name] = at
        at += n
    lay2, at = {}, 0
    for name, n, src in (("n1_2", 16, d["norm1_g_2"]), ("n2_2", 16, d["norm2_g_2"]), ("sb_2", 8, None)):
        src = src.rearrange("l (k p) -> (l k) p", p=128) if src is not None else d["sgu_b_2"].rearrange("l g p -> (l g) p")
        A.dma(g, r2[at:at + n, :], src, r2.w)
        lay2[name] = at
        at += n
    c.rows = (r1, r2, g)
    c.col = {k: v for k, v in lay.items()} | {k: v + 128 for k, v in lay2.items()}
    S.dma(g1, c.x[:, :, :], d["x"].rearrange("o (t p) n -> p (o t) n", p=128))
    c.x_t = g1.all
    c.ctx_ = mem.take("ctx", [2, 1024])
    c.ctx_t = g2.all

    bank, bw = c.p.take()
    t = c.tr(bank[:, 0:32], r0[:, :], g0.all, bw)
    c.conds = []
    for i in range(2):
        s = mem.take(f"cond{i}", [8, 32])
        z = c.set(V, s[:, :, :], 0.0, s.w)
        e = c.act(s[:, :, 0:2].rearrange("p k w -> p w k"), bank[:, 16 * i:16 * i + 16].rearrange("p (w k) -> p w k", w=2), ACT.Silu, t, z)
        c.conds.append((s, e))
    c.p.give(bank, [e for _, e in c.conds])
    mem.give(r0, t)
    c.ctx_g = g2


def vectors(c):
    r1, r2, g = c.rows
    c.S.dma(c.ctx_g, c.ctx_[:, :, :], c.d["ctx"].rearrange("o (t p) n -> p (o t) n", p=128))
    c.xn, c.xnt = c.normed(c.x, "xn", c.x_t)
    c.vec = c.mem.take("vec", [168])
    bank, bw = c.p.take()
    c.tr(bank[:, 0:128], r1[:, :], g.all, bw, c.eye_t)
    t = c.tr(bank[:, 128:168], r2[:, :])
    c.vec_t = c.cp(c.V, c.vec[:, :], bank[:, 0:168], t, c.vec.w)
    c.p.give(bank, c.vec_t)
    c.mem.give(r1, t)
    c.mem.give(r2, t)


def column(c, name, n, at=0):
    b = c.col[name] + at
    return c.vec[:, b:b + n]


def scale_shift(c, m, which, seg_shift, seg_scale, gain, name):
    a = c.mem.take(name, [8])
    t = c.stt(c.V, a[:, :], m["col"][which][:, seg_scale * 8:seg_scale * 8 + 8], 1.0, gain, ALU.add, ALU.mult,
              m["ct"][seg_scale // 2], c.vec_t, a.w)
    return a, m["col"][which][:, seg_shift * 8:seg_shift * 8 + 8], [t, m["ct"][seg_shift // 2]]


def sine(c, arg, n, t, out, *w):
    mem, V = c.mem, c.V
    k = mem.take("sink", [256])
    magic = 12582912.0
    c1 = 6.28125
    c2 = float(np.float32(np.round((2 * math.pi - c1) * 2 ** 22) / 2 ** 22))
    c3 = float(np.float32(2 * math.pi - c1 - c2))
    a, kk = arg[0:n, :], k[0:n, :]
    t = c.ts(V, kk, a, 1 / (2 * math.pi), magic, ALU.mult, ALU.add, t, k.w)
    t = c.ts(V, kk, kk, magic, None, ALU.subtract, None, t)
    for cc in (c1, c2, c3):
        t = c.stt(V, a, kk, -cc, a, ALU.mult, ALU.add, t)
    t = c.ts(V, a, a, 3.1415925, -3.1415925, ALU.min, ALU.max, t)
    mem.give(k, t)
    return c.act(out, a, ACT.Sin, t, w)


def filters(c):
    d, mem, V, A, G = c.d, c.mem, c.V, c.A, c.G
    g = c.group("hyf")
    feat, w1, w2, w3, sc = (mem.take(n, s) for n, s in (("feat", [256]), ("hw1", [64]), ("hw2", [64]), ("hw3", [1024]), ("hsc", [3])))
    for dst, src, b in ((feat[0:33, :], d["k_feat"], feat), (w1[0:33, :], d["hy_ffn_w1"][0], w1), (w2[0:64, :], d["hy_ffn_w2"][0], w2),
                        (w3[0:64, :], d["hy_ffn_w3"][0], w3), (sc[0:64, 0:1], d["hy_ffn_b1"].rearrange("o n -> n o"), sc),
                        (sc[0:64, 1:2], d["hy_ffn_b2"].rearrange("o n -> n o"), sc), (sc[0:64, 2:3], d["hy_ffn_freq"].rearrange("o n -> n o"), sc)):
        G.dma(g, dst, src, b.w)
    dft = c.dft = mem.take("dft", [6, 2, 128])
    G.dma(g, dft[:, :, :, :], d["k_dft"].rearrange("p (b k f) -> p b k f", b=6, k=2), dft.w)
    decay = mem.take("decay", [2, 1024])
    G.dma(g, decay[:, :, :], d["k_decay"].rearrange("p (t n) -> p t n", t=2), decay.w)
    c.dft_t = g.all
    yield
    arg = mem.take("harg", [256])
    hid = mem.take("hid", [256])
    t = None
    for w, b, rhs, kk in ((w1, 0, feat, 33), (w2, 1, hid, 64)):
        bank, bw = c.p.take()
        t = c.mm(bank[0:64, 0:256], w[0:kk, :], rhs[0:kk, :], True, True, g.all, bw, t)
        e = c.ts(V, arg[0:64, :], bank[0:64, 0:256], sc[0:64, b:b + 1], sc[0:64, 2:3], ALU.add, ALU.mult, t, arg.w)
        c.p.give(bank, e)
        t = sine(c, arg, 64, e, hid[0:64, :], hid.w)
        yield
    filt = mem.take("filt", [2, 1024])
    ab = mem.take("fabs", [2, 1024])
    es, ea = [], []
    for tt in range(2):
        for h in range(2):
            bank, bw = c.p.take()
            m = c.mm(bank[:, :], hid[0:64, tt * 128:tt * 128 + 128], w3[0:64, h * 512:h * 512 + 512], True, True, t, bw)
            o = filt[:, tt, h * 512:h * 512 + 512]
            e = c.tt(V, o, bank[:, :], decay[:, tt, h * 512:h * 512 + 512], ALU.mult, m, filt.w)
            c.p.give(bank, e)
            es.append(e)
            ea.append(c.act(ab[:, tt, h * 512:h * 512 + 512], o, ACT.Abs, e, ab.w))
            yield
    mem.give(feat, t); mem.give(w1, t); mem.give(w2, t); mem.give(w3, m); mem.give(sc, es); mem.give(arg, t); mem.give(hid, m)
    mem.give(decay, es)
    inv = mem.take("finv", [2, 512])
    er = []
    for h in range(2):
        bank, bw = c.p.take()
        for tt in range(2):
            m = c.mm(bank[:, :], c.eye[:, 2, :], ab[:, tt, h * 512:h * 512 + 512], tt == 0, tt == 1, ea, bw)
        e = c.recip(inv[:, h, :], bank[:, :], m, inv.w)
        c.p.give(bank, e)
        er.append(e)
        yield
    mem.give(ab, m)
    fn = []
    for h in range(2):
        for tt in range(2):
            o = filt[:, tt, h * 512:h * 512 + 512]
            fn.append(c.tt(G, o, o, inv[:, h, :], ALU.mult, er[h], es))
    mem.give(inv, fn)
    yield
    sm = mem.take("fsum", [2, 2, 512])
    hs = [c.tt(G, sm[:, i, :, :], filt[:, :, 0:512], filt[:, :, 512:1024], op, fn, sm.w) for i, op in enumerate((ALU.add, ALU.subtract))]
    mem.give(filt, hs)
    c.hf = mem.take("hf", [5, 512])
    c.hf_t = []
    for i, (blk, s) in enumerate(((0, 0), (1, 0), (2, 1), (3, 1), (5, 0))):
        bank, bw = c.p.take()
        for k in range(2):
            m = c.mm(bank[:, :], dft[:, blk, k, :], sm[:, s, k, :], k == 0, k == 1, hs, bw)
        e = c.cp(A, c.hf[:, i, :], bank[:, :], m, c.hf.w)
        c.p.give(bank, e)
        c.hf_t.append(e)
        yield
    mem.give(sm, m)


def hyena(c, u, ut):
    d, mem, V, A, G = c.d, c.mem, c.V, c.A, c.G
    cv = mem.take("conv", [12, 256])
    ct = []
    for k in range(12):
        o = cv[:, k, :]
        w = lambda j: column(c, "cw", 1, 12 * j + k)
        t = c.ts(V, o, u[:, k, 1:257], w(1), column(c, "cb", 1, k), ALU.mult, ALU.add, ut[k], cv.w, c.vec_t)
        t = c.stt(V, o, u[:, k, 0:256], w(0), o, ALU.mult, ALU.add, t)
        t = c.stt(V, o, u[:, k, 2:258], w(2), o, ALU.mult, ALU.add, t)
        ct.append(t)
        if k % 4 == 3:
            yield
    mem.give(u, ct)
    z = cv[:, 4:8, :]
    zt = c.tt(V, z, z, cv[:, 8:12, :], ALU.mult, ct)
    ztok = mem.take("ztok", [2, 512])
    e = []
    for t in range(2):
        bank, bw = c.p.take()
        for k in range(4):
            m = c.tr(bank[:, k * 128:k * 128 + 128], cv[:, 4 + k, t * 128:t * 128 + 128], zt, bw)
        e.append(c.cp(A, ztok[:, t, :], bank[:, :], m, ztok.w))
        c.p.give(bank, e[-1])
        yield
    while not c.hf_t or len(c.hf_t) < 5:
        yield
    zf = mem.take("zf", [4, 512])
    ez = []
    for i, blk in enumerate((0, 1, 4, 3)):
        bank, bw = c.p.take()
        for k in range(2):
            m = c.mm(bank[:, :], c.dft[:, blk, k, :], ztok[:, k, :], k == 0, k == 1, e, bw, c.dft_t)
        ez.append(c.cp(A, zf[:, i, :], bank[:, :], m, zf.w))
        c.p.give(bank, ez[-1])
        yield
    mem.give(ztok, m)
    mem.give(c.dft, m)
    yf = mem.take("yf", [4, 512])
    tmp = mem.take("yt", [2, 512])
    hr, hi = c.hf[:, 0:2, :], c.hf[:, 2:4, :]
    zc, zs = zf[:, 0:2, :], zf[:, 2:4, :]
    a = c.tt(V, yf[:, 0:2, :], zc, hr, ALU.mult, ez, c.hf_t, yf.w)
    b = c.tt(G, tmp[:, :, :], zs, hi, ALU.mult, ez, c.hf_t, tmp.w)
    y1 = c.tt(V, yf[:, 0:2, :], yf[:, 0:2, :], tmp[:, :, :], ALU.subtract, a, b)
    b = c.tt(G, tmp[:, :, :], zc, hi, ALU.mult, ez, c.hf_t, y1)
    a0 = c.tt(V, yf[:, 2, :], zf[:, 2, :], c.hf[:, 4, :], ALU.mult, ez, c.hf_t, yf.w)
    a1 = c.tt(V, yf[:, 3, :], zf[:, 3, :], c.hf[:, 1, :], ALU.mult, ez, c.hf_t, yf.w)
    y2 = c.tt(V, yf[:, 2:4, :], yf[:, 2:4, :], tmp[:, :, :], ALU.add, a0, a1, b)
    mem.give(zf, y1, y2)
    mem.give(c.hf, y1, y2)
    mem.give(tmp, y1, y2)
    yield
    idft = mem.take("idft", [4, 256])
    g = c.group("idft")
    G.dma(g, idft[:, :, :], d["k_idft"].rearrange("p (b t) -> p b t", b=4), idft.w)
    yield
    done = []
    out = c.hy = c.operand("hy", [4, 256], True)
    tmp = mem.take("hyt", [2, 256])
    for k in range(4):
        bank, bw = c.p.take()
        for i in range(4):
            m = c.mm(bank[:, 0:256], yf[:, i, k * 128:k * 128 + 128], idft[:, i, :], i == 0, i == 3, y1, y2, bw, g.all)
        o = tmp[:, k % 2, :]
        e = c.stt(V, o, cv[:, 4 + k, :], column(c, "skip", 1, k), bank[:, 0:256], ALU.mult, ALU.add, m, tmp.w, done[-2:])
        c.p.give(bank, e)
        e = c.tt(V, o, o, cv[:, k, :], ALU.mult, e)
        done.append(c.part(out, k, o, e))
        yield
    mem.give(tmp, done)
    mem.give(yf, m)
    mem.give(idft, m)
    mem.give(cv, done)


def decays(c):
    d, mem, V, A, G = c.d, c.mem, c.V, c.A, c.G
    g = c.group("decay")
    lg = mem.take("lg", [8])
    w = mem.take("lgw", [5, 8])
    ret = mem.take("kret", [1024])
    G.dma(g, lg[:, :], d["ret_decay_logit"].rearrange("o a h -> o (a h)").to_broadcast([128, 8]), lg.w)
    G.dma(g, ret[:, :], d["k_ret"], ret.w)
    e, u, dd, z, s = (w[:, i, :] for i in range(5))
    t = c.act(e, lg[:, :], ACT.Abs, g.all, w.w)
    t = c.act(e, e, ACT.Exp, t, scale=-1.0)
    t = c.ts(V, u, e, 1.0, None, ALU.add, None, t, w.w)
    t1 = c.act(s, u, ACT.Ln, t, w.w)
    t = c.ts(V, dd, u, -1.0, None, ALU.add, None, t, w.w)
    tz = c.ts(V, z, dd, 0.0, None, ALU.is_equal, None, t, w.w)
    t = c.tt(V, dd, dd, z, ALU.add, tz)
    t = c.recip(dd, dd, t)
    t = c.tt(V, dd, dd, s, ALU.mult, t, t1)
    t = c.tt(V, dd, dd, z, ALU.add, t)
    t = c.tt(V, dd, dd, e, ALU.mult, t)
    t = c.stt(V, lg[:, :], lg[:, :], 0.0, dd, ALU.min, ALU.subtract, t)
    mem.give(w, t)
    yield
    c.dk = mem.take("dk", [2, 4, 2])
    c.dq = mem.take("dq", [2, 4, 2])
    c.dm = mem.take("dm", [4, 512])
    c.dk_t, c.dq_t, c.dm_t = [], [], []
    for i in range(2):
        for h in range(4):
            l = lg[:, i * 4 + h:i * 4 + h + 1]
            c.dk_t.append(c.act(c.dk[:, i, h, :], c.small[:, 50 + 2 * i:52 + 2 * i], ACT.Exp, t, c.dk.w, scale=l))
            c.dq_t.append(c.act(c.dq[:, i, h, :], c.small[:, 54 + 2 * i:56 + 2 * i], ACT.Exp, t, c.dq.w, scale=l))
    c.dk_t = [c.ts(V, c.dk[:, :, :, :], c.dk[:, :, :, :], 128.0 ** -0.5, None, ALU.mult, None, c.dk_t)]
    yield
    last = []
    for h in range(4):
        o = c.dm[:, h, :]
        t1 = c.ts(V, o, ret[:, 0:512], lg[:, h:h + 1], None, ALU.mult, None, t, c.dm.w)
        t1 = c.stt(V, o, ret[:, 512:1024], lg[:, 4 + h:5 + h], o, ALU.mult, ALU.add, t1)
        last.append(t1)
        c.dm_t.append(c.act(o, o, ACT.Exp, t1))
        yield
    mem.give(ret, last)
    mem.give(lg, last, c.dq_t, c.dk_t)


def states(c, kc, kct, vc, vct):
    mem, V, A, G = c.mem, c.V, c.A, c.G
    c.st = mem.take("st", [4, 2, 256])
    c.st_t = []
    kd = mem.take("kd", [2, 2, 2, 128])
    last = [[], []]
    for h in range(4):
        b = h % 2
        kt = []
        for i in range(2):
            for t in range(2):
                kt.append(c.ts(V, kd[:, b, i, t, :], kc[:, t, h * 128:h * 128 + 128], c.dk[:, i, h, t:t + 1], None, ALU.mult, None,
                               kct, c.dk_t, kd.w, last[b]))
        bank, bw = c.p.take()
        for i in range(2):
            for t in range(2):
                m = c.mm(bank[:, i * 256:i * 256 + 256], kd[:, b, i, t, :], vc[:, t, h * 256:h * 256 + 256], t == 0, t == 1, kt, vct, bw)
        last[b] = m
        e = c.cp(A, c.st[:, h, :, :], bank[:, :].rearrange("p (i v) -> p i v", i=2), m, c.st.w)
        c.p.give(bank, e)
        c.st_t.append(e)
        yield
    mem.give(kd, last)
    mem.give(kc, kt)
    mem.give(vc, m)
    mem.give(c.dk, kt)


def turn_heads(c, x, xt, rope, rt, out):
    V, G = c.V, c.G
    toks = []
    for p in range(2):
        bank, bw = c.p.take()
        for h in range(2):
            m = c.mm(bank[:, h * 256:h * 256 + 256], rope[:, 512:640], x[:, 2 * p + h, :], True, True, xt[2 * p + h], rt, bw)
        o, i = out[:, 2 * p:2 * p + 2, :], x[:, 2 * p:2 * p + 2, :]
        sin = rope[:, 256:512].unsqueeze(1).to_broadcast([128, 2, 256])
        cos = rope[:, 0:256].unsqueeze(1).to_broadcast([128, 2, 256])
        e = c.tt(V, o, bank[:, :].rearrange("p (h t) -> p h t", h=2), sin, ALU.mult, m, rt, out.w)
        c.p.give(bank, e)
        f = c.tt(V, i, i, cos, ALU.mult, xt[2 * p:2 * p + 2], rt, m)
        toks.append(c.tt(V, o, o, i, ALU.add, e, f))
        yield
    c.turned_t = toks


def retention(c, q, qt, k, kt, v, vt, o):
    d, mem, V, A, G = c.d, c.mem, c.V, c.A, c.G
    rope = mem.take("rope", [640])
    g = c.group("rope")
    G.dma(g, rope[:, :], d["k_rope"], rope.w)
    qr = mem.take("qr", [4, 256])
    kr = mem.take("kr", [4, 256])
    yield
    yield from turn_heads(c, k, kt, rope, g.all, kr)
    krt = c.turned_t
    mem.give(k, krt)
    yield from turn_heads(c, q, qt, rope, g.all, qr)
    qrt = c.turned_t
    mem.give(q, qrt)
    mem.give(rope, qrt)
    while not vt or not c.st_t or len(c.st_t) < 4 or len(c.dm_t) < 4:
        yield
    sc = mem.take("rsc", [2, 512])
    c.oss = mem.take("oss", [8])
    junk = mem.take("ojunk", [2, 256])
    c.o_t, c.oss_t = [], []
    last = [[], []]
    js = [[], []]
    for h in range(4):
        b = h % 2
        bank, bw = c.p.take()
        for j in range(2):
            m = c.mm(bank[:, j * 256:j * 256 + 256], kr[:, h, j * 128:j * 128 + 128], qr[:, h, :], True, True, krt, qrt, bw)
        e = c.stt(V, sc[:, b, :], bank[:, :], 128.0 ** -0.5, c.dm[:, h, :], ALU.mult, ALU.mult, m, c.dm_t[h], sc.w, last[b])
        c.p.give(bank, e)
        yield
        bank, bw = c.p.take()
        for t in range(2):
            out = bank[:, t * 256:t * 256 + 256]
            for j in range(2):
                m = c.mm(out, sc[:, b, j * 256 + t * 128:j * 256 + t * 128 + 128], v[:, j, h * 256:h * 256 + 256], j == 0, j == 1, e, vt, bw)
        ci = c.cp(A, o[:, :, h * 256:h * 256 + 256], bank[:, :].rearrange("p (t v) -> p t v", t=2), m, o.w)
        c.p.give(bank, ci)
        last[b] = m
        yield
        es = []
        for t in range(2):
            bank, bw = c.p.take()
            m = c.mm(bank[:, :], qr[:, h, t * 128:t * 128 + 128], c.st[:, h, :, :], True, True, c.st_t[h], bw)
            x, y = o[:, t, h * 256:h * 256 + 256], ci
            for i in range(2):
                y = c.stt(V, x, bank[:, i * 256:i * 256 + 256], c.dq[:, i, h, t:t + 1], x, ALU.mult, ALU.add, m, y, c.dq_t)
            c.p.give(bank, y)
            es.append(y)
            a = c.act(junk[:, t, :], x, ACT.Square, y, junk.w, c.oss.w, js[t], accum=c.oss[:, t * 4 + h:t * 4 + h + 1])
            js[t] = [a]
            c.oss_t.append(a)
        c.o_t += es
        yield
    mem.give(junk, c.oss_t)
    mem.give(sc, m)
    mem.give(qr, m)
    mem.give(kr, m)
    mem.give(v, m)
    mem.give(c.st, m)
    mem.give(c.dq, es)
    mem.give(c.dm, e)


def first_mix(c):
    d, mem, V, A, G, S = c.d, c.mem, c.V, c.A, c.G, c.S
    w, b_in = d["w_in"][0], d["b_in"]
    m = c.mods["m1"]
    ctx = c.ctx_
    cn, cnt = c.normed(ctx, "cn", c.ctx_t)
    mem.give(ctx, cnt)
    ax, shx, st = scale_shift(c, m, 0, 0, 1, column(c, "n1", 8), "ax")
    h = c.operand("h", [8, 256], True)
    c.turned(c.xn, c.xnt, ax, shx, h, st)
    mem.give(c.xn, c.pe_last())
    ac, shc, sct = scale_shift(c, m, 1, 0, 1, column(c, "n1", 8), "ac")
    hc = c.operand("hc", [8, 256], True)
    c.turned(cn, cnt, ac, shc, hc, sct)
    mem.give(cn, c.pe_last())
    mem.give(ax, h.toks)
    mem.give(ac, hc.toks)
    jobs = []

    def step(n=1):
        for _ in range(n):
            for j in list(jobs):
                if next(j, "end") == "end":
                    jobs.remove(j)

    cols = [3072 + 256 * i for i in range(6)] + [512, 768, 1024, 1280, 1536, 1792] + [0, 256] + [2048 + 256 * i for i in range(4)] + [4608 + 256 * i for i in range(8)]
    items = [by_cols(w, c0) for c0 in cols]
    hw, rw, wo = d["hy_w_o"][0], d["ret_w_o"][0], d["w_out"][0]
    for n in range(2):
        items.append((hw[:, n * 512:n * 512 + 512].rearrange("(k p) c -> p k c", p=128), [lambda v: v[:, :, 0:256], lambda v: v[:, :, 256:512]]))
        items += [by_cols(rw, n * 512 + 256 * i) for i in range(2)]
    items += [by_cols(wo, n * 256) for n in range(4)]
    st = Stream(c, items, True, 3)

    def to_heads(dst, toks, base, b0):
        def evac(i, ps, t):
            e = c.act(dst[:, base + i, :], ps, ACT.Identity, t, dst.w, c.vec_t, bias=column(c, "b_in", 1, b0 + base + i))
            toks.append(e)
            return e
        return evac
    u = mem.take("u", [12, 258], top=True)
    uz = c.set(G, u[:, :, 0:258:257], 0.0, u.w)
    ut = [None] * 12

    def to_u(base):
        def evac(i, ps, t):
            k = base + i
            ut[k] = [c.act(u[:, k, 1:257], ps, ACT.Identity, t, u.w, uz, c.vec_t, bias=column(c, "b_in", 1, 24 + k))]
            return ut[k]
        return evac
    for n in range(6):
        c.unit(st, 2, [("cols", h, to_u(2 * n))])
        step()
        yield
    jobs.append(hyena(c, u, ut))
    kT = mem.take("kT", [4, 256])
    kc = mem.take("kc", [2, 512])
    bias = mem.take("bias", [1536])
    gb = c.group("bias")
    G.dma(gb, bias[:, :], b_in[0:1, 512:2048].to_broadcast([128, 1536]), bias.w)
    kt, qt, kct, vct, vt = [], [], [], [], []

    def to_tok(dst, toks, base, boff):
        def evac(t, ps, tok):
            e = c.tt(V, dst[:, t, base:base + 256], ps, bias[:, boff:boff + 256], ALU.add, tok, gb.all, dst.w)
            toks.append(e)
            return e
        return evac
    for n in range(2):
        c.unit(st, 2, [("cols", h, to_heads(kT, kt, 2 * n, 4)), ("toks", hc, to_tok(kc, kct, 256 * n, 256 * n))])
        step(6)
        yield
    vc = mem.take("vc", [2, 1024])
    v = mem.take("v", [2, 1024])
    tx = []
    for n in range(4):
        c.unit(st, 2, [("toks", hc, to_tok(vc, vct, n * 256, 512 + n * 256)), ("toks", h, to_tok(v, tx, n * 256, 512 + n * 256))])
        step(3)
        yield
    vt.extend(tx)
    c.drop(hc, c.last_mm)
    mem.give(bias, vt, vct, kct)
    jobs.append(states(c, kc, kct, vc, vct))
    qT = mem.take("qT", [4, 256])
    for n in range(2):
        c.unit(st, 2, [("cols", h, to_heads(qT, qt, 2 * n, 0))])
        step(1)
        yield
    o = mem.take("o", [2, 1024])
    jobs.append(retention(c, qT, qt, kT, kt, v, vt, o))
    sg = mem.take("sg", [2, 1024])
    bias2 = mem.take("bias2", [1024])
    gb2 = c.group("bias2")
    G.dma(gb2, bias2[:, :], b_in[0:1, 2048:3072].to_broadcast([128, 1024]), bias2.w)
    sgt, sga = [], []

    def to_sg(n):
        def evac(t, ps, tok):
            s = slice(n * 256, n * 256 + 256)
            e = c.tt(V, sg[:, t, s], ps, bias2[:, s], ALU.add, tok, gb2.all, sg.w)
            sga.append(e)
            sgt.append(c.act(sg[:, t, s], sg[:, t, s], ACT.Silu, e))
            return e
        return evac
    for n in range(4):
        c.unit(st, 2, [("toks", h, to_sg(n))])
        step(2)
        yield
    mem.give(bias2, sga)
    gr = [None, None]
    grt = [[None] * 8, [None] * 8]

    def to_gate(i, base):
        if base == 0:
            gr[i] = mem.take(f"gate{i}", [8, 256])

        def evac(k, ps, t):
            grt[i][base + k] = c.act(gr[i][:, base + k, :], ps, ACT.Sigmoid, t, gr[i].w, c.vec_t, bias=column(c, "b_in", 1, 36 + 8 * i + base + k))
            return grt[i][base + k]
        return evac
    for n in range(8):
        c.unit(st, 2, [("cols", h, to_gate(n // 4, 2 * (n % 4)))])
        step(2)
        yield
    c.drop(h, c.last_mm)
    while jobs:
        step()
        yield
    r = c.rstd(c.oss[:, :], c.oss[:, :], 256.0, c.oss_t)
    og = []
    for hh in range(4):
        for t in range(2):
            s = slice(hh * 256, hh * 256 + 256)
            og.append(c.stt(V, o[:, t, s], o[:, t, s], c.oss[:, t * 4 + hh:t * 4 + hh + 1], sg[:, t, s], ALU.mult, ALU.mult, r, sgt, c.o_t))
    mem.give(c.oss, og)
    mem.give(sg, og)
    c.fill(3)
    ogT = c.operand("ogT", [8, 256], True)
    tmp = [mem.take("ogt", [2, 256], top=True) for _ in range(2)]
    last = [[], []]
    for k2 in range(4):
        bank, bw = c.p.take()
        for k in range(2):
            for t in range(2):
                kk = (2 * k2 + k) * 128
                mt = c.tr(bank[:, k * 256 + t * 128:k * 256 + t * 128 + 128], o[:, t, kk:kk + 128], og[2 * k2 + t], bw)
        b = k2 % 2
        e = c.cp(A if b else V, tmp[b][:, :, :], bank[:, :].rearrange("p (k t) -> p k t", k=2), mt, tmp[b].w, last[b])
        c.p.give(bank, e)
        last[b] = [c.part(ogT, slice(2 * k2, 2 * k2 + 2), tmp[b][:, :, :], e)]
    for b in range(2):
        mem.give(tmp[b], last[b])
    mem.give(o, mt)
    mixed = c.operand("mixed", [8, 256], True)
    mx = [None] * 8
    mh = [None] * 8

    def to_hy(base):
        def evac(k, ps, t):
            kk = base + k
            o_ = gr[1][:, kk, :]
            mh[kk] = c.tt(V, o_, ps, o_, ALU.mult, t, grt[1][kk])
            return mh[kk]
        return evac

    def to_mix(base):
        def evac(k, ps, t):
            kk = base + k
            o_ = gr[0][:, kk, :]
            e = c.tt(V, o_, ps, o_, ALU.mult, t, grt[0][kk])
            mx[kk] = c.tt(V, o_, o_, gr[1][:, kk, :], ALU.add, e, mh[kk])
            mx[kk] = c.part(mixed, kk, o_, mx[kk])
            return e
        return evac
    for n in range(2):
        for i in range(2):
            c.unit(st, 1, [("cols", c.hy, to_hy(4 * n + 2 * i))])
        for i in range(2):
            c.unit(st, 2, [("cols", ogT, to_mix(4 * n + 2 * i))])
        yield
    c.drop(c.hy, c.last_mm)
    c.drop(ogT, c.last_mm)
    mem.give(gr[0], mx)
    mem.give(gr[1], mx)
    gt = mem.take("gt1", [1024])
    gtt = c.gate(m, 0, 2, gt)
    c.x.new = []
    tmp = mem.take("xtmp", [4, 256])
    last = [[] for _ in range(4)]
    for n in range(4):
        c.unit(st, 2, [("toks", mixed, add_gated(c, c.x, c.x_t, gt, gtt, tmp, last, n))])
        yield
    c.drop(mixed, c.last_mm)
    mem.give(gt, c.x.new)
    mem.give(tmp, c.x.new)
    c.x_t = c.x.new


def first_hot(c, eq, n, base, out, t):
    mem, V = c.mem, c.V
    cand = mem.take("cand", [2, n])
    mn = mem.take("cmin", [2])
    t = c.stt(V, cand[:, :, :], eq, -64.0, base.unsqueeze(1).to_broadcast([128, 2, n]), ALU.mult, ALU.add, t, cand.w, c.eye_t)
    t = c.red(mn[:, :], cand[:, :, :], ALU.min, t, mn.w)
    t = c.tt(V, out, cand[:, :, :], mn[:, :].unsqueeze(2).to_broadcast([128, 2, n]), ALU.is_equal, t)
    mem.give(cand, t)
    mem.give(mn, t)
    return t


def route(c, h2, h2t):
    d, mem, V, A, G = c.d, c.mem, c.V, c.A, c.G
    rw, rb, rt = c.rw, c.rb, c.rw_t
    L = mem.take("logits", [2, 36])
    bank, bw = c.p.take()
    for t in range(2):
        for k in range(8):
            m = c.mm(bank[:, t * 64:t * 64 + 36], h2[:, k, t * 128:t * 128 + 128], rw[:, k, :], k == 0, k == 7, h2t, rt, bw)
    lt = [c.tt(V, L[:, t, :], bank[:, t * 64:t * 64 + 36], rb[:, :], ALU.add, m, L.w, rt) for t in range(2)]
    c.p.give(bank, lt)
    mem.give(rw, m)
    mem.give(rb, lt)
    gl, el = L[:, :, 0:4], L[:, :, 4:36].rearrange("p t (g e) -> p t e g", g=4)
    w = mem.take("rtw", [2, 96])
    iota = c.small[:, 0:32]
    gx, eq, oh = w[:, :, 0:4], w[:, :, 4:8], w[:, :, 8:12]
    one = lambda i: w[:, :, 12 + i]
    bc = lambda a, n: a.unsqueeze(2).to_broadcast([128, 2, n])
    gm, ps, m1, m2, e2, w1, w2, sm = (one(i) for i in range(8))
    t = c.red(gm, gl, ALU.max, lt, w.w)
    t1 = c.tt(V, gx, gl, bc(gm, 4), ALU.subtract, t)
    t2 = c.tt(V, eq, gl, bc(gm, 4), ALU.is_equal, t)
    ex = c.act(gx, gx, ACT.Exp, t1)
    to = first_hot(c, eq, 4, iota[:, 0:4], oh, t2)
    t = c.red(ps, gx, ALU.add, ex)
    tp = c.recip(ps, ps, t)
    pr = mem.take("prod", [2, 8, 4])
    t = c.tt(V, pr[:, :, :, :], el, oh.unsqueeze(2).to_broadcast([128, 2, 8, 4]), ALU.mult, to, pr.w, lt)
    ing, eq1, oh1, oh2 = (w[:, :, 24 + 8 * i:32 + 8 * i] for i in range(4))
    t = c.red(ing, pr[:, :, :, :], ALU.add, t)
    mem.give(pr, t)
    mem.give(L, t)
    t = c.red(m1, ing, ALU.max, t)
    t = c.tt(V, eq1, ing, bc(m1, 8), ALU.is_equal, t)
    to1 = first_hot(c, eq1, 8, iota[:, 0:8], oh1, t)
    t = c.stt(V, ing, oh1, NEG, ing, ALU.mult, ALU.add, to1)
    t = c.red(m2, ing, ALU.max, t)
    t2 = c.tt(V, e2, m2, m1, ALU.subtract, t)
    x2 = c.act(e2, e2, ACT.Exp, t2)
    t = c.tt(V, eq1, ing, bc(m2, 8), ALU.is_equal, t)
    to2 = first_hot(c, eq1, 8, iota[:, 0:8], oh2, t)
    t = c.ts(V, sm, e2, 1.0, None, ALU.add, None, x2)
    t = c.recip(sm, sm, t)
    tw1 = c.tt(V, w1, ps, sm, ALU.mult, t, tp)
    tw2 = c.tt(V, w2, w1, e2, ALU.mult, tw1)
    ab = mem.take("assign", [3, 2, 32])
    a1, a2, al = (ab[:, i, :, :] for i in range(3))
    c.wt = mem.take("wt", [2, 32])
    c.rk = mem.take("rk", [2, 32])
    as3 = lambda a, t: a[:, t, :].rearrange("p (g e) -> p g e", g=4)
    ta, tw = [], []
    for i in range(2):
        o4 = oh[:, i, :].unsqueeze(2).to_broadcast([128, 4, 8])
        s1 = c.tt(V, as3(a1, i), o4, oh1[:, i, :].unsqueeze(1).to_broadcast([128, 4, 8]), ALU.mult, to, to1, ab.w)
        s2 = c.tt(V, as3(a2, i), o4, oh2[:, i, :].unsqueeze(1).to_broadcast([128, 4, 8]), ALU.mult, to2, ab.w)
        ta.append(c.tt(V, al[:, i, :], a1[:, i, :], a2[:, i, :], ALU.add, s1, s2))
        s = c.ts(V, c.wt[:, i, :], a1[:, i, :], w1[:, i:i + 1], None, ALU.mult, None, s1, tw2, c.wt.w)
        tw.append(c.stt(V, c.wt[:, i, :], a2[:, i, :], w2[:, i:i + 1], c.wt[:, i, :], ALU.mult, ALU.add, s))
    bank, bw = c.p.take()
    c.mm(bank[:, 0:32], c.eye[:, 1, :], al[:, 0, :], True, True, ta, bw)
    c.mm(bank[:, 32:64], c.eye[:, 2, :], al[:, 0, :], True, False)
    c.mm(bank[:, 32:64], c.eye[:, 1, :], al[:, 1, :], False, True)
    c.mm(bank[:, 64:96], c.eye[:, 2, :], al[:, 0, :], True, False)
    m = c.mm(bank[:, 64:96], c.eye[:, 2, :], al[:, 1, :], False, True)
    t = c.stt(V, c.rk[:, :, :], bank[:, 0:64].rearrange("p (t e) -> p t e", t=2), 1.0, al, ALU.add, ALU.mult, m, c.rk.w)
    c.rk_t = c.ts(V, c.rk[:, :, :], c.rk[:, :, :], -1.0, None, ALU.add, None, t)
    c.cnt = mem.take("cnt", [33])
    tc = c.cp(V, c.cnt[:, 0:32], bank[:, 64:96], m, c.cnt.w)
    t_ = c.red(c.cnt[:, 32:33], c.cnt[:, 0:32], ALU.max, tc)
    c.cnti = mem.take("cnti", [1], I32)
    c.cnt_t = c.cp(V, c.cnti[:, :], c.cnt[:, 32:33], t_, c.cnti.w)
    c.p.give(bank, t, tc)
    mem.give(ab, c.rk_t, tw)
    mem.give(w, tw)
    c.wt_t = tw


def experts(c, xn, xnt, ax, shx, axt, gt, gtt):
    d, mem, V, A, G = c.d, c.mem, c.V, c.A, c.G
    w1, w3, w2 = (d[n][0] for n in ("expert_w1", "expert_w3", "expert_w2"))
    iota = c.small[:, 0:32].unsqueeze(1).to_broadcast([128, 4, 32])
    P = mem.take("P", [2, 2, 128])
    xg = [mem.take("xg", [8, 128]) for _ in range(2)]
    pw = [mem.take("pw", [256]) for _ in range(2)]
    last_x, last_pw, last_P = [[], []], [[], []], []

    def prepare(g):
        nonlocal last_P
        b = g % 2
        pt, ws = [], []
        for t in range(2):
            sel, wgt = (P[:, i, t, :].rearrange("p (e s) -> p e s", e=4) for i in range(2))
            e = c.tt(V, sel, c.rk[:, t, 4 * g:4 * g + 4].unsqueeze(2).to_broadcast([128, 4, 32]), iota, ALU.is_equal, c.rk_t, P.w, last_P)
            pt.append(e)
            ws.append(c.tt(V, wgt, sel, c.wt[:, t, 4 * g:4 * g + 4].unsqueeze(2).to_broadcast([128, 4, 32]), ALU.mult, e, c.wt_t))
        es = []
        for k4 in range(2):
            bank, bw = c.p.take()
            for k in range(4):
                o = bank[:, k * 128:k * 128 + 128]
                kk = k4 * 4 + k
                for t in range(2):
                    m = c.mm(o, xn[:, t, kk * 128:kk * 128 + 128], P[:, 0, t, :], t == 0, t == 1, xnt, pt, bw)
            ev = []
            for k in range(4):
                o, kk = bank[:, k * 128:k * 128 + 128], k4 * 4 + k
                if k4:
                    ev.append(c.act(xg[b][:, kk, :], o, ACT.Identity, m, axt, xg[b].w, last_x[b], scale=ax[:, kk:kk + 1], bias=shx[:, kk:kk + 1]))
                else:
                    ev.append(c.ts(V, xg[b][:, kk, :], o, ax[:, kk:kk + 1], shx[:, kk:kk + 1], ALU.mult, ALU.add, m, axt, xg[b].w, last_x[b]))
            c.p.give(bank, ev)
            es += ev
        bank, bw = c.p.take()
        for t in range(2):
            m = c.tr(bank[:, t * 128:t * 128 + 128], P[:, 1, t, :], ws[t], bw)
        e = c.cp(A, pw[b][:, :], bank[:, 0:256], m, pw[b].w, last_pw[b])
        c.p.give(bank, e)
        last_P = [m]
        return es, e
    ready = prepare(0)
    yield
    xt = {(t, h): c.x_t for t in range(2) for h in range(2)}
    sl = mem.take("mh", [2, 512])
    hT = mem.take("mhT", [4, 128])
    y = mem.take("my", [2, 512])
    hl, hTl, yl = [], [], [[], []]
    for g in range(8):
        (xe, pwt), xb = ready, xg[g % 2]
        b1, w1w = c.p.take()
        b3, w3w = c.p.take()
        for k in range(8):
            for w, bank, bw in ((w1, b1, w1w), (w3, b3, w3w)):
                s, v, lt = c.load(w[4 * g:4 * g + 4, k * 128:k * 128 + 128, :].rearrange("e p f -> p e f"))
                for j in range(4):
                    m = c.mm(bank[32 * j:32 * j + 32, :], xb[:, k, 32 * j:32 * j + 32], v[:, j, :], k == 0, k == 7, lt, xe, bw)
                c.done(s, m)
            yield
        last_x[g % 2] = [m]
        e1 = c.act(sl[:, 0, :], b1[:, :], ACT.Silu, m, sl.w, hl)
        e3 = c.tt(V, sl[:, 1, :], sl[:, 0, :], b3[:, :], ALU.mult, e1, m)
        c.p.give(b1, e1)
        c.p.give(b3, e3)
        if g < 7:
            ready = prepare(g + 1)
        yield
        bank, bw = c.p.take()
        for k in range(4):
            m = c.tr(bank[:, k * 128:k * 128 + 128], sl[:, 1, k * 128:k * 128 + 128], e3, bw)
        hl = [m]
        e = c.cp(A, hT[:, :, :], bank[:, :].rearrange("p (k s) -> p k s", k=4), m, hT.w, hTl)
        c.p.give(bank, e)
        yield
        for h in range(2):
            bank, bw = c.p.take()
            for k in range(4):
                s, v, lt = c.load(w2[4 * g:4 * g + 4, k * 128:k * 128 + 128, h * 512:h * 512 + 512].rearrange("e p f -> p e f"))
                for j in range(4):
                    m = c.mm(bank[32 * j:32 * j + 32, :], hT[:, k, 32 * j:32 * j + 32], v[:, j, :], k == 0, k == 3, lt, e, bw)
                c.done(s, m)
                if k % 2:
                    yield
            hTl = [m]
            ey = c.tt(V, y[:, h, :], bank[:, :], gt[:, h * 512:h * 512 + 512], ALU.mult, m, gtt, y.w, yl[h])
            c.p.give(bank, ey)
            for t in range(2):
                bank, bw = c.p.take()
                m = c.mm(bank[:, :], pw[g % 2][:, t * 128:t * 128 + 128], y[:, h, :], True, True, ey, pwt, bw)
                o = c.x[:, t, h * 512:h * 512 + 512]
                xt[t, h] = c.tt(V, o, o, bank[:, :], ALU.add, m, xt[t, h])
                c.p.give(bank, xt[t, h])
            yl[h] = [m]
            yield
        last_pw[g % 2] = [m]
    c.x_t = list(xt.values())
    mem.give(P, last_P)
    for i in range(2):
        mem.give(xg[i], last_x[i])
        mem.give(pw[i], m)
    mem.give(sl, hl)
    mem.give(hT, hTl)
    mem.give(y, yl)


def crowded(c):
    c.most = {}
    for q in (c.T, c.V, c.A, c.S):
        def fn(e, w, q=q):
            for t in w:
                e.wait_ge(*t.resolve())
            c.most[id(q)] = e.value_load(c.cnti[0:1, 0:1], min_val=0, max_val=256)
        q.raw(fn, c.cnt_t)


def beyond(c, xn, ax, shx, gt):
    d, mem, nc = c.d, c.mem, c.nc
    w1, w3, w2 = (d[n][0] for n in ("expert_w1", "expert_w3", "expert_w2"))
    N = 224
    P, XT, wa, wb, hh, pwT, y, tmp = (mem.take("o" + n, s) for n, s in (
        ("P", [2, 2, N]), ("XT", [8, N]), ("wa", [8, 512]), ("wb", [8, 512]), ("hh", [2, 4, N]),
        ("pwT", [2, 256]), ("y", [2, 1024]), ("tmp", [2, 2, 32])))
    bufs = (P, XT, wa, wb, hh, pwT, y, tmp)
    wc = wa[:, :, :].rearrange("p (k h) n -> p k (h n)", h=2)
    before = flat([b.w for b in bufs]) + [Tok(q, len(q.ops) - 1) for q in (c.T, c.V, c.A)]
    sv, sp, sa, sd = (c.sem("over_" + n) for n in "vpad")
    bk = c.banks
    slots = ((0, 128), (128, 96))
    iota = c.small[:, 64:288]

    def enter(e, w):
        for t in w:
            e.wait_ge(*t.resolve())

    def leave(e):
        e.wait_ge(sv, 32 * 7 + 1)

    def vec(e, w):
        with e.If(c.most[id(c.V)] > 32):
            enter(e, w)
            e.sem_inc(sv, 1)
            with e.Fori(0, 32) as i:
                e.wait_ge(sv, i * 7 + 1)
                for t in range(2):
                    e.tensor_scalar(P[:, 0, t, :], iota, c.rk[:, t, 0:1], None, ALU.is_equal)
                    m = e.tensor_scalar(P[:, 1, t, :], iota, c.rk[:, t, 0:1], c.wt[:, t, 0:1], ALU.is_equal, ALU.mult)
                m.then_inc(sv, 1)
                e.wait_ge(sp, i * 4 + 2)
                for k in range(8):
                    e.tensor_scalar(XT[:, k, :], bk[k // 2][:, (k % 2) * N:(k % 2) * N + N], ax[:, k:k + 1], shx[:, k:k + 1], ALU.mult, ALU.add)
                e.tensor_copy(pwT[:, 0, :], bk[4][:, 0:256])
                e.tensor_copy(pwT[0:96, 1, :], bk[4][0:96, 256:512]).then_inc(sv, 1)
                e.wait_ge(sa, i + 1)
                for h in range(2):
                    m = e.tensor_tensor(hh[:, 1, 2 * h:2 * h + 2, :], hh[:, 0, 2 * h:2 * h + 2, :],
                                        bk[(7 + h) % 8][:, 0:2 * N].rearrange("p (f s) -> p f s", f=2), ALU.mult)
                m.then_inc(sv, 1)
                e.wait_ge(sp, i * 4 + 4)
                for s, (_, n) in enumerate(slots):
                    for h in range(2):
                        m = e.tensor_tensor(y[0:n, s, h * 512:h * 512 + 512], bk[1 + 2 * s + h][0:n, :], gt[0:n, h * 512:h * 512 + 512], ALU.mult)
                m.then_inc(sv, 1)
                e.wait_ge(sp, i * 4 + 5)
                for t in range(2):
                    for h in range(2):
                        o = c.x[:, t, h * 512:h * 512 + 512]
                        m = e.tensor_tensor(o, o, bk[(5 + 2 * t + h) % 8][:, :], ALU.add)
                m.then_inc(sv, 1)
                e.tensor_copy(tmp[:, 0, :, 0:31], c.rk[:, :, 1:32])
                e.tensor_copy(tmp[:, 1, :, 0:31], c.wt[:, :, 1:32]).then_inc(sv, 1)
                e.wait_ge(sv, i * 7 + 7)
                e.tensor_copy(c.rk[:, :, 0:31], tmp[:, 0, :, 0:31])
                e.tensor_copy(c.wt[:, :, 0:31], tmp[:, 1, :, 0:31]).then_inc(sv, 1)
            leave(e)

    def pe(e, w):
        with e.If(c.most[id(c.T)] > 32):
            enter(e, w)
            e.sem_inc(sp, 1)
            with e.Fori(0, 32) as i:
                e.wait_ge(sv, i * 7 + 2)
                for k in range(8):
                    for t in range(2):
                        e.matmul(bk[k // 2][:, (k % 2) * N:(k % 2) * N + N], xn[:, t, k * 128:k * 128 + 128], P[:, 0, t, :], start=t == 0, stop=t == 1)
                for s, (s0, n) in enumerate(slots):
                    for t in range(2):
                        m = e.transpose(bk[4][0:n, s * 256 + t * 128:s * 256 + t * 128 + 128], P[:, 1, t, s0:s0 + n], c.eye[:, 0, :])
                m.then_inc(sp, 1)
                e.wait_ge(sv, i * 7 + 3)
                e.wait_ge(sd, i * 48 + 32)
                for b, wt in ((5, wa), (7, wb)):
                    for f in range(4):
                        for k in range(8):
                            m = e.matmul(bk[(b + f // 2) % 8][:, (f % 2) * N:(f % 2) * N + N], wt[:, k, f * 128:f * 128 + 128], XT[:, k, :], start=k == 0, stop=k == 7)
                m.then_inc(sp, 1)
                e.wait_ge(sv, i * 7 + 4)
                e.wait_ge(sd, i * 48 + 48)
                for s, (s0, n) in enumerate(slots):
                    for h in range(2):
                        for f in range(4):
                            m = e.matmul(bk[1 + 2 * s + h][0:n, :], hh[:, 1, f, s0:s0 + n], wc[:, f, h * 512:h * 512 + 512], start=f == 0, stop=f == 3)
                m.then_inc(sp, 1)
                e.wait_ge(sv, i * 7 + 5)
                for t in range(2):
                    for h in range(2):
                        for s, (_, n) in enumerate(slots):
                            m = e.matmul(bk[(5 + 2 * t + h) % 8][:, :], pwT[0:n, s, t * 128:t * 128 + 128], y[0:n, s, h * 512:h * 512 + 512], start=s == 0, stop=s == 1)
                m.then_inc(sp, 1)
            leave(e)

    def act(e, w):
        with e.If(c.most[id(c.A)] > 32):
            enter(e, w)
            with e.Fori(0, 32) as i:
                e.wait_ge(sp, i * 4 + 3)
                for h in range(2):
                    m = e.activation(hh[:, 0, 2 * h:2 * h + 2, :], bk[5 + h][:, 0:2 * N].rearrange("p (f s) -> p f s", f=2), ACT.Silu)
                m.then_inc(sa, 1)
            leave(e)

    def sp_(e, w):
        with e.If(c.most[id(c.S)] > 32):
            enter(e, w)
            with e.Fori(0, 32) as i:
                e.wait_ge(sp, i * 4 + 1)
                for dst, src in ((wa[:, :, :], w1), (wb[:, :, :], w3), (wc, w2)):
                    if src is w2:
                        e.wait_ge(sp, i * 4 + 3)
                    e.dma_start(dst, src[bass.ds(i, 1), :, :].rearrange("o (k p) n -> p (o k) n", p=128)).then_inc(sd, 16)
            leave(e)
    for q, fn in ((c.T, pe), (c.V, vec), (c.A, act), (c.S, sp_)):
        q.raw(fn, before)
    done = c.V(lambda e: e.drain())
    for b in bufs:
        mem.give(b, done)
    return done


def second_consts(c):
    d, mem, V, A, G = c.d, c.mem, c.V, c.A, c.G
    g = c.group("second")
    c.fft = mem.take("fft", [1280])
    c.rope2 = mem.take("rope2", [640])
    c.hd = mem.take("hd", [128])
    for b, n in ((c.fft, "k_fft"), (c.rope2, "k_rope2"), (c.hd, "k_hd")):
        G.dma(g, b[:, :], d[n], b.w)
    dl = mem.take("dl", [2, 4, 32])
    for i, n in enumerate(("diff_lq1_2", "diff_lk1_2", "diff_lq2_2", "diff_lk2_2")):
        G.dma(g, dl[:, :, i, :], d[n].rearrange("(o l) n -> o l n", o=1).to_broadcast([128, 2, 32]), dl.w)
    c.lam = mem.take("lam", [2, 2])
    c.subg = mem.take("subg", [2])
    for l in range(2):
        for i in range(2):
            G.dma(g, c.subg[64 * i:64 * i + 64, l:l + 1], d["diff_subln_g_2"][l:l + 1, :].rearrange("o n -> n o"), c.subg.w)
    c.second_t = g.all
    yield
    t = [c.tt(V, dl[:, :, 2 * i, :], dl[:, :, 2 * i, :], dl[:, :, 2 * i + 1, :], ALU.mult, g.all) for i in range(2)]
    t = [c.red(c.lam[:, i, :], dl[:, :, 2 * i, :], ALU.add, t[i], c.lam.w) for i in range(2)]
    mem.give(dl, t)
    t = c.act(c.lam[:, :, :], c.lam[:, :, :], ACT.Exp, t)
    init = [0.8 - 0.6 * math.exp(-0.3 * l) for l in range(2)]
    t = c.tt(V, c.lam[:, 0, :], c.lam[:, 1, :], c.lam[:, 0, :], ALU.subtract, t)
    c.lam_t, c.subg_t = [], []
    for l in range(2):
        c.lam_t.append(c.ts(V, c.lam[:, 0, l:l + 1], c.lam[:, 0, l:l + 1], -init[l], None, ALU.add, None, t))
        c.subg_t.append(c.ts(V, c.subg[:, l:l + 1], c.subg[:, l:l + 1], 1.0 - init[l], None, ALU.mult, None, g.all))
    yield


def attend(c, q, qt, nb, keys, vals, bias, lam, evac):
    mem, V, A = c.mem, c.V, c.A
    nk = 256 * len(keys)
    P = [[mem.take("ap", [nk], top=True) for _ in range(nb)] for _ in range(2)]
    pt = [mem.take("apt", [nk // 128, 256], top=True) for _ in range(2)]
    st = [mem.take("ast", [2 * nb], top=True) for _ in range(2)]
    last_p, last_t, last_s = [[[] for _ in range(nb)] for _ in range(2)], [[], []], [[], []]
    pe, es = [None, None], [[], []]
    ob = [None, None]

    def scores(i):
        h, t, r = i // 2, i % 2, i % 2
        pair, hh = h // 2, h % 2
        s, pe[r] = st[r], []
        for b in range(nb):
            bank, bw = c.p.take()
            for k, (kb, kt) in enumerate(keys):
                with_bias = bias is not None and k == 0
                o = bank[:, k * 256:k * 256 + 256]
                m = c.mm(o, q[:, pair, hh * nb + b, t * 128:t * 128 + 128], kb[:, pair, :], True, not with_bias, qt, kt, bw)
                if with_bias:
                    m = c.mm(o, c.eye[:, 3, :], bias[0][:, h, t, :], False, True, bias[1])
            x = c.red(s[:, b:b + 1], bank[:, 0:nk], ALU.max, m, s.w, last_s[r], negate=True)
            e = c.act(P[r][b][:, :], bank[:, 0:nk], ACT.Exp, x, P[r][b].w, last_p[r][b], bias=s[:, b:b + 1], accum=s[:, nb + b:nb + b + 1])
            c.p.give(bank, e)
            pe[r].append(e)

    def weights(i):
        h, t, r = i // 2, i % 2, i % 2
        s, p = st[r], P[r]
        w = c.recip(s[:, nb:2 * nb], s[:, nb:2 * nb], pe[r])
        e = c.ts(V, p[0][:, :], p[0][:, :], s[:, nb:nb + 1], None, ALU.mult, None, w)
        if nb == 2:
            w = c.tt(V, s[:, nb + 1:nb + 2], s[:, nb + 1:nb + 2], lam[0], ALU.mult, w, lam[1])
            e = c.stt(V, p[0][:, :], p[1][:, :], s[:, nb + 1:nb + 2], p[0][:, :], ALU.mult, ALU.add, e, w)
            last_p[r][1] = [e]
        last_s[r] = [e]
        bank, bw = c.p.take()
        for k in range(nk // 128):
            m = c.tr(bank[:, k * 128:k * 128 + 128], p[0][:, k * 128:k * 128 + 128], e, bw)
        last_p[r][0] = [m]
        b = h % 2
        e = c.cp(V if i % 2 else A, pt[b][:, :, t * 128:t * 128 + 128], bank[:, 0:nk].rearrange("p (k q) -> p k q", q=128), m, pt[b].w, last_t[b])
        c.p.give(bank, e)
        es[b] = es[b] + [e] if t else [e]

    def values(h):
        pair, hh = h // 2, h % 2
        if not hh:
            ob[:] = c.p.take()
        for k in range(nk // 128):
            vb, vt = vals[k // 2]
            m = c.mm(ob[0][64 * hh:64 * hh + 64, 0:256], vb[:, k % 2, h * 64:h * 64 + 64], pt[hh][:, k, :], k == 0, k == nk // 128 - 1, es[hh], vt, ob[1])
        last_t[hh] = [m]
        if hh:
            c.p.give(ob[0], evac(pair, ob[0][:, 0:256], m))
    scores(0)
    yield
    for i in range(8):
        if i < 7:
            scores(i + 1)
        if i > 1 and i % 2 == 0:
            values(i // 2 - 1)
        yield
        weights(i)
        yield
    values(3)
    for r in range(2):
        for b in range(nb):
            mem.give(P[r][b], last_p[r][b])
        mem.give(pt[r], last_t[r])
        mem.give(st[r], last_s[r])


IN_COLS = (512, 768, 256, 1536, 1792, 2048, 0, 1024, 1280)


def layer_items(c, l):
    d = c.d
    items = [by_cols(d["w_in_2"][l], c0) for c0 in IN_COLS]
    items += [by_cols(d["w_out_2"][l], c0) for c0 in range(0, 1024, 256)]
    up = [by_cols(d["w_ff1_2"][l], c0) for c0 in range(0, 4096, 256)]
    w2 = d["w_ff2_2"][l]
    down = [(w2[r0:r0 + 256, :].rearrange("(k p) n -> p k n", p=128), [lambda v: v[:, 0:1, :], lambda v: v[:, 1:2, :]]) for r0 in range(0, 4096, 256)]
    items += up[0:2]
    for b in range(8):
        if b < 7:
            items += up[2 * b + 2:2 * b + 4]
        items += down[2 * b:2 * b + 2]
    return items


def mixers(c, l, h, own, kv, st, name, split):
    d, mem, V, A, G = c.d, c.mem, c.V, c.A, c.G
    out_op, parts, jobs = [None if split else c.operand(name + "y", [8, 256], False)], [], []

    def step(n=1):
        for _ in range(n):
            for j in list(jobs):
                if next(j, "end") == "end":
                    jobs.remove(j)

    def place(k, n):
        if split:
            b = mem.take(name + "y", [n, 256], top=True)
            return b, b[:, :, :], b.w
        return None, out_op[0].raw[:, k:k + n, :], out_op[0].raw.w

    def made(k, n, b, o, *toks):
        if split:
            parts.append((slice(k, k + n), b, o, toks))
            settle()
        else:
            out_op[0].toks += flat(toks)

    def settle():
        if out_op[0] is not None:
            while parts:
                s, b, o, t = parts.pop(0)
                mem.give(b, c.part(out_op[0], s, o, t))

    def new(n, shape, top=False):
        b = mem.take(name + n, shape, top=top)
        b.toks = []
        return b

    def keep(b, c0=None):
        def evac(i, ps, t):
            o = b[:, i, :] if c0 is None else b[:, i, c0:c0 + 256]
            e = c.cp(V if i % 2 else A, o, ps, t, b.w)
            b.toks.append(e)
            return e
        return evac
    if not own:
        rp = d["na_rpb_2"]
        bias = new("bias", [4, 2, 256])
        mask = new("mask", [256])
        gb = c.group(name + "bias")
        for hh in range(4):
            for t in range(2):
                for r in range(2):
                    off = ((l * 4 + hh) * 15 + 6 - 2 * t + r) * 31 - 48
                    G.dma(gb, bias[64 * r:64 * r + 64, hh, t, :].rearrange("p (i k) -> p i k", i=4),
                          bass.AP(tensor=rp.tensor, offset=off, ap=[[1, 64], [31, 4], [1, 64]]), bias.w)
        G.dma(gb, mask[:, :], d["k_mask"][:, 0:256], mask.w)
        bt = c.tt(G, bias[:, :, :, :].rearrange("p h t k -> p (h t) k"), bias[:, :, :, :].rearrange("p h t k -> p (h t) k"),
                  mask[:, :].unsqueeze(1).to_broadcast([128, 8, 256]), ALU.add, gb.all)
        mem.give(mask, bt)
    ln = new("ln", [2, 256])
    ws = new("ws", [4, 128])
    gl = c.group(name + "ln")
    G.dma(gl, ln[:, 0, :], d["sgu_ln_g_2"][l:l + 1, :].to_broadcast([128, 256]), ln.w)
    G.dma(gl, ln[:, 1, :], d["sgu_ln_b_2"][l:l + 1, :].to_broadcast([128, 256]), ln.w)
    G.dma(gl, ws[:, :, :], d["sgu_w_2"][l].rearrange("g p q -> p g q"), ws.w)

    nk, nv = new("nk", [2, 256]), new("nv", [2, 256])
    qm = new("nq", [2, 2, 256])
    c.unit(st, 2, [("cols", h, keep(nk))])
    yield
    c.unit(st, 2, [("toks", h, keep(nv))])
    yield

    def to_qm(i, ps, t):
        e = [c.ts(V, qm[:, i, u, :], ps, c.small[:, 48 + u:49 + u], None, ALU.mult, None, t, qm.w) for u in range(2)]
        qm.toks.extend(e)
        return e
    c.unit(st, 2, [("cols", h, to_qm)])
    yield

    def window():
        def out(pair, ps, t):
            b, o, w = place(2 + pair, 1)
            e = c.cp(A, o[:, 0, :], ps, t, w)
            made(2 + pair, 1, b, o, e)
            return e
        if own:
            keys, vals = [(nk, nk.toks)], [(nv, nv.toks)]
        else:
            keys, vals = [(nk, nk.toks), (kv["nk"], kv["nk"].toks)], [(nv, nv.toks), (kv["nv"], kv["nv"].toks)]
        yield from attend(c, qm, qm.toks, 1, keys, vals, None if own else (bias, bt), None, out)
        e = c.pe_last()
        mem.give(qm, e)
        if not own:
            for b_ in (bias, nk, nv, kv["nk"], kv["nv"]):
                mem.give(b_, e)
    jobs.append(window())
    dq, dk, dv = (new(n, [2, 256]) if n != "dq" or not own else None for n in ("dq", "dk", "dv"))
    dm = new("dm", [2, 4, 256])

    def to_dm(i, ps, t):
        e = [c.ts(V, dm[:, i, u, :], ps, c.small[:, 40 + u:41 + u], None, ALU.mult, None, t, dm.w) for u in range(4)]
        dm.toks.extend(e)
        return e
    for kind, evac in (("cols", to_dm if own else keep(dq)), ("cols", keep(dk)), ("toks", keep(dv))):
        c.unit(st, 2, [(kind, h, evac)])
        step()
        yield

    def spin(x, out):
        bank, bw = c.p.take()
        for i in range(2):
            m = c.mm(bank[:, i * 256:i * 256 + 256], c.rope2[:, 512:640], x[:, i, :], True, True, x.toks, c.second_t, bw)
        cos = c.rope2[:, 0:256].unsqueeze(1).to_broadcast([128, 2, 256])
        sin = c.rope2[:, 256:512].unsqueeze(1).to_broadcast([128, 2, 256])
        e = c.tt(V, out[:, :, :], bank[:, :].rearrange("p (i t) -> p i t", i=2), sin, ALU.mult, m, out.w)
        c.p.give(bank, e)
        f = c.tt(V, x[:, :, :], x[:, :, :], cos, ALU.mult, m)
        out.toks.append(c.tt(V, out[:, :, :], out[:, :, :], x[:, :, :], ALU.add, e, f))
        mem.give(x, out.toks)

    def differential():
        k_ = dk
        if not own:
            qr, k_ = new("dqr", [2, 256]), new("dkr", [2, 256])
            spin(dq, qr)
            yield
            spin(dk, k_)
            for pair in range(2):
                for u in range(4):
                    dm.toks.append(c.ts(V, dm[:, pair, u, :], qr[:, pair, :], c.small[:, 40 + u:41 + u], None, ALU.mult, None, qr.toks, dm.w))
            mem.give(qr, dm.toks)
            yield
        od = new("od", [2, 256], True)
        sq = new("osq", [2, 256], True)

        def out(pair, ps, t):
            e = c.cp(A, od[:, pair, :], ps, t, od.w)
            sq.toks.append(c.act(sq[:, pair, :], od[:, pair, :], ACT.Square, e, sq.w))
            od.toks.append(e)
            return e
        if own:
            keys, vals = [(dk, dk.toks)], [(dv, dv.toks)]
        else:
            keys, vals = [(k_, k_.toks), (kv["dk"], kv["dk"].toks)], [(dv, dv.toks), (kv["dv"], kv["dv"].toks)]
        yield from attend(c, dm, dm.toks, 2, keys, vals, None, (c.lam[:, 0, l:l + 1], c.lam_t[l]), out)
        e = c.pe_last()
        mem.give(dm, e)
        if not own:
            for b_ in (k_, dv, kv["dk"], kv["dv"]):
                mem.give(b_, e)
        yield
        bank, bw = c.p.take()
        for i in range(2):
            m = c.mm(bank[:, i * 256:i * 256 + 256], c.hd[:, :], sq[:, i, :], True, True, sq.toks, bw, c.second_t)
        t = c.act(sq[:, :, :], bank[:, :].rearrange("p (i t) -> p i t", i=2), ACT.Sqrt, m, bias=c.eps, scale=1.0 / 64)
        c.p.give(bank, t)
        t = c.recip(sq[:, :, :], sq[:, :, :], t)
        b, o, w = place(6, 2)
        e = c.stt(V, o, od[:, :, :], c.subg[:, l:l + 1], sq[:, :, :], ALU.mult, ALU.mult, t, od.toks, c.subg_t[l], w)
        made(6, 2, b, o, e)
        mem.give(od, e)
        mem.give(sq, e)
    jobs.append(differential())
    fa = new("fa", [2, 256])
    c.unit(st, 2, [("toks", h, keep(fa))])
    step()
    yield

    def fourier():
        f = new("ff", [2, 512], True)
        for i in range(2):
            bank, bw = c.p.take()
            for k in range(2):
                m = c.mm(bank[:, :], fa[:, k, i * 128:i * 128 + 128], c.fft[:, k * 512:k * 512 + 512], k == 0, k == 1, fa.toks, c.second_t, bw)
            e = c.cp(A, f[:, i, :], bank[:, :], m, f.w)
            c.p.give(bank, e)
            f.toks.append(e)
            yield
        mem.give(fa, m)
        bank, bw = c.p.take()
        for i in range(2):
            for k in range(2):
                m = c.mm(bank[:, i * 256:i * 256 + 256], c.fft[:, 1024 + k * 128:1152 + k * 128], f[:, i, k * 256:k * 256 + 256], k == 0, k == 1, f.toks, bw)
        b, o, w = place(0, 2)
        e = c.cp(A, o, bank[:, :].rearrange("p (i t) -> p i t", i=2), m, w)
        c.p.give(bank, e)
        mem.give(f, m)
        made(0, 2, b, o, e)
    jobs.append(fourier())
    uv = new("uv", [2, 512])

    def to_uv(n):
        def evac(t, ps, tok):
            e = c.act(uv[:, t, n * 256:n * 256 + 256], ps, ACT.Gelu_apprx_tanh, tok, uv.w)
            uv.toks.append(e)
            return e
        return evac
    for n in range(2):
        c.unit(st, 2, [("toks", h, to_uv(n))])
        step()
        yield
    c.drop(h, c.last_mm)
    if split:
        out_op[0] = c.operand(name + "y2", [8, 256], True)
        settle()

    def gating():
        s_ = new("lst", [4])
        t0 = []
        t = c.red(s_[:, 0:2], uv[:, :, 256:512], ALU.add, uv.toks, s_.w)
        t = c.ts(V, s_[:, 0:2], s_[:, 0:2], -1.0 / 256, None, ALU.mult, None, t)
        sqb = new("lsq", [2, 256], True)
        for i in range(2):
            e = c.ts(V, uv[:, i, 256:512], uv[:, i, 256:512], s_[:, i:i + 1], None, ALU.add, None, t)
            t0.append(c.act(sqb[:, i, :], uv[:, i, 256:512], ACT.Square, e, sqb.w, s_.w, accum=s_[:, 2 + i:3 + i]))
        r = c.rstd(s_[:, 2:4], s_[:, 2:4], 256.0, t0)
        mem.give(sqb, t0)
        et = []
        for i in range(2):
            o = uv[:, i, 256:512]
            e = c.stt(V, o, o, s_[:, 2 + i:3 + i], ln[:, 0, :], ALU.mult, ALU.mult, r, gl.all)
            et.append(c.tt(V, o, o, ln[:, 1, :], ALU.add, e))
        mem.give(s_, et)
        mem.give(ln, et)
        wT = new("wsT", [4, 128], True)
        bank, bw = c.p.take()
        for g_ in range(4):
            m = c.tr(bank[:, g_ * 128:g_ * 128 + 128], ws[:, g_, :], gl.all, bw)
        e = c.cp(A, wT[:, :, :], bank[:, :].rearrange("p (g q) -> p g q", g=4), m, wT.w)
        c.p.give(bank, e)
        mem.give(ws, m)
        yield
        bank, bw = c.p.take()
        for g_ in range(4):
            m = c.mm(bank[:, g_ * 128:g_ * 128 + 128], wT[:, g_, :], uv[:, :, 256 + g_ * 64:320 + g_ * 64], True, True, e, et, bw)
        mem.give(wT, m)
        es = []
        for g_ in range(4):
            u_ = uv[:, :, g_ * 64:g_ * 64 + 64]
            es.append(c.stt(V, u_, bank[:, g_ * 128:g_ * 128 + 128].rearrange("p (t n) -> p t n", t=2), column(c, "sb_2", 1, l * 4 + g_), u_, ALU.add, ALU.mult, m, c.vec_t))
        c.p.give(bank, es)
        yield
        bank, bw = c.p.take()
        for i in range(2):
            for t_ in range(2):
                m = c.tr(bank[:, i * 256 + t_ * 128:i * 256 + t_ * 128 + 128], uv[:, t_, i * 128:i * 128 + 128], es, bw)
        b, o, w = place(4, 2)
        e = c.cp(A, o, bank[:, :].rearrange("p (i t) -> p i t", i=2), m, w)
        c.p.give(bank, e)
        mem.give(uv, m)
        made(4, 2, b, o, e)
    jobs.append(gating())
    while jobs:
        step()
        if not own:
            c.fill(1)
        yield
    if own:
        kv.update(nk=nk, nv=nv, dk=dk, dv=dv)
    c.y_ = out_op[0]


def last_keys(c, l, h, kv, st, name):
    for k, kind in (("nk", "cols"), ("nv", "toks"), ("dk", "cols"), ("dv", "toks")):
        buf = c.mem.take(name + k, [2, 256])
        buf.toks = []

        def evac(i, ps, t):
            e = c.cp(c.A if i % 2 else c.V, buf[:, i, :], ps, t, buf.w)
            buf.toks.append(e)
            return e
        c.unit(st, 2, [(kind, h, evac)])
        kv[k] = buf
        yield


def add_gated(c, x, xt, gate, gt, tmp, last, n):
    def evac(t, ps, tok):
        s = slice(n * 256, n * 256 + 256)
        b = (2 * n + t) % 4
        e = c.tt(c.V, tmp[:, b, :], ps, gate[:, s], ALU.mult, tok, gt, tmp.w, last[b])
        last[b] = [c.tt(c.V, x[:, t, s], x[:, t, s], tmp[:, b, :], ALU.add, e, xt)]
        x.new.append(last[b][0])
        return e
    return evac


def ffn(c, h, x, xt, gate, gt, st, name, split):
    mem, V, A = c.mem, c.V, c.A
    hid = [c.operand(name + "hid", [4, 256], split) for _ in range(2)]
    rl = mem.take(name + "relu", [4, 256])
    last_h, last_r = [[], []], [[] for _ in range(4)]

    def up(b):
        op = hid[b % 2]
        op.toks = []

        def relu2(base):
            def evac(i, ps, t):
                k = base + i
                r = rl[:, k, :]
                w = (op.raw or op.hi).w
                e = c.act(r, ps, ACT.Relu, t, rl.w, last_r[k])
                if split:
                    f = c.tt(V, r, r, r, ALU.mult, e)
                    hi, lo = op.hi[:, k, :], op.lo[:, k, :]
                    f = c.cp(A, hi, r, f, w, last_h[b % 2])
                    f = c.tt(V, lo, r, hi.bitcast(F32), ALU.subtract, f, op.lo.w, last_h[b % 2])
                else:
                    f = c.tt(V, op.raw[:, k, :], r, r, ALU.mult, e, w, last_h[b % 2])
                last_r[k] = [f]
                op.toks.append(f)
                return e
            return evac
        for n in range(2):
            c.unit(st, 2, [("cols", h, relu2(2 * n))])
            yield

    def down(b):
        op = hid[b % 2]
        for k in range(4):
            u = st.get()
            for t in range(2):
                for n in range(2):
                    ops = c.passes(op, u)
                    for j, (p, w) in enumerate(ops):
                        m = c.mm(acc[t][n][0][:, :], p[:, k, t * 128:t * 128 + 128], w[:, 0, n * 512:n * 512 + 512],
                                 b == 0 and k == 0 and j == 0, b == 7 and k == 3 and j == len(ops) - 1, op.toks, u.toks, acc[t][n][1])
                    acc[t][n] = (acc[t][n][0], acc[t][n][1], m)
            st.done(m)
            if k % 2:
                yield
        last_h[b % 2] = [m]
    yield from up(0)
    acc = [[(*c.p.take(), None) for _ in range(2)] for _ in range(2)]
    for b in range(8):
        if b < 7:
            yield from up(b + 1)
        yield from down(b)
    c.drop(h, c.last_mm)
    for i in range(2):
        c.drop(hid[i], last_h[i])
    mem.give(rl, last_r)
    x.new = []
    tmp = mem.take(name + "tmp", [2, 2, 512])
    for t in range(2):
        for n in range(2):
            s = slice(n * 512, n * 512 + 512)
            e = c.tt(V, tmp[:, t, n, :], acc[t][n][0][:, :], gate[:, s], ALU.mult, acc[t][n][2], gt, tmp.w)
            c.p.give(acc[t][n][0], e)
            x.new.append(c.tt(V, x[:, t, s], x[:, t, s], tmp[:, t, n, :], ALU.add, e, xt))
    mem.give(tmp, x.new)
    yield


def layer(c, l, x, xt, m, which, kv, st, name, split):
    mem = c.mem
    own = which == 1
    xn, xnt = c.normed(x, name + "xn", xt)
    if not own:
        c.fill(7)
    while m["ct"][0] is None:
        yield
    a, sh, at = scale_shift(c, m, which, 0, 1, column(c, "n1_2", 8, 8 * l), name + "a")
    h = c.operand(name + "h", [8, 256], split)
    c.turned(xn, xnt, a, sh, h, at)
    mem.give(xn, c.pe_last())
    mem.give(a, h.toks)
    if not own:
        c.fill(3)
    yield
    yield from mixers(c, l, h, own, kv, st, name, split)
    y = c.y_
    gate = mem.take(name + "g", [1024])
    gt = c.gate(m, which, 2, gate)
    tmp = mem.take(name + "t", [4, 256])
    x.new, last = [], [[] for _ in range(4)]
    for n in range(4):
        c.unit(st, 2, [("toks", y, add_gated(c, x, xt, gate, gt, tmp, last, n))])
        yield
    c.drop(y, c.last_mm)
    mem.give(tmp, x.new)
    mem.give(gate, x.new)
    xt = x.new
    if name == "x0":
        c.fillers.append(context_keys(c))
    xn, xnt = c.normed(x, name + "xn", xt)
    if not own:
        c.fill(8)
    yield
    a, sh, at = scale_shift(c, m, which, 3, 4, column(c, "n2_2", 8, 8 * l), name + "a")
    h = c.operand(name + "h", [8, 256], split)
    c.turned(xn, xnt, a, sh, h, at)
    mem.give(xn, c.pe_last())
    mem.give(a, h.toks)
    gate = mem.take(name + "g", [1024])
    gt = c.gate(m, which, 5, gate)
    if not own:
        c.fill(3)
    yield
    yield from ffn(c, h, x, xt, gate, gt, st, name, split)
    mem.give(gate, x.new)
    x.toks = x.new


def context_keys(c):
    mem = c.mem
    m = c.mods["m3"]
    xn, xnt = c.normed(c.cx, "c1xn", c.cx.toks)
    mem.give(c.cx, xnt)
    yield
    a, sh, at = scale_shift(c, m, 1, 0, 1, column(c, "n1_2", 8, 8), "c1a")
    h = c.operand("c1h", [8, 256], False)
    c.turned(xn, xnt, a, sh, h, at)
    mem.give(xn, c.pe_last())
    mem.give(a, h.toks)
    yield
    st = Stream(c, [by_cols(c.d["w_in_2"][1], c0) for c0 in (512, 768, 1792, 2048)], False, 0)
    yield from last_keys(c, 1, h, c.kv[1], st, "c1")
    c.drop(h, c.last_mm)


def normed_by(c, x, xt, gain, gt, out):
    xn, t = c.normed(x, "fin", xt)
    toks = [c.tt(c.V, out[:, i, :], xn[:, i, :], gain[:, :], ALU.mult, t, gt) for i in range(2)]
    c.mem.give(xn, toks)
    return toks


def run(gens):
    gens = list(gens)
    while gens:
        for g in list(gens):
            if next(g, "end") == "end":
                gens.remove(g)


def share(a, b, na, nb):
    live = [a, b]
    while live:
        for g, n in ((a, na), (b, nb)):
            for _ in range(n):
                if g in live and next(g, "end") == "end":
                    live.remove(g)


def program(nc, d, out):
    with ExitStack() as ctx:
        c = Core(nc, ctx, d)
        mem = c.mem
        c.hf_t, c.st_t, c.dm_t = [], [], []
        c.kv = [{}, {}]
        c.more_slots(4)
        c.more_pairs(4)
        setup(c)
        cond, ct = c.conds[0]
        ada1 = c.ada("m1", d["ada_w"][0], d["ada_b"][0], cond, ct)
        pre = [filters(c), decays(c)]
        next(ada1)
        vectors(c)
        while c.mods["m1"]["ct"][0] is None:
            next(ada1)
            for j in list(pre):
                if next(j, "end") == "end":
                    pre.remove(j)
        run(pre)
        cond, ct = c.conds[1]
        ada2 = c.ada("m2", d["ada_w_2"][0], d["ada_b_2"][0], cond, ct)
        c.fillers = [ada1, ada2]
        for _ in first_mix(c):
            c.fill(1)
        c.fill(99)
        c.less_pairs(4)
        c.more_slots(4)

        m1 = c.mods["m1"]
        xn, xt = c.normed(c.x, "xn2", c.x_t)
        ax, sh, at = scale_shift(c, m1, 0, 3, 4, column(c, "n2", 8), "ax2")
        c.rw, c.rb = mem.take("rw", [8, 36]), mem.take("rb", [36])
        g = c.group("router")
        c.G.dma(g, c.rw[:, :, 0:4], d["router_group_w"][0].rearrange("(k p) n -> p k n", p=128), c.rw.w)
        c.G.dma(g, c.rw[:, :, 4:36], d["router_expert_w"][0].rearrange("(k p) n -> p k n", p=128), c.rw.w)
        c.G.dma(g, c.rb[:, 0:4], d["router_group_b"].to_broadcast([128, 4]), c.rb.w)
        c.G.dma(g, c.rb[:, 4:36], d["router_expert_b"].to_broadcast([128, 32]), c.rb.w)
        c.rw_t = g.all
        h2 = c.operand("h2", [8, 256], False)
        c.turned(xn, xt, ax, sh, h2, at)
        route(c, h2.raw, h2.toks)
        c.drop(h2, c.pe_last())
        gate = mem.take("gt2", [1024])
        gtt = c.gate(m1, 0, 5, gate)
        mem.give(m1["sb"], gtt)

        c.cx = mem.take("cx", [2, 1024])
        g = c.group("cx")
        c.S.dma(g, c.cx[:, :, :], d["ctx_2"].rearrange("o (t p) n -> p (o t) n", p=128), c.cx.w)
        for _ in second_consts(c):
            pass
        crowded(c)
        st = Stream(c, layer_items(c, 0), False, 0)
        share(experts(c, xn, xt, ax, sh, at, gate, gtt), layer(c, 0, c.cx, g.all, c.mods["m2"], 1, c.kv[0], st, "c0", False), 1, 1)
        c.x_t = [beyond(c, xn, ax, sh, gate)]
        for b in (xn, gate, c.rk, c.wt, c.cnt, c.cnti, ax, m1["col"][0], m1["col"][1]):
            mem.give(b, c.x_t)
        c.less_slots(4)
        c.more_pairs(3)
        gain = mem.take("gain", [1024])
        g = c.group("gain")
        c.S.dma(g, gain[:, :], d["final_norm_g"].rearrange("(o n) -> o n", o=1).to_broadcast([128, 1024]), gain.w)
        c.fillers = [c.ada("m3", d["ada_w_2"][1], d["ada_b_2"][1], cond, ct)]
        x_t = normed_by(c, c.x, c.x_t, gain, g.all, c.x)
        c.fill(6)
        mem.give(gain, x_t)
        st = Stream(c, layer_items(c, 0) + layer_items(c, 1), True, 2)
        run([layer(c, 0, c.x, x_t, c.mods["m2"], 0, c.kv[0], st, "x0", True)])
        c.fill(99)
        run([layer(c, 1, c.x, c.x.toks, c.mods["m3"], 0, c.kv[1], st, "x1", True)])
        gain = mem.take("gain2", [1024])
        g = c.group("gain2")
        c.S.dma(g, gain[:, :], d["final_g_2"].rearrange("(o n) -> o n", o=1).to_broadcast([128, 1024]), gain.w)
        x_t = normed_by(c, c.x, c.x.toks, gain, g.all, c.x)
        c.S.dma(c.outs, out.rearrange("o (t p) n -> p (o t) n", p=128), c.x[:, :, :], x_t)

        number([c.T, c.V, c.A, c.G, c.S])
        with nc.Block() as block:
            @block.tensor
            def _(e):
                c.T.play(e)

            @block.vector
            def _(e):
                c.V.play(e)

            @block.scalar
            def _(e):
                c.A.play(e)

            @block.gpsimd
            def _(e):
                c.G.play(e)

            @block.sync
            def _(e):
                c.S.play(e)
                e.wait_ge(c.outs.sem, c.outs.n)
    return c


_INS = ['x', 'c', 'ctx', 'c_ctx', 'ada_w', 'ada_b', 'norm1_g', 'norm2_g', 'w_in', 'b_in', 'ret_decay_logit', 'ret_w_o',
        'hy_conv_w', 'hy_conv_b', 'hy_ffn_w1', 'hy_ffn_b1', 'hy_ffn_freq', 'hy_ffn_w2', 'hy_ffn_b2', 'hy_ffn_w3', 'hy_skip',
        'hy_w_o', 'w_out', 'router_group_w', 'router_group_b', 'router_expert_w', 'router_expert_b', 'expert_w1', 'expert_w3',
        'expert_w2', 'final_norm_g', 'c_2', 'ctx_2', 'c_ctx_2', 'ada_w_2', 'ada_b_2', 'norm1_g_2', 'norm2_g_2', 'w_in_2',
        'w_out_2', 'na_rpb_2', 'sgu_ln_g_2', 'sgu_ln_b_2', 'sgu_w_2', 'sgu_b_2', 'diff_lq1_2', 'diff_lk1_2', 'diff_lq2_2',
        'diff_lk2_2', 'diff_subln_g_2', 'w_ff1_2', 'w_ff2_2', 'final_g_2']


def kernel(**inputs):
    import numpy as _np
    import concourse.bacc as _bacc
    from concourse import mybir as _mybir
    from concourse.bass_utils import run_bass_kernel_spmd as _run

    nc = _bacc.Bacc("TRN2", target_bir_lowering=False, num_devices=1)
    arrays, d = {}, {}
    named = [(n, _np.ascontiguousarray(inputs[n])) for n in _INS] + list(constants().items())
    for name, a in named:
        arrays[f"in_{name}_dram"] = a
        d[name] = nc.dram_tensor(f"in_{name}_dram", a.shape, _mybir.dt.from_np(a.dtype), kind="ExternalInput").ap()
    out = nc.dram_tensor("out_0_dram", (1, 256, 1024), _mybir.dt.float32, kind="ExternalOutput").ap()
    program(nc, d, out)
    r = _run(nc, [arrays], core_ids=[0])
    return r.results[0]["out_0_dram"]
```

```python
import math
from contextlib import ExitStack

import numpy as np

import concourse.bass as bass
from concourse import mybir
from concourse.alu_op_type import AluOpType as ALU

F32 = mybir.dt.float32
F32R = mybir.dt.float32r
I32 = mybir.dt.int32
ACT = mybir.ActivationFunctionType
AX = mybir.AxisListType

EPS = 1e-6
NEG = -1.0e30


def _rope(n_freq):
    t = np.arange(256)
    inv = (10000.0 ** (-np.arange(n_freq, dtype=np.float32) / np.float32(n_freq))).astype(np.float32)
    row = (t // 64).astype(np.float32)[None, :] * inv[:, None]
    col = (t % 64).astype(np.float32)[None, :] * inv[:, None]
    return np.cos(row), np.sin(row), np.cos(col), np.sin(col)


def _swap(n, width):
    m = np.zeros((n, n), np.float32)
    for b in range(0, n, 2 * width):
        for i in range(width):
            m[b + width + i, b + i] = -1.0
            m[b + i, b + width + i] = 1.0
    return m


def constants():
    f = np.float32
    c = {}
    p = np.arange(128)
    c["k_eye"] = np.stack([np.eye(128), p[:, None] < p[None, :], np.ones((128, 128)), np.eye(128)[::-1]], 1).astype(f)
    small = np.zeros((128, 288), f)
    small[:, 0:32] = np.arange(32)
    small[:, 32] = EPS
    j = (np.arange(2)[None, :] * 128 + p[:, None]).astype(f)
    small[:, 50:52] = 255 - j
    small[:, 52:54] = j
    small[:, 54:56] = j + 1
    small[:, 56:58] = 256 - j
    small[:, 64:288] = np.arange(32, 256)
    c["k_small"] = small
    i = np.arange(256)
    jj = j[:, :, None]
    c["k_ret"] = np.concatenate([np.maximum(i[None, None, :] - jj, 0).reshape(128, 512),
                                 np.maximum(jj - i[None, None, :], 0).reshape(128, 512)], 1).astype(f)
    cr, sr, cc, sc = _rope(32)
    c["k_rope"] = np.concatenate([np.concatenate([cr, cr, cc, cc], 0), np.concatenate([sr, sr, sc, sc], 0), _swap(128, 32)], 1).astype(f)
    cr, sr, cc, sc = _rope(8)
    c["k_rope2"] = np.concatenate([np.tile(np.concatenate([cr, cr, cc, cc], 0), (4, 1)),
                                   np.tile(np.concatenate([sr, sr, sc, sc], 0), (4, 1)), _swap(128, 8)], 1).astype(f)
    t = np.arange(256, dtype=np.float64)
    ang = 2 * np.pi * (np.outer(t, t) % 512) / 512
    co, si = np.cos(ang), np.sin(ang)
    alt = (-1.0) ** t
    si1, co1 = si.copy(), co.copy()
    si1[:, 0] = alt
    co1[:, 0] = alt
    blocks = [co[:, :128], co[:, 128:], si[:, :128], si[:, 128:], si1[:, :128], co1[:, :128]]
    fw = np.stack([b.reshape(2, 128, 128) for b in blocks], 0)
    c["k_dft"] = fw.transpose(2, 0, 1, 3).reshape(128, 1536).astype(f)
    ic, isn = co * 2 / 512, si * 2 / 512
    ic[0] = 1.0 / 512
    isn[0] = alt / 512
    inv = np.concatenate([ic, isn], 0).reshape(4, 128, 256)
    c["k_idft"] = inv.transpose(1, 0, 2).reshape(128, 1024).astype(f)
    tn = (np.arange(256, dtype=f) / f(256)).astype(f)
    bands = np.linspace(1e-4, 15, 16, dtype=f)
    ph = (f(2.0 * math.pi) * tn[:, None] * bands[None, :]).astype(f)
    c["k_feat"] = np.ascontiguousarray(np.concatenate([tn[:, None], np.cos(ph), -np.sin(ph)], 1).T).astype(f)
    slow, fast = abs(math.log(1e-2)) / 1.5, abs(math.log(1e-2)) / 0.3
    deltas = np.linspace(slow, fast, 512, dtype=f)
    dec = np.exp((-tn[:, None] * deltas[None, :]).astype(f)).astype(f)
    c["k_decay"] = np.ascontiguousarray(dec.reshape(2, 128, 512).transpose(1, 0, 2).reshape(128, 1024))
    ang = 2 * np.pi * (np.outer(t, t) % 256) / 256
    cs = np.concatenate([np.cos(ang), np.sin(ang)], 1).reshape(2, 128, 512)
    d = np.arange(64)
    a64 = 2 * np.pi * (np.outer(d, d) % 64) / 64
    bd = np.zeros((2, 128, 128))
    for h in range(2):
        s = slice(64 * h, 64 * h + 64)
        bd[0, s, s] = np.cos(a64) / 128
        bd[1, s, s] = -np.sin(a64) / 128
    c["k_fft"] = np.concatenate([cs.transpose(1, 0, 2).reshape(128, 1024), bd.transpose(1, 0, 2).reshape(128, 256)], 1).astype(f)
    hd = np.zeros((128, 128), f)
    hd[:64, :64] = 1
    hd[64:, 64:] = 1
    c["k_hd"] = hd
    mask = np.zeros((128, 2, 256), f)
    q = np.arange(64)
    start = np.clip(q - 8, 0, 48)
    inw = (q[None, :] >= start[:, None]) & (q[None, :] < start[:, None] + 16)
    m64 = np.where(inw, 0.0, NEG).astype(f)
    full = np.tile(m64, (2, 4))
    mask[:, :, :] = full[::-1][:, None, :]
    c["k_mask"] = mask.reshape(128, 512)
    return {k: np.ascontiguousarray(v, dtype=f) for k, v in c.items()}


class Tok:
    def __init__(self, q, i, at):
        self.q, self.i, self.at = q, i, at

    def resolve(self):
        return self.q.sem, self.q.count[self.i]


class DTok:

    def __init__(self, owner, val, at):
        self.owner, self.val, self.at = owner, val, at

    def resolve(self):
        return self.owner.sem, self.owner.n if self.val is None else self.val


def flat(x):
    if x is None:
        return []
    if isinstance(x, (list, tuple)):
        return [t for y in x for t in flat(y)]
    return [x]


LATER = 1e9


def when(*toks):
    return max([t.at for t in flat(toks)], default=0.0)


class Link:

    def __init__(self):
        self.now = 0.0


class Queue:
    def __init__(self, sem, link):
        self.sem, self.ops, self.count, self.now, self.busy, self.link = sem, [], {}, 0.0, 0.0, link

    def __call__(self, fn, *waits, cost=0.08):
        w = flat(waits)
        self.ops.append((fn, w, False))
        self.now = max([self.now] + [t.at + 0.1 for t in w]) + cost
        self.busy += cost
        return Tok(self, len(self.ops) - 1, self.now)

    def raw(self, fn, *waits):
        w = flat(waits)
        self.ops.append((lambda e: fn(e, w), w, True))

    def dma(self, owner, dst, src, *waits):
        w = flat(waits)
        self.ops.append((lambda e: e.dma_start(dst, src).then_inc(owner.sem, 16), w, False))
        owner.n += 16
        self.now = max([self.now] + [t.at for t in w]) + 0.06
        self.link.now = max(self.link.now, self.now) + float(np.prod(dst.shape)) * 4 / 3.6e5
        owner.at = max(owner.at, self.link.now + 2.0)
        return DTok(owner, owner.n, self.link.now + 2.0)

    def play(self, eng):
        seen = {}
        for i, (fn, waits, raw) in enumerate(self.ops):
            if raw:
                fn(eng)
                continue
            need = {}
            for w in waits:
                sem, val = w.resolve()
                need[sem.name] = (sem, max(val, need.get(sem.name, (sem, 0))[1]))
            for name, (sem, val) in need.items():
                if seen.get(name, 0) < val:
                    eng.wait_ge(sem, val)
                    seen[name] = val
            if fn is None:
                continue
            ins = fn(eng)
            if i in self.count:
                ins.then_inc(self.sem, 1)


def number(queues):
    wanted = {}
    for q in queues:
        for _, waits, _ in q.ops:
            for w in waits:
                if isinstance(w, Tok):
                    wanted.setdefault(id(w.q), set()).add(w.i)
    for q in queues:
        for n, i in enumerate(sorted(wanted.get(id(q), ()))):
            q.count[i] = n + 1


class Loads:

    def __init__(self, sem):
        self.sem, self.n, self.at = sem, 0, 0.0

    @property
    def all(self):
        return DTok(self, None, self.at)


class Slot:
    def __init__(self, ap, sem):
        self.ap, self.sem, self.n, self.last, self.at = ap, sem, 0, [], 0.0


class Pool:

    def __init__(self, banks):
        self.free = [(b, []) for b in banks]

    def take(self):
        return self.free.pop(0)

    def give(self, bank, *toks):
        self.free.append((bank, flat(toks)))


class Buf:
    def __init__(self, t, lo, hi, w):
        self.t, self.lo, self.hi, self.w = t, lo, hi, w

    def __getitem__(self, k):
        return self.t[k]


class Mem:

    def __init__(self, nc, lo, hi):
        self.nc, self.free, self.n, self.end, self.low = nc, [(lo, hi, [])], 0, hi, hi - lo
        self.live, self.clock = {}, None

    def spans(self, size):
        spans = []
        for lo, hi, toks in self.free:
            if spans and spans[-1][1] == lo:
                spans[-1] = (spans[-1][0], hi)
            else:
                spans.append((lo, hi))
        return [x for x in spans if x[1] - x[0] >= size]

    def fits(self, size):
        return bool(self.spans(size))

    def take(self, name, shape, dtype=F32, parts=128, top=False):
        size = (4 * int(np.prod(shape)) + 31) // 32 * 32
        spans = self.spans(size)
        if not spans:
            raise MemoryError(f"{name} {size}: free {[(a, b) for a, b, _ in self.free]} live {self.live}")
        def cost(span):
            if self.clock is None:
                return 0.0, span[1] - span[0]
            lo = span[1] - size if top else span[0]
            at = when([t for a, b, t in self.free if b > lo and a < lo + size])
            return max(at - self.clock() - 1.0, 0.0), span[1] - span[0]
        tight = min(spans, key=cost)
        lo = tight[1] - size if top else tight[0]
        toks, rest = [], []
        for a, b, t in self.free:
            if b <= lo or a >= lo + size:
                rest.append((a, b, t))
                continue
            toks += t
            if a < lo:
                rest.append((a, lo, t))
            if b > lo + size:
                rest.append((lo + size, b, t))
        self.free = rest
        self.n += 1
        t = self.nc.alloc_sbuf_tensor_at(f"{name}_{self.n}", [parts, *shape], dtype, offset=lo)
        self.low = min(self.low, sum(b - a for a, b, _ in self.free))
        buf = Buf(t, lo, lo + size, toks)
        buf.key = name + f"_{self.n}"
        self.live[buf.key] = size
        return buf

    def give(self, buf, *toks):
        del self.live[buf.key]
        self.free.append((buf.lo, buf.hi, flat(toks)))
        self.free.sort(key=lambda x: x[0])


class Op:

    def __init__(self, raw=None, hi=None, lo=None, toks=None, low=None):
        self.raw, self.hi, self.lo, self.toks, self.by, self.low = raw, hi, lo, toks or [], {}, {}
        if low:
            self.low[None] = low

    def high_at(self, k):
        return self.toks + self.by.get(k, [])

    def at(self, k):
        return self.toks + self.by.get(k, []) + self.low.get(k, []) + self.low.get(None, [])

    def came(self, rows, *toks, low=None):
        for k in rows:
            self.by.setdefault(k, []).extend(flat(toks))
            self.low.setdefault(k, []).extend(flat([low]))

    @property
    def all(self):
        return self.toks + flat(list(self.by.values())) + flat(list(self.low.values()))


class Rows:

    def __init__(self, buf, toks):
        self.buf, self.t = buf, {(t, h): flat(toks) for t in range(2) for h in range(2)}
        self.ss, self.st, self.banks = None, [], None
        self.rms, self.then = None, None

    @property
    def all(self):
        return flat(list(self.t.values()))


class Stream:

    def __init__(self, c, items, split, ahead, deep, then=None):
        self.c, self.items, self.split, self.ahead, self.deep, self.then = c, list(items), split, ahead, deep, then
        self.loads, self.ready, self.unit = [], [], None

    def preload(self, n):
        while len(self.loads) < n and self.items and self.c.slots:
            src, views = self.items.pop(0)
            self.loads.append((self.c.load(src), list(views)))
        if self.then is not None and not self.items and n > len(self.loads):
            self.then.preload(min(n - len(self.loads), 3))

    def prime(self, n):
        while len(self.ready) < n and self.issue():
            pass
        if self.then is not None and not self.items and not self.loads and self.unit is None and n > len(self.ready):
            self.then.prime(n - len(self.ready))

    def issue(self):
        c = self.c
        if self.unit is None:
            if not self.loads and self.items:
                self.preload(1)
            if not self.loads:
                return False
        if self.split and not c.pairs:
            return False
        if self.unit is None:
            self.unit = self.loads.pop(0)
        (s, v, lt), views = self.unit
        w = views.pop(0)(v)
        end = not views
        if end:
            self.unit = None
        if not self.split:
            self.ready.append((Op(raw=w, toks=[lt]), s, end))
            return True
        hi, lo, free = c.pairs.pop(0)
        a, b = w.shape[1:]
        hv, lv = (x[:, 0:a * b].rearrange("p (a b) -> p a b", a=a) for x in (hi, lo))
        th = c.cp(c.A, hv, w, lt, free)
        t = c.tt(c.V, lv, w, hv.bitcast(F32), ALU.subtract, lt, th, free)
        if end:
            c.done(s, t)
        self.ready.append((Op(hi=hv, lo=lv, toks=[th], low=[t]), (hi, lo), None))
        return True

    def get(self):
        if not self.ready:
            self.issue()
        self.part = self.ready.pop(0)
        self.prime(self.ahead)
        self.preload(self.deep)
        return self.part[0]

    def done(self, *toks):
        _, owner, last = self.part
        if self.split:
            self.c.pairs.append((*owner, flat(toks)))
        elif last:
            self.c.done(owner, *toks)


def by_rows(w, r0):
    return w[r0:r0 + 256, :].rearrange("(k p) n -> p k n", p=128), [lambda v: v[:, 0:1, :], lambda v: v[:, 1:2, :]]


def by_cols(w, c0, n=256):
    return w[:, c0:c0 + n].rearrange("(k p) c -> p k c", p=128), [lambda v: v[:, 0:4, :], lambda v: v[:, 4:8, :]]


class Job:

    def __init__(self, c, gen):
        self.c, self.gen, self.toks, self.over = c, gen, [], False

    @property
    def at(self):
        return self.toks() if callable(self.toks) else when(self.toks)

    def step(self):
        self.toks = next(self.gen, "end")
        if self.toks == "end":
            self.toks, self.over = [], True
        return True

    def go(self):
        return self.at <= self.c.T.now + 0.2 and self.step()


class Jobs:

    def __init__(self, c):
        self.c, self.list = c, []

    def add(self, gen):
        self.list.append(Job(self.c, gen))

    def tidy(self):
        self.list = [j for j in self.list if not j.over]

    def go(self, n=99):
        while n > 0 and any(j.go() for j in self.list):
            self.tidy()
            n -= 1

    def ahead(self, at):
        while self.list:
            j = min(self.list, key=lambda j: j.at)
            if max(j.at, self.c.T.now) > at - 0.5:
                return
            j.step()
            self.tidy()

    def drain(self):
        while self.list:
            j = min(self.list, key=lambda j: max(j.at, self.c.T.now))
            yield j.toks
            while j.at > self.c.T.now + 0.5 and self.c.fill():
                pass
            j.step()
            self.tidy()


class Core:

    def __init__(self, nc, ctx, dram):
        self.nc, self.ctx, self.d = nc, ctx, dram
        self.link = Link()
        self.T, self.V, self.A, self.G, self.S = (Queue(self.sem(n), self.link) for n in ("pe", "dve", "act", "pool", "sp"))
        self.mem = Mem(nc, 16896, 229344)
        self.banks = [ctx.enter_context(nc.psum_tensor(f"bank{i}", [128, 512], F32)) for i in range(8)]
        self.p = Pool(self.banks)
        self.slots, self.pairs, self.nslot = [], [], 0
        self.slot_bufs, self.pair_bufs, self.slot_sems = {}, {}, []
        self.fillers, self.loaded = [], 0
        self.outs = Loads(self.sem("stores"))

    def sem(self, name):
        return self.ctx.enter_context(self.nc.semaphore(name))

    def group(self, name):
        return Loads(self.sem(name))

    def more_slots(self, n, some=False):
        for i in range(n):
            if some and not self.mem.fits(8192):
                return i
            b = self.mem.take("slot", [2048])
            s = self.slot_sems.pop() if self.slot_sems else Slot(None, self.sem(f"ring{self.nslot}"))
            self.nslot += 1
            s.ap, s.last, s.buf = b.t, b.w, b
            self.slots.append(s)
        return n

    def less_slots(self, n):
        for _ in range(n):
            s = self.slots.pop(0)
            self.mem.give(s.buf, s.last)
            self.slot_sems.append(s)

    def more_pairs(self, n):
        for _ in range(n):
            hi, lo = (self.mem.take(x, [1024], F32R) for x in ("whi", "wlo"))
            self.pair_bufs[id(hi)] = (hi, lo)
            self.pairs.append((hi, lo, hi.w + lo.w))

    def less_pairs(self, n):
        for _ in range(n):
            hi, lo, toks = self.pairs.pop(0)
            self.mem.give(hi, toks)
            self.mem.give(lo, toks)

    def load(self, src):
        self.loaded += 1
        s = self.slots.pop(0)
        shape = src.shape
        n = int(np.prod(shape[1:]))
        dst = s.ap[:, 0:n]
        if len(shape) == 3:
            dst = dst.rearrange("p (a b) -> p a b", a=shape[1])
        tok = self.S.dma(s, dst, src, s.last)
        return s, dst, tok

    def done(self, slot, *toks):
        slot.last = flat(toks)
        self.slots.append(slot)

    def fill(self, n=1, force=False):
        done = 0
        while done < n and self.fillers and (self.fillers[0].step() if force else self.fillers[0].go()):
            done += 1
            if self.fillers[0].over:
                self.fillers.pop(0)
        return done

    def pe_last(self):
        return Tok(self.T, len(self.T.ops) - 1, self.T.now)

    def width(self, ap):
        return int(np.prod(ap.shape[1:])) / 1000.0

    def cost(self, q, ap, rate=1.04):
        n = self.width(ap)
        return 0.1 + (0.85 * n if q is self.A else 2.2 * n if q is self.G else rate * n)

    def mm(self, out, lhsT, rhs, start, stop, *w):
        n = max(self.width(out), 0.064)
        k = 0.417 * n + 0.0025 if lhsT.dtype == F32R else 1.667 * n + 0.005
        return self.T(lambda e: e.matmul(out, lhsT, rhs, start=start, stop=stop), *w, cost=k * {32: 0.27, 64: 0.55}.get(out.shape[0], 1.0))

    def tr(self, out, in_, *w):
        n = in_.shape[0]
        ident = self.eye[0:n, 0, 0:n]
        return self.T(lambda e: e.transpose(out, in_, ident), *w, cost=0.11)

    def tt(self, q, out, a, b, op, *w):
        return q(lambda e: e.tensor_tensor(out, a, b, op), *w, cost=self.cost(q, out))

    def ts(self, q, out, a, s1, s2, op0, op1, *w):
        k = self.cost(q, out, 0.6)
        if op1 is None:
            return q(lambda e: e.tensor_scalar(out, a, s1, None, op0), *w, cost=k)
        return q(lambda e: e.tensor_scalar(out, a, s1, s2, op0, op1), *w, cost=k)

    def stt(self, q, out, in0, s, in1, op0, op1, *w):
        return q(lambda e: e.scalar_tensor_tensor(out, in0, s, in1, op0, op1), *w, cost=self.cost(q, out))

    def cp(self, q, out, in_, *w):
        if q is self.A:
            return q(lambda e: e.copy(out, in_), *w, cost=self.cost(q, out))
        return q(lambda e: e.tensor_copy(out, in_), *w, cost=self.cost(q, out))

    def act(self, out, in_, func, *w, bias=None, scale=None, accum=None):
        kw = {}
        if bias is not None:
            kw["bias"] = bias
        if scale is not None:
            kw["scale"] = scale
        if accum is not None:
            kw["accum_out"] = accum
        return self.A(lambda e: e.activation(out, in_, func, **kw), *w, cost=self.cost(self.A, out))

    def red(self, out, in_, op, *w, negate=False):
        k = self.cost(self.V, in_)
        if negate:
            return self.V(lambda e: e.tensor_reduce(out, in_, AX.X, op, negate=True), *w, cost=k)
        return self.V(lambda e: e.tensor_reduce(out, in_, AX.X, op), *w, cost=k)

    def recip(self, out, in_, *w):
        return self.V(lambda e: e.reciprocal(out, in_), *w, cost=self.cost(self.V, out, 6.4))

    def set(self, q, out, val, *w):
        return q(lambda e: e.memset(out, val), *w)

    def rstd(self, out, sums, width, *w):
        t = self.act(out, sums, ACT.Sqrt, *w, bias=self.eps[0:out.shape[0]], scale=1.0 / width)
        return self.recip(out, out, t)

    def rsqrt(self, out, x, *w):
        n = int(np.prod(out.shape[1:]))
        b = self.mem.take("newton", [n])
        t = self.ts(self.V, out.bitcast(I32), x.bitcast(I32), -0.5, float(0x5F3759DF), ALU.mult, ALU.add, w, b.w)
        for _ in range(3):
            t = self.tt(self.V, b[:, :], out, out, ALU.mult, t)
            t = self.stt(self.V, b[:, :], b[:, :], -0.5, x, ALU.mult, ALU.mult, t)
            t = self.stt(self.V, out, b[:, :], 1.5, out, ALU.add, ALU.mult, t)
        self.mem.give(b, t)
        return t

    def operand(self, name, shape, split, top=False):
        if split:
            return Op(hi=self.mem.take(name + "h", shape, F32R, top=top), lo=self.mem.take(name + "l", shape, F32R, top=top))
        return Op(raw=self.mem.take(name, shape, top=top))

    def drop(self, op, *toks):
        for b in (op.raw, op.hi, op.lo):
            if b is not None:
                self.mem.give(b, *toks)

    def part(self, op, k, src, *w):
        hi, lo = op.hi[:, k, :], op.lo[:, k, :]
        th = self.cp(self.A, hi, src, w, op.hi.w)
        t = self.tt(self.V, lo, src, hi.bitcast(F32), ALU.subtract, th, w, op.lo.w)
        op.came(range(k.start, k.stop), th, low=t)
        return t

    def place(self, op, k, src, *w):
        if op.hi is not None:
            return self.part(op, k, src, *w)
        t = self.cp(self.A, op.raw[:, k, :], src, w, op.raw.w)
        op.came(range(k.start, k.stop), t)
        return t

    def squared(self, r, t, h):
        self.junk_t = self.act(self.junk[:, :], r.buf[:, t, h * 512:h * 512 + 512], ACT.Square, r.t[t, h], r.ss.w, self.junk.w,
                               self.junk_t, accum=r.ss[:, t, h:h + 1])
        r.st.append(self.junk_t)

    def squared_sum(self, out, x, total, *w):
        return self.V(lambda e: e.tensor_tensor_reduce(out, x, x, 1.0, 0.0, ALU.mult, ALU.add, total), *w, cost=self.cost(self.V, out))

    def squares(self, r):
        r.ss, r.st = self.mem.take("ss", [2, 2]), []
        for t in range(2):
            for h in range(2):
                self.squared(r, t, h)
                yield

    def sums(self):
        return self.mem.take("sum", [2, 512], top=True), self.mem.take("ss", [2, 2])

    def added(self, r, acc, gate, gt, sums, each=None):
        tmp, r.ss = sums
        r.st, last = [], [[], []]
        self.roots()
        for t in range(2):
            for h in range(2):
                s, o = slice(h * 512, h * 512 + 512), tmp[:, h, :]
                bank, _, m = acc[t][h]
                e = self.tt(self.V, o, bank[:, :], gate[:, s], ALU.mult, m, gt, tmp.w, last[h])
                self.p.give(bank, e)
                r.t[t, h] = last[h] = [self.tt(self.V, r.buf[:, t, s], r.buf[:, t, s], o, ALU.add, e, r.t[t, h])]
                self.squared(r, t, h)
                if each:
                    each(t, h)
        self.mem.give(tmp, last)

    def roots(self):
        self.root_t = self.act(self.root[:, :], self.eps, ACT.Sqrt, self.eye_t, self.root.w, self.root_t)

    def inverse(self, r, name):
        o = self.mem.take(name, [2])
        t = self.red(o[:, :], r.ss[:, :, :], ALU.add, r.st, o.w)
        self.mem.give(r.ss, t)
        return o, self.rstd(o[:, :], o[:, :], 1024.0, t)

    def turn(self, r):
        r.banks = []
        for k2 in range(4):
            bank, bw = self.p.take()
            for k in range(2):
                for t in range(2):
                    i = r.buf[:, t, (2 * k2 + k) * 128:(2 * k2 + k + 1) * 128]
                    m = self.tr(bank[:, k * 256 + t * 128:k * 256 + t * 128 + 128], i, r.t[t, k2 // 2], bw, self.eye_t)
            r.banks.append((bank, m))
        return r.banks

    def turned_rows(self, r, o, ot, scale, shift, op, *w, fill=0, between=None):
        R = self.mem.take("spread", [256], top=True)
        tmp = [self.mem.take("turn", [256], top=True) for _ in range(3)]
        banks = r.banks or self.turn(r)
        bank, bw = self.p.take()
        for t in range(2):
            m = self.mm(bank[:, t * 128:t * 128 + 128], o[:, t:t + 1].to_broadcast([128, 128]), self.eye[:, 0, :], True, True, ot, bw)
        rt = self.cp(self.A, R[:, :], bank[:, 0:256], m, R.w)
        self.p.give(bank, rt)
        self.fill(fill)
        last, todo = [[], [], []], []

        def rest():
            kt, b, e = todo.pop(0)
            if op.hi is None:
                f = self.act(op.raw[:, kt, :], tmp[b][:, :], ACT.Identity, e, w, op.raw.w, bias=shift[:, kt:kt + 1])
            else:
                hi, lo = op.hi[:, kt, :], op.lo[:, kt, :]
                th = self.act(hi, tmp[b][:, :], ACT.Identity, e, w, op.hi.w, bias=shift[:, kt:kt + 1])
                f = self.stt(self.V, lo, tmp[b][:, :], shift[:, kt:kt + 1], hi.bitcast(F32), ALU.add, ALU.subtract, th, op.lo.w)
                op.came([kt], th, low=f)
            last[b] = [f]
            if op.hi is None:
                op.came([kt], f)
        es = []
        for kt in range(8):
            (bank, m), b = banks[kt // 2], kt % 3
            e = self.stt(self.V, tmp[b][:, :], bank[:, kt % 2 * 256:kt % 2 * 256 + 256], scale[:, kt:kt + 1], R[:, :], ALU.mult, ALU.mult,
                         m, rt, w, tmp[b].w, last[b])
            es.append(e)
            if kt % 2:
                self.p.give(bank, es[-2:])
            todo.append((kt, b, e))
            if kt:
                rest()
            if kt == 1 and between:
                between()
        rest()
        r.banks = None
        self.mem.give(R, es)
        for b in range(3):
            self.mem.give(tmp[b], last[b])

    def scaled_rows(self, r, o, ot):
        b = self.mem.take("scaled", [2, 1024])
        s = Rows(b, [])
        for t, q in ((0, self.V), (1, self.V)):
            if q is self.A:
                e = self.act(b[:, t, :], r.buf[:, t, :], ACT.Identity, ot, r.t[t, 0], r.t[t, 1], b.w, scale=o[:, t:t + 1])
            else:
                e = self.ts(q, b[:, t, :], r.buf[:, t, :], o[:, t:t + 1], None, ALU.mult, None, ot, r.t[t, 0], r.t[t, 1], b.w)
            s.t[t, 0] = s.t[t, 1] = [e]
        self.mem.give(o, s.all)
        return s

    def moved_rows(self, s, scale, shift, op, *w, between=None):
        if op.hi is None:
            for kt in range(8):
                (bank, m), k = s.banks[kt // 2], slice(kt, kt + 1)
                v, o = bank[:, kt % 2 * 256:kt % 2 * 256 + 256], op.raw[:, kt, :]
                if kt // 2 % 2:
                    e = self.ts(self.V, o, v, scale[:, k], shift[:, k], ALU.mult, ALU.add, m, w, op.raw.w)
                else:
                    e = self.act(o, v, ACT.Identity, m, w, op.raw.w, bias=shift[:, k], scale=scale[:, k])
                if kt % 2:
                    self.p.give(bank, e)
                op.came([kt], e)
            return
        tmp = [self.mem.take("turn", [256], top=True) for _ in range(4)]
        last, todo = [[], [], [], []], []

        def rest():
            kt, b, e = todo.pop(0)
            hi, lo = op.hi[:, kt, :], op.lo[:, kt, :]
            th = self.cp(self.A, hi, tmp[b][:, :], e, op.hi.w)
            f = self.tt(self.G if kt % 2 else self.V, lo, tmp[b][:, :], hi.bitcast(F32), ALU.subtract, e, th, op.lo.w)
            last[b] = [f]
            op.came([kt], th, low=f)
        for kt in range(8):
            if kt % 3 == 0 and between:
                between(kt // 3 + 1)
            (bank, m), b = s.banks[kt // 2], kt % 4
            v, k = bank[:, kt % 2 * 256:kt % 2 * 256 + 256], slice(kt, kt + 1)
            if kt // 2 % 2 == 1:
                e = self.ts(self.V, tmp[b][:, :], v, scale[:, k], shift[:, k], ALU.mult, ALU.add, m, w, tmp[b].w, last[b])
            else:
                e = self.act(tmp[b][:, :], v, ACT.Identity, m, w, tmp[b].w, last[b], scale=scale[:, k], bias=shift[:, k])
            if kt % 2:
                self.p.give(bank, e)
            todo.append((kt, b, e))
            if kt:
                rest()
        rest()
        for b in range(4):
            self.mem.give(tmp[b], last[b])

    def add_rows(self, stream, op, nk, acc, first, last):
        k = 0
        while k < nk:
            both = last and k == nk - 2 and stream.split
            us = []
            for i in range(2 if both else 1):
                us.append(stream.get())
                owner = stream.part
                us[-1].owner = owner
            yield [op.at(k + i) + u.at(0) for i, u in enumerate(us)]
            for t in range(2):
                for n in range(2):
                    bank, bw = acc[t][n][:2]
                    for i, u in enumerate(us):
                        ops = self.passes(op, k + i, u, 0)
                        for j, (p, w, toks) in enumerate(ops):
                            m = self.mm(bank[:, :], p[:, k + i, t * 128:t * 128 + 128], w[:, 0, n * 512:n * 512 + 512],
                                        first and k + i == 0 and j == 0, last and k + i == nk - 1 and j == len(ops) - 1, toks, bw)
                    acc[t][n] = (bank, bw, m)
            for u in us:
                stream.part = u.owner
                stream.done(m)
            self.last_mm = m
            k += len(us)

    def accumulators(self):
        return [[(*self.p.take(), None) for _ in range(2)] for _ in range(2)]

    def passes(self, a, ka, b, kb):
        if a.raw is not None:
            return ((a.raw, b.raw, a.at(ka) + b.at(kb)),)
        ha, hb = a.high_at(ka), b.high_at(kb)
        return (a.hi, b.hi, ha + hb), (a.hi, b.lo, ha + b.at(kb)), (a.lo, b.hi, a.at(ka) + hb)

    def unit(self, *a):
        for _ in self.halves(*a):
            pass

    def halves(self, stream, nparts, consumers, kpart=4):
        groups = [(kind, h, evac, i, *self.p.take()) for kind, h, evac in consumers for i in range(2)]
        last = [None] * len(groups)
        for part in range(nparts):
            if part and not stream.split:
                yield
            u = stream.get()
            for k in range(kpart):
                kk = part * kpart + k
                for n, (kind, h, _, i, bank, bw) in enumerate(groups):
                    s = slice(i * 128, i * 128 + 128)
                    if kind == "cols":
                        ops = [(a[:, k, s], b[:, kk, :], w) for a, b, w in self.passes(u, k, h, kk)]
                    else:
                        ops = [(b[:, kk, s], a[:, k, :], w) for b, a, w in self.passes(h, kk, u, k)]
                    for j, (a, b, w) in enumerate(ops):
                        last[n] = self.mm(bank[:, 0:256], a, b, kk == 0 and j == 0, kk == nparts * kpart - 1 and j == len(ops) - 1,
                                          w, bw)
            stream.done(last[-1])
        self.last_mm = last[-1]
        for n, (kind, h, evac, i, bank, bw) in enumerate(groups):
            self.p.give(bank, evac(i, bank[:, 0:256], last[n]))

    def ada(self, name, w, bias, cond, ct):
        c = self
        m = {"sb": [None] * 3, "col": [c.mem.take(name + f"c{i}", [48]) for i in range(2)], "t": [None] * 3, "ct": [None] * 3}
        self.mods[name] = m
        sts = [None]
        for q in (2, 1, 0):
            sts.insert(0, Stream(c, [(w[k * 128:k * 128 + 128, q * 2048:q * 2048 + 2048], [lambda v: v]) for k in range(8)], False, 0, 2))
        for q, st in enumerate(sts[:3]):
            br = c.mem.take(name + "b", [512], top=True)
            sb = m["sb"][q] = c.mem.take(name + "sb", [512], top=True)
            z = c.set(c.G, br[:, :], 0.0, br.w)
            g = c.group(f"{name}b{q}")
            for i in range(2):
                c.G.dma(g, br[i::32, :], bias[q * 2048:q * 2048 + 2048].rearrange("(j n) -> j n", j=4), z)
            bank, bw = self.p.take()
            for k in range(8):
                u = st.get()
                yield u.toks
                for j in range(4):
                    t = c.mm(bank[32 * j:32 * j + 32, :], cond[:, k, :], u.raw[:, j * 512:j * 512 + 512], k == 0, k == 7, u.toks, bw, ct)
                st.done(t)
                m["lt"] = u.toks
            m["t"][q] = e = c.tt(c.V, sb[:, :], bank[:, :], br[:, :], ALU.add, t, g.all, sb.w)
            self.p.give(bank, e)
            c.mem.give(br, e)
            yield e
            bank, bw = self.p.take()
            for b in range(4):
                t = c.tr(bank[:, b * 128:b * 128 + 128], sb[:, b * 128:b * 128 + 128], e, bw, c.eye_t)
            v = bank[:, :].rearrange("p (b j r) -> p j b r", b=4, j=4)
            e = [c.cp(c.V, m["col"][i][:, q * 16:q * 16 + 16].rearrange("p (j b) -> p j b", j=4), v[:, :, :, i], t, m["col"][i].w) for i in range(2)]
            self.p.give(bank, e)
            m["ct"][q] = e
            if name == "m1" and q == 2:
                c.mem.give(cond, t)
            if q == 0:
                c.mem.give(sb, t)
            if q < 2:
                yield

    def gate(self, m, which, seg, dst):
        toks = []
        for h in range(2):
            r = 32 * ((seg % 2) * 2 + h) + which
            o, i, t = dst[:, h * 512:h * 512 + 512], m["sb"][seg // 2], m["t"][seg // 2]
            if which == 0:
                src = i[r:r + 1, :]
                toks.append(self.G(lambda e, o=o, src=src: e.partition_broadcast(o, src), t, dst.w))
                self.G(None, toks)
                continue
            bank, bw = self.p.take()
            t = self.mm(bank[:, :], self.eye[:, 0, r:r + 1].to_broadcast([128, 128]), i[:, :], True, True, t, bw, self.eye_t)
            e = self.cp(self.A, o, bank[:, :], t, dst.w)
            self.p.give(bank, e)
            toks.append(e)
        return toks


def load_rows(c, name, dst, q=None):
    g = c.group(name)
    (q or c.S).dma(g, dst[:, :, :], c.d[name].rearrange("o (t p) n -> p (o t) n", p=128), dst.w)
    return g.all


def setup(c):
    d, mem, T, V, A, G, S = c.d, c.mem, c.T, c.V, c.A, c.G, c.S
    c.mods = {}
    c.small = mem.take("small", [288])
    c.junk, c.junk_t = mem.take("junk", [512]), []
    c.root, c.root_t = mem.take("root", [1]), []
    c.vec = mem.take("vec", [168])
    c.eye = mem.take("eye", [4, 128])
    c.eps = c.small[:, 32:33]
    c.x = mem.take("x", [2, 1024])
    r0, r1, r2 = mem.take("r0", [128], parts=32), mem.take("r1", [128]), mem.take("r2", [128], parts=40)
    g0, g = c.group("g0"), c.group("vec")
    S.dma(g0, r0[:, :], d["rows"][0:32, :])
    S.dma(g0, c.eye[:, :, :], d["k_eye"])
    A.dma(g0, c.small[:, :], d["k_small"])
    c.eye_t = g0.all
    A.dma(g, r1[0:120, :], d["rows"][32:152, :], c.set(V, r1[:, :], 0.0, r1.w))
    A.dma(g, r2[:, :], d["rows"][152:192, :], r2.w)
    c.rows = (r1, r2, g)
    c.col, at = {}, 0
    for name, n in (("n1", 8), ("n2", 8), ("b_in", 52), ("cw", 36), ("cb", 12), ("skip", 4), (None, 8), ("n1_2", 16), ("n2_2", 16), ("sb_2", 8)):
        c.col[name] = at
        at += n
    c.ctx_ = mem.take("ctx", [2, 1024])

    bank, bw = c.p.take()
    t = c.tr(bank[:, 0:32], r0[:, :], g0.all, bw)
    c.conds = []
    for i in range(2):
        s = mem.take(f"cond{i}", [8, 32])
        z = c.set(V, s[:, :, :], 0.0, s.w)
        e = c.act(s[:, :, 0:2].rearrange("p k w -> p w k"), bank[:, 16 * i:16 * i + 16].rearrange("p (w k) -> p w k", w=2), ACT.Silu, t, z)
        c.conds.append((s, e))
    c.p.give(bank, [e for _, e in c.conds])
    mem.give(r0, t)


def vectors(c):
    r1, r2, g = c.rows
    bank, bw = c.p.take()
    c.tr(bank[:, 0:128], r1[:, :], g.all, bw, c.eye_t)
    t = c.tr(bank[:, 128:168], r2[:, :])
    c.vec_t = c.cp(c.V, c.vec[:, :], bank[:, 0:168], t, c.vec.w)
    c.p.give(bank, c.vec_t)
    c.mem.give(r1, t)
    c.mem.give(r2, t)


def column(c, name, n, at=0):
    b = c.col[name] + at
    return c.vec[:, b:b + n]


def scale_shift(c, m, which, seg_shift, seg_scale, gain, name):
    a = c.mem.take(name, [8])
    t = c.stt(c.V, a[:, :], m["col"][which][:, seg_scale * 8:seg_scale * 8 + 8], 1.0, gain, ALU.add, ALU.mult,
              m["ct"][seg_scale // 2], c.vec_t, a.w)
    return a, m["col"][which][:, seg_shift * 8:seg_shift * 8 + 8], [t, m["ct"][seg_shift // 2]]


def sine(c, arg, n, t, out, *w):
    mem, V = c.mem, c.V
    k = mem.take("sink", [256])
    magic = 12582912.0
    c1 = 6.28125
    c2 = float(np.float32(np.round((2 * math.pi - c1) * 2 ** 22) / 2 ** 22))
    c3 = float(np.float32(2 * math.pi - c1 - c2))
    a, kk = arg[0:n, :], k[0:n, :]
    t = c.ts(V, kk, a, 1 / (2 * math.pi), magic, ALU.mult, ALU.add, t, k.w)
    t = c.ts(V, kk, kk, magic, None, ALU.subtract, None, t)
    for cc in (c1, c2, c3):
        t = c.stt(V, a, kk, -cc, a, ALU.mult, ALU.add, t)
    t = c.ts(V, a, a, 3.1415925, -3.1415925, ALU.min, ALU.max, t)
    mem.give(k, t)
    return c.act(out, a, ACT.Sin, t, w)


def filters(c):
    d, mem, V, A, G, S = c.d, c.mem, c.V, c.A, c.G, c.S
    g = c.group("hyf")
    hp = mem.take("hyp", [1411])
    S.dma(g, hp[0:64, :], d["hyp"], hp.w)
    feat, w1, w2, w3, sc = hp[:, 0:256], hp[:, 256:320], hp[:, 320:384], hp[:, 384:1408], hp[:, 1408:1411]
    decay, gd = mem.take("decay", [2, 512]), c.group("decay")
    S.dma(gd, decay[:, :, :], d["k_decay"].rearrange("p (t n) -> p t n", t=2), decay.w)
    yield g.all
    arg = mem.take("harg", [256])
    hid = mem.take("hid", [256])
    t = None
    for w, b, rhs, kk in ((w1, 0, feat, 33), (w2, 1, hid, 64)):
        bank, bw = c.p.take()
        t = c.mm(bank[0:64, 0:256], w[0:kk, :], rhs[0:kk, :], True, True, g.all, bw, t)
        e = c.ts(V, arg[0:64, :], bank[0:64, 0:256], sc[0:64, b:b + 1], sc[0:64, 2:3], ALU.add, ALU.mult, t, arg.w)
        c.p.give(bank, e)
        t = sine(c, arg, 64, e, hid[0:64, :], hid.w)
        yield t if b == 0 else [t, gd.all]
    filt = mem.take("filt", [2, 1024])
    ab = mem.take("fabs", [2, 1024])
    es, ea = [], []
    for tt in range(2):
        for h in range(2):
            bank, bw = c.p.take()
            m = c.mm(bank[:, :], hid[0:64, tt * 128:tt * 128 + 128], w3[0:64, h * 512:h * 512 + 512], True, True, t, bw)
            o = filt[:, tt, h * 512:h * 512 + 512]
            e = c.tt(V, o, bank[:, :], decay[:, tt, :], ALU.mult, m, gd.all, filt.w)
            c.p.give(bank, e)
            es.append(e)
            ea.append(c.act(ab[:, tt, h * 512:h * 512 + 512], o, ACT.Abs, e, ab.w))
    yield ea
    dft, gf = c.dft, c.dft_t
    mem.give(hp, m, es)
    mem.give(arg, t)
    mem.give(hid, m)
    mem.give(decay, es)
    inv = mem.take("finv", [8])
    bank, bw = c.p.take()
    for j in range(8):
        for tt in range(2):
            m = c.mm(bank[:, j:j + 1], ab[:, tt, j * 128:j * 128 + 128], c.eye[:, 2, 0:1], tt == 0, tt == 1, ea, bw)
    mem.give(ab, m)
    er = c.recip(inv[:, :], bank[:, 0:8], m, inv.w)
    c.p.give(bank, er)
    yield er
    fn = []
    for h in range(2):
        bank, bw = c.p.take()
        for j in range(4):
            m = c.mm(bank[:, j * 128:j * 128 + 128], inv[:, 4 * h + j:4 * h + j + 1].to_broadcast([128, 128]), c.eye[:, 0, :], True, True, er, bw)
        for tt in range(2):
            o = filt[:, tt, h * 512:h * 512 + 512]
            fn.append(c.tt(V, o, o, bank[:, :], ALU.mult, m, es))
        c.p.give(bank, fn[-2:])
    mem.give(inv, m)
    sm = mem.take("fsum", [2, 2, 512])
    hs = [c.tt(V, sm[:, i, :, :], filt[:, :, 0:512], filt[:, :, 512:1024], op, fn, sm.w) for i, op in enumerate((ALU.add, ALU.subtract))]
    mem.give(filt, hs)
    yield [hs, gf]
    c.hf = mem.take("hf", [5, 512])
    c.hf_t = []
    for i, (blk, s) in enumerate(((0, 0), (1, 0), (2, 1), (3, 1), (5, 0))):
        bank, bw = c.p.take()
        for k in range(2):
            m = c.mm(bank[:, :], dft[:, blk, k, :], sm[:, s, k, :], k == 0, k == 1, hs, bw, gf)
        e = c.cp(A, c.hf[:, i, :], bank[:, :], m, c.hf.w)
        c.p.give(bank, e)
        c.hf_t.append(e)
        yield
    mem.give(sm, m)


def hyena(c, u, ut):
    d, mem, V, A, G = c.d, c.mem, c.V, c.A, c.G
    cv = mem.take("conv", [12, 256])
    ct = []
    for k in range(12):
        o = cv[:, k, :]
        w = lambda j: column(c, "cw", 1, 12 * j + k)
        t = c.ts(V, o, u[:, k, 1:257], w(1), column(c, "cb", 1, k), ALU.mult, ALU.add, ut[k], cv.w, c.vec_t)
        t = c.stt(V, o, u[:, k, 0:256], w(0), o, ALU.mult, ALU.add, t)
        t = c.stt(V, o, u[:, k, 2:258], w(2), o, ALU.mult, ALU.add, t)
        ct.append(t)
        if k % 4 == 3:
            yield
    mem.give(u, ct)
    z = cv[:, 4:8, :]
    zt = c.tt(V, z, z, cv[:, 8:12, :], ALU.mult, ct)
    yield zt
    ztok = mem.take("ztok", [2, 512])
    e = []
    for t in range(2):
        bank, bw = c.p.take()
        for k in range(4):
            m = c.tr(bank[:, k * 128:k * 128 + 128], cv[:, 4 + k, t * 128:t * 128 + 128], zt, bw)
        e.append(c.cp(A, ztok[:, t, :], bank[:, :], m, ztok.w))
        c.p.give(bank, e[-1])
    yield e
    zf = mem.take("zf", [4, 512])
    ez = []
    for i, blk in enumerate((0, 1, 4, 3)):
        bank, bw = c.p.take()
        for k in range(2):
            m = c.mm(bank[:, :], c.dft[:, blk, k, :], ztok[:, k, :], k == 0, k == 1, e, bw, c.dft_t)
        ez.append(c.cp(A, zf[:, i, :], bank[:, :], m, zf.w))
        c.p.give(bank, ez[-1])
    mem.give(ztok, m)
    yield lambda: when(c.hf_t) if len(c.hf_t) == 5 else LATER
    mem.give(c.dft, m)
    yc, ys = mem.take("yc", [2, 512]), mem.take("ys", [2, 512])
    tmp = mem.take("yt", [2, 512])
    hr, hi = c.hf[:, 0:2, :], c.hf[:, 2:4, :]
    zc, zs = zf[:, 0:2, :], zf[:, 2:4, :]
    a = c.tt(V, yc[:, :, :], zc, hr, ALU.mult, ez, c.hf_t, yc.w)
    b = c.tt(G, tmp[:, :, :], zs, hi, ALU.mult, ez, c.hf_t, tmp.w)
    y1 = c.tt(V, yc[:, :, :], yc[:, :, :], tmp[:, :, :], ALU.subtract, a, b)
    b = c.tt(G, tmp[:, :, :], zc, hi, ALU.mult, ez, c.hf_t, y1)
    a0 = c.tt(V, ys[:, 0, :], zf[:, 2, :], c.hf[:, 4, :], ALU.mult, ez, c.hf_t, ys.w)
    a1 = c.tt(V, ys[:, 1, :], zf[:, 3, :], c.hf[:, 1, :], ALU.mult, ez, c.hf_t, ys.w)
    y2 = c.tt(V, ys[:, :, :], ys[:, :, :], tmp[:, :, :], ALU.add, a0, a1, b)
    mem.give(zf, y1, y2)
    mem.give(c.hf, y1, y2)
    mem.give(tmp, y1, y2)
    idft = mem.take("idft", [4, 256])
    g = c.group("idft")
    G.dma(g, idft[:, :, :], d["k_idft"].rearrange("p (b t) -> p b t", b=4), idft.w)
    yield [y1, y2, g.all]
    done = []
    out = c.hy = c.operand("hy", [4, 256], True)
    tmp = mem.take("hyt", [2, 256])
    for k in range(4):
        bank, bw = c.p.take()
        for i in range(4):
            m = c.mm(bank[:, 0:256], (yc, ys)[i // 2][:, i % 2, k * 128:k * 128 + 128], idft[:, i, :], i == 0, i == 3, y1, y2, bw, g.all)
        o = tmp[:, k % 2, :]
        e = c.stt(V, o, cv[:, 4 + k, :], column(c, "skip", 1, k), bank[:, 0:256], ALU.mult, ALU.add, m, tmp.w, done[-2:])
        c.p.give(bank, e)
        e = c.tt(V, o, o, cv[:, k, :], ALU.mult, e)
        done.append(c.part(out, slice(k, k + 1), o.unsqueeze(1), e))
        yield
    mem.give(tmp, done)
    mem.give(yc, m)
    mem.give(ys, m)
    mem.give(idft, m)
    mem.give(cv, done)


def decays(c):
    d, mem, V, A, S = c.d, c.mem, c.V, c.A, c.S
    g = c.group("retlog")
    lg = mem.take("lg", [8])
    w = mem.take("lgw", [5, 8])
    ret = mem.take("kret", [1024])
    S.dma(g, lg[:, :], d["ret_decay_logit"].rearrange("o a h -> o (a h)").to_broadcast([128, 8]), lg.w)
    yield g.all
    e, u, dd, z, s = (w[:, i, :] for i in range(5))
    t = c.act(e, lg[:, :], ACT.Abs, g.all, w.w)
    t = c.act(e, e, ACT.Exp, t, scale=-1.0)
    yield t
    t = c.ts(V, u, e, 1.0, None, ALU.add, None, t, w.w)
    yield t
    t1 = c.act(s, u, ACT.Ln, t, w.w)
    yield t1
    t = c.ts(V, dd, u, -1.0, None, ALU.add, None, t, w.w)
    tz = c.ts(V, z, dd, 0.0, None, ALU.is_equal, None, t, w.w)
    t = c.tt(V, dd, dd, z, ALU.add, tz)
    t = c.recip(dd, dd, t)
    t = c.tt(V, dd, dd, s, ALU.mult, t, t1)
    t = c.tt(V, dd, dd, z, ALU.add, t)
    t = c.tt(V, dd, dd, e, ALU.mult, t)
    t = c.stt(V, lg[:, :], lg[:, :], 0.0, dd, ALU.min, ALU.subtract, t)
    mem.give(w, t)
    yield
    c.dk = mem.take("dk", [2, 4, 2])
    c.dq = mem.take("dq", [2, 4, 2])
    c.dm = mem.take("dm", [4, 512])
    c.dk_t, c.dq_t, c.dm_t = [], [], []
    for h in range(4):
        for i in range(2):
            l = lg[:, i * 4 + h:i * 4 + h + 1]
            c.dk_t.append(c.act(c.dk[:, i, h, :], c.small[:, 50 + 2 * i:52 + 2 * i], ACT.Exp, t, c.dk.w, scale=l))
            c.dq_t.append(c.act(c.dq[:, i, h, :], c.small[:, 54 + 2 * i:56 + 2 * i], ACT.Exp, t, c.dq.w, scale=l))
        yield c.dq_t[-1]
    c.dk_t = [c.ts(V, c.dk[:, :, :, :], c.dk[:, :, :, :], 128.0 ** -0.5, None, ALU.mult, None, c.dk_t)]
    c.dk_made = True
    g = c.group("kret")
    S.dma(g, ret[:, :], d["k_ret"], ret.w)
    yield g.all
    last = []
    for h in range(4):
        o = c.dm[:, h, :]
        t1 = c.ts(V, o, ret[:, 0:512], lg[:, h:h + 1], None, ALU.mult, None, t, g.all, c.dm.w)
        t1 = c.stt(V, o, ret[:, 512:1024], lg[:, 4 + h:5 + h], o, ALU.mult, ALU.add, t1)
        last.append(t1)
        c.dm_t.append(c.act(o, o, ACT.Exp, t1))
        yield c.dm_t[-1]
    mem.give(ret, last)
    mem.give(lg, last, c.dq_t, c.dk_t)


def states(c, kc, kct, vc, vct):
    mem, V, A, G = c.mem, c.V, c.A, c.G
    yield lambda: when(c.dk_t) if c.dk_made else LATER
    c.st = mem.take("st", [4, 2, 256])
    c.st_t = []
    kd = mem.take("kd", [2, 2, 2, 128])
    last = [[], []]
    for h in range(4):
        b = h % 2
        kt = []
        for i in range(2):
            for t in range(2):
                kt.append(c.ts(V, kd[:, b, i, t, :], kc[:, t, h * 128:h * 128 + 128], c.dk[:, i, h, t:t + 1], None, ALU.mult, None,
                               kct, c.dk_t, kd.w, last[b]))
        yield kt
        bank, bw = c.p.take()
        for i in range(2):
            for t in range(2):
                m = c.mm(bank[:, i * 256:i * 256 + 256], kd[:, b, i, t, :], vc[:, t, h * 256:h * 256 + 256], t == 0, t == 1, kt, vct, bw)
        last[b] = m
        e = c.cp(A, c.st[:, h, :, :], bank[:, :].rearrange("p (i v) -> p i v", i=2), m, c.st.w)
        c.p.give(bank, e)
        c.st_t.append(e)
    mem.give(kd, last)
    mem.give(kc, kt)
    mem.give(vc, m)
    mem.give(c.dk, kt)


def turn_heads(c, x, xt, rope, rt, out):
    V, G = c.V, c.G
    toks = []
    for p in range(2):
        bank, bw = c.p.take()
        for h in range(2):
            m = c.mm(bank[:, h * 256:h * 256 + 256], rope[:, 512:640], x[:, 2 * p + h, :], True, True, xt[2 * p + h], rt, bw)
        o, i = out[:, 2 * p:2 * p + 2, :], x[:, 2 * p:2 * p + 2, :]
        sin = rope[:, 256:512].unsqueeze(1).to_broadcast([128, 2, 256])
        cos = rope[:, 0:256].unsqueeze(1).to_broadcast([128, 2, 256])
        e = c.tt(V, o, bank[:, :].rearrange("p (h t) -> p h t", h=2), sin, ALU.mult, m, rt, out.w)
        c.p.give(bank, e)
        f = c.tt(V, i, i, cos, ALU.mult, xt[2 * p:2 * p + 2], rt, m)
        toks.append(c.tt(V, o, o, i, ALU.add, e, f))
        yield
    c.turned_t = toks


def retention(c, q, qt, k, kt, v, vt, o):
    d, mem, V, A, G = c.d, c.mem, c.V, c.A, c.G
    rope = mem.take("rope", [640])
    g = c.group("rope")
    G.dma(g, rope[:, :], d["k_rope"], rope.w)
    qr = mem.take("qr", [4, 256])
    kr = mem.take("kr", [4, 256])
    yield g.all
    yield from turn_heads(c, k, kt, rope, g.all, kr)
    krt = c.turned_t
    mem.give(k, krt)
    yield from turn_heads(c, q, qt, rope, g.all, qr)
    qrt = c.turned_t
    mem.give(q, qrt)
    mem.give(rope, qrt)
    yield lambda: when(krt, qrt, vt, c.st_t, c.dm_t) if len(c.st_t) == 4 and len(c.dm_t) == 4 else LATER
    sc = mem.take("rsc", [2, 512])
    c.oss = mem.take("oss", [8])
    junk = mem.take("ojunk", [2, 256])
    c.o_t, c.oss_t = [], []
    last = [[], []]
    js = [[], []]
    for h in range(4):
        b = h % 2
        bank, bw = c.p.take()
        for j in range(2):
            m = c.mm(bank[:, j * 256:j * 256 + 256], kr[:, h, j * 128:j * 128 + 128], qr[:, h, :], True, True, krt, qrt, bw)
        e = c.stt(V, sc[:, b, :], bank[:, :], 128.0 ** -0.5, c.dm[:, h, :], ALU.mult, ALU.mult, m, c.dm_t[h], sc.w, last[b])
        c.p.give(bank, e)
        yield e
        bank, bw = c.p.take()
        for t in range(2):
            out = bank[:, t * 256:t * 256 + 256]
            for j in range(2):
                m = c.mm(out, sc[:, b, j * 256 + t * 128:j * 256 + t * 128 + 128], v[:, j, h * 256:h * 256 + 256], j == 0, j == 1, e, vt, bw)
        ci = c.cp(A, o[:, :, h * 256:h * 256 + 256], bank[:, :].rearrange("p (t v) -> p t v", t=2), m, o.w)
        c.p.give(bank, ci)
        last[b] = m
        yield c.st_t[h]
        es = []
        for t in range(2):
            bank, bw = c.p.take()
            m = c.mm(bank[:, :], qr[:, h, t * 128:t * 128 + 128], c.st[:, h, :, :], True, True, c.st_t[h], bw)
            x, y = o[:, t, h * 256:h * 256 + 256], ci
            for i in range(2):
                y = c.stt(V, x, bank[:, i * 256:i * 256 + 256], c.dq[:, i, h, t:t + 1], x, ALU.mult, ALU.add, m, y, c.dq_t)
            c.p.give(bank, y)
            es.append(y)
            a = c.act(junk[:, t, :], x, ACT.Square, y, junk.w, c.oss.w, js[t], accum=c.oss[:, t * 4 + h:t * 4 + h + 1])
            js[t] = [a]
            c.oss_t.append(a)
        c.o_t += es
        yield
    mem.give(junk, c.oss_t)
    mem.give(sc, m)
    mem.give(qr, m)
    mem.give(kr, m)
    mem.give(v, m)
    mem.give(c.st, m)
    mem.give(c.dq, es)
    mem.give(c.dm, e)


def first_stream(c):
    d = c.d
    w = d["w_in"][0]
    cols = [3072 + 256 * i for i in range(6)] + [512, 768, 1024, 1280, 1536, 1792] + [0, 256] + [2048 + 256 * i for i in range(4)] + [4608 + 256 * i for i in range(8)]
    items = [by_cols(w, c0) for c0 in cols]
    hw, rw, wo = d["hy_w_o"][0], d["ret_w_o"][0], d["w_out"][0]
    for n in range(2):
        items.append((hw[:, n * 512:n * 512 + 512].rearrange("(k p) c -> p k c", p=128), [lambda v: v[:, :, 0:256], lambda v: v[:, :, 256:512]]))
        items += [by_cols(rw, n * 512 + 256 * i) for i in range(2)]
    items += [by_rows(wo, n * 256) for n in range(4)]
    return Stream(c, items, True, 2, 1)


def first_mix(c):
    d, mem, V, A, G, S = c.d, c.mem, c.V, c.A, c.G, c.S
    w, b_in = d["w_in"][0], d["b_in"]
    m = c.mods["m1"]
    ctx = c.ctx_
    ax, shx, st = scale_shift(c, m, 0, 0, 1, column(c, "n1", 8), "ax")
    h = c.operand("h", [8, 256], True)
    c.moved_rows(c.scaled_x, ax, shx, h, st, between=c.first.prime)
    mem.give(ax, h.all)
    jobs, st = c.early, c.first

    def to_heads(dst, toks, base, b0):
        def evac(i, ps, t):
            e = c.act(dst[:, base + i, :], ps, ACT.Identity, t, dst.w, c.vec_t, bias=column(c, "b_in", 1, b0 + base + i))
            toks.append(e)
            return e
        return evac
    u = mem.take("u", [12, 258], top=True)
    uz = c.set(G, u[:, :, 0:258:257], 0.0, u.w)
    ut = [None] * 12

    def to_u(base):
        def evac(i, ps, t):
            k = base + i
            ut[k] = [c.act(u[:, k, 1:257], ps, ACT.Identity, t, u.w, uz, c.vec_t, bias=column(c, "b_in", 1, 24 + k))]
            return ut[k]
        return evac
    for n in range(6):
        c.unit(st, 2, [("cols", h, to_u(2 * n))])
        if n == 1:
            rc = Rows(ctx, c.ctx_t)
            run(c.squares(rc))
            oc = c.inverse(rc, "oc")
            ac, shc, sct = scale_shift(c, m, 1, 0, 1, column(c, "n1", 8), "ac")
        if n == 2:
            hc = c.operand("hc", [8, 256], True)
            c.turned_rows(rc, *oc, ac, shc, hc, sct)
            mem.give(oc[0], c.pe_last())
            mem.give(ctx, c.pe_last())
            mem.give(ac, hc.all)
        jobs.go(3)
        yield
    jobs.add(hyena(c, u, ut))
    long = jobs.list[-1]
    kT = mem.take("kT", [4, 256])
    kc = mem.take("kc", [2, 512])
    bias = mem.take("bias", [1536])
    gb = c.group("bias")
    G.dma(gb, bias[:, :], b_in[0:1, 512:2048].to_broadcast([128, 1536]), bias.w)
    kt, qt, kct, vct, vt = [], [], [], [], []

    def to_tok(dst, toks, base, boff):
        def evac(t, ps, tok):
            e = c.tt(V, dst[:, t, base:base + 256], ps, bias[:, boff:boff + 256], ALU.add, tok, gb.all, dst.w)
            toks.append(e)
            return e
        return evac
    for n in range(2):
        c.unit(st, 2, [("cols", h, to_heads(kT, kt, 2 * n, 4)), ("toks", hc, to_tok(kc, kct, 256 * n, 256 * n))])
        jobs.go(3)
        yield
    vc = mem.take("vc", [2, 1024])
    v = mem.take("v", [2, 1024])
    tx = []
    for n in range(4):
        c.unit(st, 2, [("toks", hc, to_tok(vc, vct, n * 256, 512 + n * 256)), ("toks", h, to_tok(v, tx, n * 256, 512 + n * 256))])
        jobs.go(3)
        yield
    vt.extend(tx)
    c.drop(hc, c.last_mm)
    mem.give(bias, vt, vct, kct)
    jobs.add(states(c, kc, kct, vc, vct))
    qT = mem.take("qT", [4, 256])
    for n in range(2):
        c.unit(st, 2, [("cols", h, to_heads(qT, qt, 2 * n, 0))])
        jobs.go(3)
        yield
    o = mem.take("o", [2, 1024])
    ogT = Op()

    def readout():
        yield from retention(c, qT, qt, kT, kt, v, vt, o)
        r = c.rstd(c.oss[:, :], c.oss[:, :], 256.0, c.oss_t)
        yield lambda: when(r, sgt) if len(sgt) == 8 else LATER
        og = []
        for hh in range(4):
            for t in range(2):
                s = slice(hh * 256, hh * 256 + 256)
                og.append(c.stt(V, o[:, t, s], o[:, t, s], c.oss[:, t * 4 + hh:t * 4 + hh + 1], sg[:, t, s], ALU.mult, ALU.mult, r, sgt, c.o_t))
            if hh % 2:
                yield og
        mem.give(c.oss, og)
        mem.give(sg, og)
        x = c.operand("ogT", [8, 256], True)
        ogT.hi, ogT.lo = x.hi, x.lo
        tmp = [mem.take("ogt", [2, 256], top=True) for _ in range(2)]
        last = [[], []]
        for k2 in range(4):
            bank, bw = c.p.take()
            for k in range(2):
                for t in range(2):
                    kk = (2 * k2 + k) * 128
                    mt = c.tr(bank[:, k * 256 + t * 128:k * 256 + t * 128 + 128], o[:, t, kk:kk + 128], og[2 * k2 + t], bw)
            b = k2 % 2
            e = c.cp(A if b else V, tmp[b][:, :, :], bank[:, :].rearrange("p (k t) -> p k t", k=2), mt, tmp[b].w, last[b])
            c.p.give(bank, e)
            last[b] = [c.part(ogT, slice(2 * k2, 2 * k2 + 2), tmp[b][:, :, :], e)]
            yield
        for b in range(2):
            mem.give(tmp[b], last[b])
        mem.give(o, mt)
    while not long.over:
        long.step()
    jobs.tidy()
    jobs.add(readout())
    sg = mem.take("sg", [2, 1024])
    bias2 = mem.take("bias2", [1024])
    gb2 = c.group("bias2")
    G.dma(gb2, bias2[:, :], b_in[0:1, 2048:3072].to_broadcast([128, 1024]), bias2.w)
    sgt, sga = [], []

    def to_sg(n):
        def evac(t, ps, tok):
            s = slice(n * 256, n * 256 + 256)
            e = c.tt(V, sg[:, t, s], ps, bias2[:, s], ALU.add, tok, gb2.all, sg.w)
            sga.append(e)
            sgt.append(c.act(sg[:, t, s], sg[:, t, s], ACT.Silu, e))
            return e
        return evac
    for n in range(4):
        c.unit(st, 2, [("toks", h, to_sg(n))])
        jobs.go(3)
        yield
    mem.give(bias2, sga)
    gr = [None, None]
    grt = [[None] * 8, [None] * 8]

    def to_gate(i, base):
        if base == 0:
            gr[i] = mem.take(f"gate{i}", [8, 256])

        def evac(k, ps, t):
            grt[i][base + k] = c.act(gr[i][:, base + k, :], ps, ACT.Sigmoid, t, gr[i].w, c.vec_t, bias=column(c, "b_in", 1, 36 + 8 * i + base + k))
            return grt[i][base + k]
        return evac
    for n in range(8):
        c.unit(st, 2, [("cols", h, to_gate(n // 4, 2 * (n % 4)))])
        jobs.go(3)
        yield
    c.drop(h, c.last_mm)
    for _ in jobs.drain():
        pass
    mixed = c.operand("mixed", [8, 256], True)
    mx = [None] * 8
    mh = [None] * 8

    def to_hy(base):
        def evac(k, ps, t):
            kk = base + k
            o_ = gr[1][:, kk, :]
            mh[kk] = c.tt(V, o_, ps, o_, ALU.mult, t, grt[1][kk])
            return mh[kk]
        return evac

    def to_mix(base):
        def evac(k, ps, t):
            kk = base + k
            o_ = gr[0][:, kk, :]
            e = c.tt(V, o_, ps, o_, ALU.mult, t, grt[0][kk])
            mx[kk] = c.tt(V, o_, o_, gr[1][:, kk, :], ALU.add, e, mh[kk])
            mx[kk] = c.part(mixed, slice(kk, kk + 1), o_.unsqueeze(1), mx[kk])
            return e
        return evac
    second_start(c)
    for n in range(2):
        for i in range(2):
            c.unit(st, 1, [("cols", c.hy, to_hy(4 * n + 2 * i))])
            yield
        for i in range(2):
            c.unit(st, 2, [("cols", ogT, to_mix(4 * n + 2 * i))])
            yield
    c.drop(c.hy, c.last_mm)
    c.drop(ogT, c.last_mm)
    mem.give(gr[0], mx)
    mem.give(gr[1], mx)
    gt = mem.take("gt1", [1024])
    gtt = c.gate(m, 0, 2, gt)
    mem.give(m["sb"][1], gtt)
    acc, sums = c.accumulators(), c.sums()
    yield from c.add_rows(st, mixed, 8, acc, True, True)
    c.added(c.rows_x, acc, gt, gtt, sums)
    c.drop(mixed, c.last_mm)
    mem.give(gt, c.rows_x.all)


def first_hot(c, eq, n, base, out, t):
    mem, V = c.mem, c.V
    cand = mem.take("cand", [2, n])
    mn = mem.take("cmin", [2])
    t = c.stt(V, cand[:, :, :], eq, -64.0, base.unsqueeze(1).to_broadcast([128, 2, n]), ALU.mult, ALU.add, t, cand.w, c.eye_t)
    t = c.red(mn[:, :], cand[:, :, :], ALU.min, t, mn.w)
    t = c.tt(V, out, cand[:, :, :], mn[:, :].unsqueeze(2).to_broadcast([128, 2, n]), ALU.is_equal, t)
    mem.give(cand, t)
    mem.give(mn, t)
    return t


def route(c, h2):
    d, mem, V, A, G = c.d, c.mem, c.V, c.A, c.G
    rw, rb, rt = c.rw, c.rb, c.rw_t
    L = mem.take("logits", [2, 36])
    banks, lt = [c.p.take() for _ in range(2)], []
    for k in range(8):
        for t, (bank, bw) in enumerate(banks):
            m = c.mm(bank[:, 0:36], h2.raw[:, k, t * 128:t * 128 + 128], rw[:, k, :], k == 0, k == 7, h2.at(k), rt, bw)
            if k == 7:
                lt.append(c.tt(V, L[:, t, :], bank[:, 0:36], rb[:, :], ALU.add, m, L.w, rt))
                c.p.give(bank, lt[t])
    mem.give(rw, m)
    mem.give(rb, lt)
    gl, el = L[:, :, 0:4], L[:, :, 4:36].rearrange("p t (g e) -> p t e g", g=4)
    w = mem.take("rtw", [2, 96])
    iota = c.small[:, 0:32]
    gx, eq, oh = w[:, :, 0:4], w[:, :, 4:8], w[:, :, 8:12]
    one = lambda i: w[:, :, 12 + i]
    bc = lambda a, n: a.unsqueeze(2).to_broadcast([128, 2, n])
    gm, ps, m1, m2, e2, w1, w2, sm = (one(i) for i in range(8))
    t = c.red(gm, gl, ALU.max, lt, w.w)
    t1 = c.tt(V, gx, gl, bc(gm, 4), ALU.subtract, t)
    t2 = c.tt(V, eq, gl, bc(gm, 4), ALU.is_equal, t)
    ex = c.act(gx, gx, ACT.Exp, t1)
    to = first_hot(c, eq, 4, iota[:, 0:4], oh, t2)
    t = c.red(ps, gx, ALU.add, ex)
    ts = t
    pr = mem.take("prod", [2, 8, 4])
    t = c.tt(V, pr[:, :, :, :], el, oh.unsqueeze(2).to_broadcast([128, 2, 8, 4]), ALU.mult, to, pr.w, lt)
    ing, eq1, oh1, oh2 = (w[:, :, 24 + 8 * i:32 + 8 * i] for i in range(4))
    t = c.red(ing, pr[:, :, :, :], ALU.add, t)
    mem.give(pr, t)
    mem.give(L, t)
    t = c.red(m1, ing, ALU.max, t)
    t = c.tt(V, eq1, ing, bc(m1, 8), ALU.is_equal, t)
    to1 = first_hot(c, eq1, 8, iota[:, 0:8], oh1, t)
    t = c.stt(V, ing, oh1, NEG, ing, ALU.mult, ALU.add, to1)
    t = c.red(m2, ing, ALU.max, t)
    t2 = c.tt(V, e2, m2, m1, ALU.subtract, t)
    x2 = c.act(e2, e2, ACT.Exp, t2)
    t = c.tt(V, eq1, ing, bc(m2, 8), ALU.is_equal, t)
    to2 = first_hot(c, eq1, 8, iota[:, 0:8], oh2, t)
    ab = mem.take("assign", [3, 2, 32])
    a1, a2, al = (ab[:, i, :, :] for i in range(3))
    c.wt = mem.take("wt", [2, 32])
    c.rk = mem.take("rk", [2, 32])
    as3 = lambda a, t: a[:, t, :].rearrange("p (g e) -> p g e", g=4)
    ta, tw = [], []
    for i in range(2):
        o4 = oh[:, i, :].unsqueeze(2).to_broadcast([128, 4, 8])
        s1 = c.tt(V, as3(a1, i), o4, oh1[:, i, :].unsqueeze(1).to_broadcast([128, 4, 8]), ALU.mult, to, to1, ab.w)
        s2 = c.tt(V, as3(a2, i), o4, oh2[:, i, :].unsqueeze(1).to_broadcast([128, 4, 8]), ALU.mult, to2, ab.w)
        ta.append(c.tt(V, al[:, i, :], a1[:, i, :], a2[:, i, :], ALU.add, s1, s2))
    c.fill(1, True)
    bank, bw = c.p.take()
    c.mm(bank[:, 0:32], c.eye[:, 1, :], al[:, 0, :], True, True, ta, bw)
    c.mm(bank[:, 32:64], c.eye[:, 2, :], al[:, 0, :], True, False)
    c.mm(bank[:, 32:64], c.eye[:, 1, :], al[:, 1, :], False, True)
    c.mm(bank[:, 64:96], c.eye[:, 2, :], al[:, 0, :], True, False)
    m = c.mm(bank[:, 64:96], c.eye[:, 2, :], al[:, 1, :], False, True)
    t = c.stt(V, c.rk[:, :, :], bank[:, 0:64].rearrange("p (t e) -> p t e", t=2), 1.0, al, ALU.add, ALU.mult, m, c.rk.w)
    c.rk_t = c.ts(V, c.rk[:, :, :], c.rk[:, :, :], -1.0, None, ALU.add, None, t)

    def weigh():
        tp = c.recip(ps, ps, ts)
        t = c.ts(V, sm, e2, 1.0, None, ALU.add, None, x2)
        t = c.recip(sm, sm, t)
        tw1 = c.tt(V, w1, ps, sm, ALU.mult, t, tp)
        tw2 = c.tt(V, w2, w1, e2, ALU.mult, tw1)
        for i in range(2):
            s = c.ts(V, c.wt[:, i, :], a1[:, i, :], w1[:, i:i + 1], None, ALU.mult, None, ta, tw2, c.wt.w)
            tw.append(c.stt(V, c.wt[:, i, :], a2[:, i, :], w2[:, i:i + 1], c.wt[:, i, :], ALU.mult, ALU.add, s))
        c.wt_t = tw
        mem.give(ab, c.rk_t, tw)
        mem.give(w, tw)

    def counts():
        c.cnt = mem.take("cnt", [33])
        tc = c.cp(V, c.cnt[:, 0:32], bank[:, 64:96], m, c.cnt.w)
        t_ = c.red(c.cnt[:, 32:33], c.cnt[:, 0:32], ALU.max, tc)
        c.cnti = mem.take("cnti", [1], I32)
        c.cnt_t = c.cp(V, c.cnti[:, :], c.cnt[:, 32:33], t_, c.cnti.w)
        c.p.give(bank, t, tc)
    c.weigh, c.counts = weigh, counts


def experts_stream(c):
    w1, w3, w2 = (c.d[n][0] for n in ("expert_w1", "expert_w3", "expert_w2"))
    items = []
    for g in range(8):
        items += [(w[4 * g:4 * g + 4, k * 128:k * 128 + 128, :].rearrange("e p f -> p e f"), [lambda v: v]) for k in range(8) for w in (w1, w3)]
        items += [(w2[4 * g:4 * g + 4, k * 128:k * 128 + 128, h * 512:h * 512 + 512].rearrange("e p f -> p e f"), [lambda v: v]) for h in range(2) for k in range(4)]
    return Stream(c, items, False, 0, 6)


def experts(c, st, r, xn, xnt, ax, shx, axt, gated):
    mem, V, A = c.mem, c.V, c.A
    iota = c.small[:, 0:32].unsqueeze(1).to_broadcast([128, 4, 32])
    P = mem.take("P", [2, 2, 128])
    xg, pw = [], []
    last_x, last_pw, last_P = [[], []], [[], []], []

    def pick(g):
        pt, ws = [], []
        for t in range(2):
            sel, wgt = (P[:, i, t, :].rearrange("p (e s) -> p e s", e=4) for i in range(2))
            e = c.tt(V, sel, c.rk[:, t, 4 * g:4 * g + 4].unsqueeze(2).to_broadcast([128, 4, 32]), iota, ALU.is_equal, c.rk_t, P.w, last_P)
            pt.append(e)
        if g == 0:
            c.weigh()
        for t in range(2):
            sel, wgt = (P[:, i, t, :].rearrange("p (e s) -> p e s", e=4) for i in range(2))
            ws.append(c.tt(V, wgt, sel, c.wt[:, t, 4 * g:4 * g + 4].unsqueeze(2).to_broadcast([128, 4, 32]), ALU.mult, pt[t], c.wt_t))
        return pt, ws

    def prepare(g, pt, ws):
        b = g % 2
        if g < 2:
            xg.append(mem.take("xg", [8, 128]))
            pw.append(mem.take("pw", [256]))
        es = []
        for k4 in range(2):
            bank, bw = c.p.take()
            for k in range(4):
                o = bank[:, k * 128:k * 128 + 128]
                kk = k4 * 4 + k
                for t in range(2):
                    m = c.mm(o, xn[:, t, kk * 128:kk * 128 + 128], P[:, 0, t, :], t == 0, t == 1, xnt, pt, bw)
            ev = []
            for k in range(4):
                o, kk = bank[:, k * 128:k * 128 + 128], k4 * 4 + k
                if k4:
                    ev.append(c.act(xg[b][:, kk, :], o, ACT.Identity, m, axt, xg[b].w, last_x[b], scale=ax[:, kk:kk + 1], bias=shx[:, kk:kk + 1]))
                else:
                    ev.append(c.ts(V, xg[b][:, kk, :], o, ax[:, kk:kk + 1], shx[:, kk:kk + 1], ALU.mult, ALU.add, m, axt, xg[b].w, last_x[b]))
            c.p.give(bank, ev)
            es += ev
        bank, bw = c.p.take()
        for t in range(2):
            m = c.tr(bank[:, t * 128:t * 128 + 128], P[:, 1, t, :], ws[t], bw)
        e = c.cp(A, pw[b][:, :], bank[:, 0:256], m, pw[b].w, last_pw[b])
        c.p.give(bank, e)
        last_P[:] = [m]
        return es, e
    picked = pick(0)
    yield picked
    ready = prepare(0, *picked)
    c.counts()
    yield ready
    xt = r.t
    hl, hTl, yl = [], [], [[], []]
    for g in range(8):
        (xe, pwt), xb = ready, xg[g % 2]
        b1, w1w = c.p.take()
        b3, w3w = c.p.take()
        for k in range(8):
            for bank, bw in ((b1, w1w), (b3, w3w)):
                u = st.get()
                for j in range(4):
                    m = c.mm(bank[32 * j:32 * j + 32, :], xb[:, k, 32 * j:32 * j + 32], u.raw[:, j, :], k == 0, k == 7, u.toks, xe[k], bw)
                st.done(m)
                if k > 2 and c.extra:
                    c.extra -= 1
                    st.deep -= 1
                    c.less_slots(1)
            if (g, k) == (0, 6):
                tables(c)
            if (g, k) == (1, 0):
                crowded(c)
            if k == 3 and g < 7:
                picked = pick(g + 1)
            yield
        last_x[g % 2] = [m]
        if g == 0:
            sl, hT, y = mem.take("mh", [2, 512]), mem.take("mhT", [4, 128]), mem.take("my", [2, 512])
            gt, gtt = gated()
        e1 = c.act(sl[:, 0, :], b1[:, :], ACT.Silu, m, sl.w, hl)
        e3 = c.tt(V, sl[:, 1, :], sl[:, 0, :], b3[:, :], ALU.mult, e1, m)
        c.p.give(b1, e1)
        c.p.give(b3, e3)
        if g < 7:
            ready = prepare(g + 1, *picked)
        yield e3
        bank, bw = c.p.take()
        for k in range(4):
            m = c.tr(bank[:, k * 128:k * 128 + 128], sl[:, 1, k * 128:k * 128 + 128], e3, bw)
        hl = [m]
        e = c.cp(A, hT[:, :, :], bank[:, :].rearrange("p (k s) -> p k s", k=4), m, hT.w, hTl)
        c.p.give(bank, e)
        yield e
        for h in range(2):
            bank, bw = c.p.take()
            for k in range(4):
                u = st.get()
                for j in range(4):
                    m = c.mm(bank[32 * j:32 * j + 32, :], hT[:, k, 32 * j:32 * j + 32], u.raw[:, j, :], k == 0, k == 3, u.toks, e, bw)
                st.done(m)
                if k % 2:
                    yield
            hTl = [m]
            ey = c.tt(V, y[:, h, :], bank[:, :], gt[:, h * 512:h * 512 + 512], ALU.mult, m, gtt, y.w, yl[h])
            c.p.give(bank, ey)
            yield ey
            for t in range(2):
                bank, bw = c.p.take()
                m = c.mm(bank[:, :], pw[g % 2][:, t * 128:t * 128 + 128], y[:, h, :], True, True, ey, pwt, bw)
                o = c.x[:, t, h * 512:h * 512 + 512]
                xt[t, h] = c.tt(V, o, o, bank[:, :], ALU.add, m, xt[t, h])
                c.p.give(bank, xt[t, h])
            yl[h] = [m]
        last_pw[g % 2] = [m]
    mem.give(P, last_P)
    for i in range(2):
        mem.give(xg[i], last_x[i])
        mem.give(pw[i], m)
    mem.give(sl, hl)
    mem.give(hT, hTl)
    mem.give(y, yl)


def crowded(c):
    c.most = {}
    for q in (c.T, c.V, c.A, c.S):
        def fn(e, w, q=q):
            for t in w:
                e.wait_ge(*t.resolve())
            c.most[id(q)] = e.value_load(c.cnti[0:1, 0:1], min_val=0, max_val=256)
        q.raw(fn, c.cnt_t)


def beyond(c, xn, ax, shx, gt):
    d, mem, nc = c.d, c.mem, c.nc
    w1, w3, w2 = (d[n][0] for n in ("expert_w1", "expert_w3", "expert_w2"))
    N = 224
    wa, wb = ([mem.take("ow", [4, 512]) for _ in range(2)] for _ in range(2))
    y, hh, XT, P, pwT, tmp = (mem.take("o" + n, s) for n, s in (
        ("y", [2, 1024]), ("hh", [2, 4, N]), ("XT", [8, N]), ("P", [2, 2, N]), ("pwT", [2, 256]), ("tmp", [2, 2, 32])))
    bufs = (*wa, *wb, y, hh, XT, P, pwT, tmp)
    wc = [b[:, :, :].rearrange("p (k h) n -> p k (h n)", h=2) for b in wa]
    before = flat([b.w for b in bufs]) + [Tok(q, len(q.ops) - 1, q.now) for q in (c.T, c.V, c.A)]
    sv, sp, sa, sd = (c.sem("over_" + n) for n in "vpad")
    bk = c.banks
    slots = ((0, 128), (128, 96))
    iota = c.small[:, 64:288]

    def enter(e, w):
        for t in w:
            e.wait_ge(*t.resolve())

    def leave(e):
        e.wait_ge(sv, 32 * 7 + 1)

    def vec(e, w):
        with e.If(c.most[id(c.V)] > 32):
            enter(e, w)
            e.sem_inc(sv, 1)
            with e.Fori(0, 32) as i:
                e.wait_ge(sv, i * 7 + 1)
                for t in range(2):
                    e.tensor_scalar(P[:, 0, t, :], iota, c.rk[:, t, 0:1], None, ALU.is_equal)
                    m = e.tensor_scalar(P[:, 1, t, :], iota, c.rk[:, t, 0:1], c.wt[:, t, 0:1], ALU.is_equal, ALU.mult)
                m.then_inc(sv, 1)
                e.wait_ge(sp, i * 4 + 2)
                for k in range(8):
                    e.tensor_scalar(XT[:, k, :], bk[k // 2][:, (k % 2) * N:(k % 2) * N + N], ax[:, k:k + 1], shx[:, k:k + 1], ALU.mult, ALU.add)
                e.tensor_copy(pwT[:, 0, :], bk[4][:, 0:256])
                e.tensor_copy(pwT[0:96, 1, :], bk[4][0:96, 256:512]).then_inc(sv, 1)
                e.wait_ge(sa, i + 1)
                for h in range(2):
                    m = e.tensor_tensor(hh[:, 1, 2 * h:2 * h + 2, :], hh[:, 0, 2 * h:2 * h + 2, :],
                                        bk[(7 + h) % 8][:, 0:2 * N].rearrange("p (f s) -> p f s", f=2), ALU.mult)
                m.then_inc(sv, 1)
                e.wait_ge(sp, i * 4 + 4)
                for s, (_, n) in enumerate(slots):
                    for h in range(2):
                        m = e.tensor_tensor(y[0:n, s, h * 512:h * 512 + 512], bk[1 + 2 * s + h][0:n, :], gt[0:n, h * 512:h * 512 + 512], ALU.mult)
                m.then_inc(sv, 1)
                e.wait_ge(sp, i * 4 + 5)
                for t in range(2):
                    for h in range(2):
                        o = c.x[:, t, h * 512:h * 512 + 512]
                        m = e.tensor_tensor(o, o, bk[(5 + 2 * t + h) % 8][:, :], ALU.add)
                m.then_inc(sv, 1)
                e.tensor_copy(tmp[:, 0, :, 0:31], c.rk[:, :, 1:32])
                e.tensor_copy(tmp[:, 1, :, 0:31], c.wt[:, :, 1:32]).then_inc(sv, 1)
                e.wait_ge(sv, i * 7 + 7)
                e.tensor_copy(c.rk[:, :, 0:31], tmp[:, 0, :, 0:31])
                e.tensor_copy(c.wt[:, :, 0:31], tmp[:, 1, :, 0:31]).then_inc(sv, 1)
            leave(e)

    def pe(e, w):
        with e.If(c.most[id(c.T)] > 32):
            enter(e, w)
            e.sem_inc(sp, 1)
            with e.Fori(0, 32) as i:
                e.wait_ge(sv, i * 7 + 2)
                for k in range(8):
                    for t in range(2):
                        e.matmul(bk[k // 2][:, (k % 2) * N:(k % 2) * N + N], xn[:, t, k * 128:k * 128 + 128], P[:, 0, t, :], start=t == 0, stop=t == 1)
                for s, (s0, n) in enumerate(slots):
                    for t in range(2):
                        m = e.transpose(bk[4][0:n, s * 256 + t * 128:s * 256 + t * 128 + 128], P[:, 1, t, s0:s0 + n], c.eye[:, 0, :])
                m.then_inc(sp, 1)
                e.wait_ge(sv, i * 7 + 3)
                e.wait_ge(sd, i * 96 + 64)
                for b, wt in ((5, wa), (7, wb)):
                    for f in range(4):
                        for k in range(8):
                            m = e.matmul(bk[(b + f // 2) % 8][:, (f % 2) * N:(f % 2) * N + N], wt[k // 4][:, k % 4, f * 128:f * 128 + 128], XT[:, k, :], start=k == 0, stop=k == 7)
                m.then_inc(sp, 1)
                e.wait_ge(sv, i * 7 + 4)
                e.wait_ge(sd, i * 96 + 96)
                for s, (s0, n) in enumerate(slots):
                    for h in range(2):
                        for f in range(4):
                            m = e.matmul(bk[1 + 2 * s + h][0:n, :], hh[:, 1, f, s0:s0 + n], wc[f // 2][:, f % 2, h * 512:h * 512 + 512], start=f == 0, stop=f == 3)
                m.then_inc(sp, 1)
                e.wait_ge(sv, i * 7 + 5)
                for t in range(2):
                    for h in range(2):
                        for s, (_, n) in enumerate(slots):
                            m = e.matmul(bk[(5 + 2 * t + h) % 8][:, :], pwT[0:n, s, t * 128:t * 128 + 128], y[0:n, s, h * 512:h * 512 + 512], start=s == 0, stop=s == 1)
                m.then_inc(sp, 1)
            leave(e)

    def act(e, w):
        with e.If(c.most[id(c.A)] > 32):
            enter(e, w)
            with e.Fori(0, 32) as i:
                e.wait_ge(sp, i * 4 + 3)
                for h in range(2):
                    m = e.activation(hh[:, 0, 2 * h:2 * h + 2, :], bk[5 + h][:, 0:2 * N].rearrange("p (f s) -> p f s", f=2), ACT.Silu)
                m.then_inc(sa, 1)
            leave(e)

    def sp_(e, w):
        with e.If(c.most[id(c.S)] > 32):
            enter(e, w)
            with e.Fori(0, 32) as i:
                e.wait_ge(sp, i * 4 + 1)
                for dst, src in (([b[:, :, :] for b in wa], w1), ([b[:, :, :] for b in wb], w3), (wc, w2)):
                    if src is w2:
                        e.wait_ge(sp, i * 4 + 3)
                    n = src.shape[1] // 2
                    for h in range(2):
                        e.dma_start(dst[h], src[bass.ds(i, 1), h * n:h * n + n, :].rearrange("o (k p) n -> p (o k) n", p=128)).then_inc(sd, 16)
            leave(e)
    for q, fn in ((c.T, pe), (c.V, vec), (c.A, act), (c.S, sp_)):
        q.raw(fn, before)
    done = c.V(lambda e: e.drain())
    for b in bufs:
        mem.give(b, done)
    return done


def tables(c):
    g = c.group("tables")
    c.fft = c.mem.take("fft", [1280])
    c.rope2 = c.mem.take("rope2", [640])
    c.hd = c.mem.take("hd", [128])
    for b, n in ((c.fft, "k_fft"), (c.rope2, "k_rope2"), (c.hd, "k_hd")):
        c.G.dma(g, b[:, :], c.d[n], b.w)
    c.second_t = g.all


def second_consts(c):
    d, mem, V, A, G = c.d, c.mem, c.V, c.A, c.G
    g = c.group("second")
    dl = mem.take("dl", [2, 4, 32])
    for i, n in enumerate(("diff_lq1_2", "diff_lk1_2", "diff_lq2_2", "diff_lk2_2")):
        G.dma(g, dl[:, :, i, :], d[n].rearrange("(o l) n -> o l n", o=1).to_broadcast([128, 2, 32]), dl.w)
    c.lam = mem.take("lam", [2, 2])
    c.subg = mem.take("subg", [2])
    for l in range(2):
        for i in range(2):
            G.dma(g, c.subg[64 * i:64 * i + 64, l:l + 1], d["diff_subln_g_2"][l:l + 1, :].rearrange("o n -> n o"), c.subg.w)
    yield
    t = [c.tt(V, dl[:, :, 2 * i, :], dl[:, :, 2 * i, :], dl[:, :, 2 * i + 1, :], ALU.mult, g.all) for i in range(2)]
    t = [c.red(c.lam[:, i, :], dl[:, :, 2 * i, :], ALU.add, t[i], c.lam.w) for i in range(2)]
    mem.give(dl, t)
    t = c.act(c.lam[:, :, :], c.lam[:, :, :], ACT.Exp, t)
    init = [0.8 - 0.6 * math.exp(-0.3 * l) for l in range(2)]
    t = c.tt(V, c.lam[:, 0, :], c.lam[:, 1, :], c.lam[:, 0, :], ALU.subtract, t)
    c.lam_t, c.subg_t = [], []
    for l in range(2):
        c.lam_t.append(c.ts(V, c.lam[:, 0, l:l + 1], c.lam[:, 0, l:l + 1], -init[l], None, ALU.add, None, t))
        c.subg_t.append(c.ts(V, c.subg[:, l:l + 1], c.subg[:, l:l + 1], 1.0 - init[l], None, ALU.mult, None, g.all))
    yield


def second_start(c):
    c.cx = c.mem.take("cx", [2, 1024])
    c.cx_t = load_rows(c, "ctx_2", c.cx, c.G)
    c.rw, c.rb = c.mem.take("rw", [8, 36]), c.mem.take("rb", [36])
    g = c.group("router")
    c.G.dma(g, c.rw[:, :, 0:4], c.d["router_group_w"][0].rearrange("(k p) n -> p k n", p=128), c.rw.w)
    c.G.dma(g, c.rw[:, :, 4:36], c.d["router_expert_w"][0].rearrange("(k p) n -> p k n", p=128), c.rw.w)
    c.G.dma(g, c.rb[:, 0:4], c.d["router_group_b"].to_broadcast([128, 4]), c.rb.w)
    c.G.dma(g, c.rb[:, 4:36], c.d["router_expert_b"].to_broadcast([128, 32]), c.rb.w)
    c.rw_t = g.all
    c.later = second_consts(c)
    next(c.later)


def attend(c, q, qt, nb, keys, vals, bias, lam, evac, dots=None):
    mem, V, A = c.mem, c.V, c.A
    nk, w = 256 * len(vals), 64 // nb
    R = 3
    P = [[mem.take("ap", [nk], top=True) for _ in range(nb)] for _ in range(R)]
    pt = [mem.take("apt", [nk // 128, 256], top=True) for _ in range(2)]
    st = [mem.take("ast", [2 * nb], top=True) for _ in range(R)]
    last_p, last_t, last_s = [[[] for _ in range(nb)] for _ in range(R)], [[], []], [[] for _ in range(R)]
    pe, es = [None] * R, [[], []]

    def scores(i):
        h, t, r = i // 2, i % 2, i % R
        pair, hh = h // 2, h % 2
        s, pe[r] = st[r], []
        for b in range(nb):
            bank, bw = c.p.take()
            if dots:
                m = dots(h, t, b, bank, bw)
            for k, (kb, kt) in enumerate([] if dots else keys):
                with_bias = bias is not None and k == 0
                o = bank[:, k * 256:k * 256 + 256]
                own = slice((hh * nb + b) * w, (hh * nb + b) * w + w)
                m = c.mm(o, q[own, pair, t * 128:t * 128 + 128], kb[own, pair, :], True, not with_bias, qt, kt, bw)
                if with_bias:
                    m = c.mm(o, c.eye[:, 3, :], bias[0][:, h, t, :], False, True, bias[1])
            x = c.red(s[:, b:b + 1], bank[:, 0:nk], ALU.max, m, s.w, last_s[r], negate=True)
            e = c.act(P[r][b][:, :], bank[:, 0:nk], ACT.Exp, x, P[r][b].w, last_p[r][b], bias=s[:, b:b + 1], accum=s[:, nb + b:nb + b + 1])
            c.p.give(bank, e)
            pe[r].append(e)

    def weigh(i):
        r = i % R
        s, p = st[r], P[r]
        f = c.recip(s[:, nb:2 * nb], s[:, nb:2 * nb], pe[r])
        e = c.ts(V, p[0][:, :], p[0][:, :], s[:, nb:nb + 1], None, ALU.mult, None, f)
        if nb == 2:
            f = c.tt(V, s[:, nb + 1:nb + 2], s[:, nb + 1:nb + 2], lam[0], ALU.mult, f, lam[1])
            e = c.stt(V, p[0][:, :], p[1][:, :], s[:, nb + 1:nb + 2], p[0][:, :], ALU.mult, ALU.add, e, f)
            last_p[r][1] = [e]
        last_s[r] = [e]
        return e

    def weights(i, e):
        h, t, r = i // 2, i % 2, i % R
        p = P[r]
        bank, bw = c.p.take()
        for k in range(nk // 128):
            m = c.tr(bank[:, k * 128:k * 128 + 128], p[0][:, k * 128:k * 128 + 128], e, bw)
        last_p[r][0] = [m]
        b = h % 2
        e = c.cp(A, pt[b][:, :, t * 128:t * 128 + 128], bank[:, 0:nk].rearrange("p (k q) -> p k q", q=128), m, pt[b].w, last_t[b])
        c.p.give(bank, e)
        es[b] = es[b] + [e] if t else [e]

    def values(pair):
        bank, bw = c.p.take()
        for k in range(nk // 128):
            vb, vt = vals[k // 2]
            for hh in range(2):
                h = 2 * pair + hh
                m = c.mm(bank[64 * hh:64 * hh + 64, 0:256], vb[:, k % 2, h * 64:h * 64 + 64], pt[hh][:, k, :], k == 0, k == nk // 128 - 1, es, vt, bw)
        last_t[:] = [m], [m]
        c.p.give(bank, evac(pair, bank[:, 0:256], m))
    yield qt
    for i in range(R - 1):
        scores(i)
        yield
    for i in range(8):
        if i + R - 1 < 8:
            scores(i + R - 1)
        e = weigh(i)
        if i == 4:
            values(0)
        yield e
        weights(i, e)
        yield
    yield es
    values(1)
    for r in range(R):
        for b in range(nb):
            mem.give(P[r][b], last_p[r][b])
        mem.give(st[r], last_s[r])
    for r in range(2):
        mem.give(pt[r], last_t[r])


IN_COLS = (1536, 1792, 2048, 1024, 1280, 512, 768, 256, 0)
OUT_ROWS = (4, 6, 0, 2)


def layer_streams(c, l, split, ahead, deep, then=None):
    d = c.d
    up, down = d["w_ff1_2"][l], d["w_ff2_2"][l]
    last = [by_cols(up, c0) for c0 in (0, 256)]
    for b in range(8):
        if b < 7:
            last += [by_cols(up, c0) for c0 in (b * 512 + 512, b * 512 + 768)]
        last += [by_rows(down, r0) for r0 in (b * 512, b * 512 + 256)]
    ffn = Stream(c, last, split, ahead, deep, then)
    out = Stream(c, [by_rows(d["w_out_2"][l], k * 128) for k in OUT_ROWS], split, ahead, deep, ffn)
    return Stream(c, [by_cols(d["w_in_2"][l], c0) for c0 in IN_COLS], split, ahead, deep, out), out, ffn


def mixers(c, l, h, own, kv, streams, name, split, late):
    d, mem, V, A, G = c.d, c.mem, c.V, c.A, c.G
    st, sto, stf = streams
    outs, jobs = {}, Jobs(c)

    def made(k, n, src, *toks):
        b = k // 2 * 2
        if b not in outs:
            outs[b] = c.operand(name + "y", [2, 256], split, top=True)
        return c.place(outs[b], slice(k - b, k - b + n), src, toks)

    def project():
        for i, k in enumerate(OUT_ROWS):
            need = OUT_ROWS if own else (k,)
            while any(b not in outs or len(outs[b].by) < 2 for b in need):
                yield lambda: when(outs[k].all) if all(b in outs and len(outs[b].by) == 2 for b in need) else LATER
            if i == 0:
                c.acc = c.accumulators()
            if i == 3:
                c.acc_sums = c.sums()
            yield from c.add_rows(sto, outs[k], 2, c.acc, i == 0, i == 3)
            c.drop(outs[k], c.last_mm)

    def new(n, shape, top=False):
        b = mem.take(name + n, shape, top=top)
        b.toks = []
        return b

    def keep(b, scale=None):
        def evac(i, ps, t):
            o = b[:, i, :]
            if scale is None:
                e = c.cp(V if i else A, o, ps, t, b.w)
            else:
                e = c.ts(V, o, ps, scale, None, ALU.mult, None, t, b.w) if i else c.act(o, ps, ACT.Identity, t, b.w, scale=scale)
            b.toks.append(e)
            return e
        return evac
    if not own:
        rp = d["na_rpb_2"]
        bias = new("bias", [4, 2, 256])
        mask = new("mask", [256])
        gb = c.group(name + "bias")
        for hh in range(4):
            for t in range(2):
                for r in range(2):
                    off = ((l * 4 + hh) * 15 + 6 - 2 * t + r) * 31 - 48
                    G.dma(gb, bias[64 * r:64 * r + 64, hh, t, :].rearrange("p (i k) -> p i k", i=4),
                          bass.AP(tensor=rp.tensor, offset=off, ap=[[1, 64], [31, 4], [1, 64]]), bias.w)
        G.dma(gb, mask[:, :], d["k_mask"][:, 0:256], mask.w)
        bt = c.tt(G, bias[:, :, :, :].rearrange("p h t k -> p (h t) k"), bias[:, :, :, :].rearrange("p h t k -> p (h t) k"),
                  mask[:, :].unsqueeze(1).to_broadcast([128, 8, 256]), ALU.add, gb.all)
        mem.give(mask, bt)
    dq, dk, dv = (new(n, [2, 256]) for n in ("dq", "dk", "dv"))
    for kind, evac in (("cols", keep(dq, 32.0 ** -0.5)), ("cols", keep(dk)), ("toks", keep(dv))):
        yield from c.halves(st, 2, [(kind, h, evac)])
        jobs.go(1)
        yield

    def spin(x):
        bank, bw = c.p.take()
        out = new("spun", [2, 256])
        for i in range(2):
            m = c.mm(bank[:, i * 256:i * 256 + 256], c.rope2[:, 512:640], x[:, i, :], True, True, x.toks, c.second_t, bw)
        cos = c.rope2[:, 0:256].unsqueeze(1).to_broadcast([128, 2, 256])
        sin = c.rope2[:, 256:512].unsqueeze(1).to_broadcast([128, 2, 256])
        e = c.tt(V, out[:, :, :], bank[:, :].rearrange("p (i t) -> p i t", i=2), sin, ALU.mult, m, out.w)
        c.p.give(bank, e)
        f = c.tt(V, x[:, :, :], x[:, :, :], cos, ALU.mult, m)
        out.toks.append(c.tt(V, out[:, :, :], out[:, :, :], x[:, :, :], ALU.add, e, f))
        mem.give(x, out.toks)
        return parted(out)

    def parted(x):
        hi, lo = (mem.take(name + n, [2, 256], F32R) for n in ("hi", "lo"))
        t = c.cp(A, hi[:, :, :], x[:, :, :], x.toks, hi.w)
        e = c.tt(V, lo[:, :, :], x[:, :, :], hi[:, :, :].bitcast(F32), ALU.subtract, t, lo.w)
        mem.give(x, e)
        return (hi, t), (lo, e)

    def parts_dots(q, ks, nb, bias=None):
        def dots(h, t, b, bank, bw):
            w = 64 // nb
            pair, own = h // 2, slice(64 * (h % 2) + w * b, 64 * (h % 2) + w * b + w)
            for i, k in enumerate(ks):
                more = bias is not None and i == 0
                for n, ((x, tx), (y, ty)) in enumerate(((q[0], k[0]), (q[0], k[1]), (q[1], k[0]))):
                    m = c.mm(bank[:, i * 256:i * 256 + 256], x[own, pair, t * 128:t * 128 + 128], y[own, pair, :], n == 0, n == 2 and not more, tx, ty, bw)
                if more:
                    m = c.mm(bank[:, 0:256], c.eye[:, 3, :], bias[0][:, h, t, :], False, True, bias[1])
            return m
        return dots

    def differential():
        dots = None
        if not own:
            kx = parted(kv["dk"])
            yield dq.toks + dk.toks
            kl, ql = spin(dk), spin(dq)
            dots, ready = parts_dots(ql, (kl, kx), 2), [ql[0][1], kl[0][1]]
        od = new("od", [2, 256], True)
        sq = new("osq", [2, 256], True)

        def out(pair, ps, t):
            e = c.cp(A, od[:, pair, :], ps, t, od.w)
            sq.toks.append(c.act(sq[:, pair, :], od[:, pair, :], ACT.Square, e, sq.w))
            od.toks.append(e)
            return e
        if own:
            keys, vals = [(dk, dk.toks)], [(dv, dv.toks)]
        else:
            keys, vals = None, [(dv, dv.toks), (kv["dv"], kv["dv"].toks)]
        yield from attend(c, dq, dq.toks if own else ready, 2, keys, vals, None, (c.lam[:, 0, l:l + 1], c.lam_t[l]), out, dots)
        e = c.pe_last()
        if own:
            mem.give(dq, e)
        else:
            for b_ in (dv, kv["dv"], *(x[0] for x in kx + kl + ql)):
                mem.give(b_, e)
        yield sq.toks
        z = new("oz", [2, 2, 2])
        bank, bw = c.p.take()
        for t in range(2):
            for i in range(2):
                m = c.mm(bank[:, 4 * t + 2 * i:4 * t + 2 * i + 2], sq[:, i, t * 128:t * 128 + 128], c.hd[:, 0:128:64], True, True, sq.toks, bw, c.second_t)
        mem.give(sq, m)
        t = c.act(z[:, :, :, :], bank[:, 0:8].rearrange("p (t i h) -> p t i h", t=2, i=2), ACT.Sqrt, m, z.w, bias=c.eps, scale=1.0 / 64)
        c.p.give(bank, t)
        f = c.recip(z[:, :, :, :], z[:, :, :, :], t)
        yield f
        bank, bw = c.p.take()
        for t in range(2):
            for i in range(2):
                for hh in range(2):
                    m = c.mm(bank[64 * hh:64 * hh + 64, i * 256 + t * 128:i * 256 + t * 128 + 128],
                             z[:, t, i, hh:hh + 1].to_broadcast([128, 64]), c.eye[:, 0, :], True, True, f, bw)
        mem.give(z, m)
        e = c.stt(V, od[:, :, :], od[:, :, :], c.subg[:, l:l + 1], bank[:, :].rearrange("p (i t) -> p i t", i=2), ALU.mult, ALU.mult, m, od.toks, c.subg_t[l])
        c.p.give(bank, e)
        e = made(6, 2, od[:, :, :], e)
        mem.give(od, e)
    jobs.add(differential())
    ln = new("ln", [2, 256])
    ws = new("ws", [4, 128])
    gl = c.group(name + "ln")
    G.dma(gl, ln[:, 0, :], d["sgu_ln_g_2"][l:l + 1, :].to_broadcast([128, 256]), ln.w)
    G.dma(gl, ln[:, 1, :], d["sgu_ln_b_2"][l:l + 1, :].to_broadcast([128, 256]), ln.w)
    G.dma(gl, ws[:, :, :], d["sgu_w_2"][l].rearrange("g p q -> p g q"), ws.w)

    uv = new("uv", [2, 512])

    def to_uv(n):
        def evac(t, ps, tok):
            e = c.act(uv[:, t, n * 256:n * 256 + 256], ps, ACT.Gelu_apprx_tanh, tok, uv.w)
            uv.toks.append(e)
            return e
        return evac
    for n in range(2):
        yield from c.halves(st, 2, [("toks", h, to_uv(n))])
        jobs.go(1)
        yield

    def gating():
        s_ = new("lst", [4])
        t0 = []
        t = c.red(s_[:, 0:2], uv[:, :, 256:512], ALU.add, uv.toks, s_.w)
        t = c.ts(V, s_[:, 0:2], s_[:, 0:2], -1.0 / 256, None, ALU.mult, None, t)
        sqb = new("lsq", [2, 256], True)
        for i in range(2):
            e = c.ts(V, uv[:, i, 256:512], uv[:, i, 256:512], s_[:, i:i + 1], None, ALU.add, None, t)
            t0.append(c.act(sqb[:, i, :], uv[:, i, 256:512], ACT.Square, e, sqb.w, s_.w, accum=s_[:, 2 + i:3 + i]))
        r = c.rstd(s_[:, 2:4], s_[:, 2:4], 256.0, t0)
        mem.give(sqb, t0)
        et = []
        for i in range(2):
            o = uv[:, i, 256:512]
            e = c.stt(V, o, o, s_[:, 2 + i:3 + i], ln[:, 0, :], ALU.mult, ALU.mult, r, gl.all)
            et.append(c.tt(V, o, o, ln[:, 1, :], ALU.add, e))
        mem.give(s_, et)
        mem.give(ln, et)
        wT = new("wsT", [4, 128], True)
        bank, bw = c.p.take()
        for g_ in range(4):
            m = c.tr(bank[:, g_ * 128:g_ * 128 + 128], ws[:, g_, :], gl.all, bw)
        e = c.cp(A, wT[:, :, :], bank[:, :].rearrange("p (g q) -> p g q", g=4), m, wT.w)
        c.p.give(bank, e)
        mem.give(ws, m)
        yield [e] + et
        bank, bw = c.p.take()
        for g_ in range(4):
            m = c.mm(bank[:, g_ * 128:g_ * 128 + 128], wT[:, g_, :], uv[:, :, 256 + g_ * 64:320 + g_ * 64], True, True, e, et, bw)
        mem.give(wT, m)
        es = []
        for g_ in range(4):
            u_ = uv[:, :, g_ * 64:g_ * 64 + 64]
            es.append(c.stt(V, u_, bank[:, g_ * 128:g_ * 128 + 128].rearrange("p (t n) -> p t n", t=2), column(c, "sb_2", 1, l * 4 + g_), u_, ALU.add, ALU.mult, m, c.vec_t))
        c.p.give(bank, es)
        yield es
        bank, bw = c.p.take()
        for i in range(2):
            for t_ in range(2):
                m = c.tr(bank[:, i * 256 + t_ * 128:i * 256 + t_ * 128 + 128], uv[:, t_, i * 128:i * 128 + 128], es, bw)
        e = made(4, 2, bank[:, :].rearrange("p (i t) -> p i t", i=2), m)
        c.p.give(bank, e)
        mem.give(uv, m)
    jobs.add(gating())
    jobs.add(project())
    nq, nk, nv = (new(n, [2, 256]) for n in ("nq", "nk", "nv"))
    yield from c.halves(st, 2, [("cols", h, keep(nk))])
    jobs.go()
    yield
    yield from c.halves(st, 2, [("toks", h, keep(nv))])
    jobs.go()
    yield

    yield from c.halves(st, 2, [("cols", h, keep(nq, 0.125))])
    jobs.go()
    yield

    def window():
        def out(pair, ps, t):
            return made(2 + pair, 1, ps.unsqueeze(1), t)
        if own:
            keys, vals, dots, ready = [(nk, nk.toks)], [(nv, nv.toks)], None, nq.toks
        else:
            keys, vals = None, [(nv, nv.toks), (kv["nv"], kv["nv"].toks)]
            kx, kl = parted(kv["nk"]), parted(nk)
            yield nq.toks
            ql = parted(nq)
            dots, ready = parts_dots(ql, (kl, kx), 1, (bias, bt)), [ql[0][1]]
        yield from attend(c, nq, ready, 1, keys, vals, None, None, out, dots)
        e = c.pe_last()
        if own:
            mem.give(nq, e)
        else:
            for b_ in (bias, nv, kv["nv"], *(x[0] for x in kx + kl + ql)):
                mem.give(b_, e)
    jobs.add(window())
    fa = new("fa", [2, 256])
    yield from c.halves(st, 2, [("toks", h, keep(fa))])
    c.drop(h, c.last_mm)
    jobs.go()
    yield

    def fourier():
        yield fa.toks
        f = [new("ff", [512], True) for _ in range(2)]
        for i in range(2):
            bank, bw = c.p.take()
            for k in range(2):
                m = c.mm(bank[:, :], fa[:, k, i * 128:i * 128 + 128], c.fft[:, k * 512:k * 512 + 512], k == 0, k == 1, fa.toks, c.second_t, bw)
            e = c.cp(A, f[i][:, :], bank[:, :], m, f[i].w)
            c.p.give(bank, e)
            f[i].toks.append(e)
        mem.give(fa, m)
        yield f[0].toks + f[1].toks
        bank, bw = c.p.take()
        for i in range(2):
            for k in range(2):
                m = c.mm(bank[:, i * 256:i * 256 + 256], c.fft[:, 1024 + k * 128:1152 + k * 128], f[i][:, k * 256:k * 256 + 256], k == 0, k == 1, f[i].toks, bw)
        e = made(0, 2, bank[:, :].rearrange("p (i t) -> p i t", i=2), m)
        c.p.give(bank, e)
        for b_ in f:
            mem.give(b_, m)
    jobs.add(fourier())
    late()
    yield from jobs.drain()
    if own:
        kv.update(nk=nk, nv=nv, dk=dk, dv=dv)


def last_keys(c, l, h, kv, st, name):
    c.left = 8
    for k, kind in (("nk", "cols"), ("nv", "toks"), ("dk", "cols"), ("dv", "toks")):
        buf = c.mem.take(name + k, [2, 256])
        buf.toks = []

        def evac(i, ps, t):
            e = c.cp(c.A if i % 2 else c.V, buf[:, i, :], ps, t, buf.w)
            buf.toks.append(e)
            return e
        for _ in c.halves(st, 2, [(kind, h, evac)]):
            c.left -= 1
            yield
        kv[k] = buf
        c.left -= 1
        yield


def ffn(c, h, r, gate, gt, st, name, split, each):
    mem, V, A = c.mem, c.V, c.A
    hid = [c.operand(name + "hid", [4, 256], split) for _ in range(2)]
    rl = mem.take(name + "relu", [4, 256])
    last_h, last_r = [[], []], [[] for _ in range(4)]

    def up(b):
        op = hid[b % 2]
        op.by, op.low = {}, {}

        def relu2(base):
            def evac(i, ps, t):
                k = base + i
                x = rl[:, k, :]
                w = (op.raw or op.hi).w
                e = c.act(x, ps, ACT.Relu, t, rl.w, last_r[k])
                if split:
                    f = c.tt(V, x, x, x, ALU.mult, e)
                    hi, lo = op.hi[:, k, :], op.lo[:, k, :]
                    fh = c.cp(A, hi, x, f, w, last_h[b % 2])
                    f = c.tt(V, lo, x, hi.bitcast(F32), ALU.subtract, fh, op.lo.w, last_h[b % 2])
                    op.came([k], fh, low=f)
                else:
                    f = c.tt(V, op.raw[:, k, :], x, x, ALU.mult, e, w, last_h[b % 2])
                    op.came([k], f)
                last_r[k] = [f]
                return e
            return evac
        for n in range(2):
            yield from c.halves(st, 2, [("cols", h, relu2(2 * n))])
            yield
    yield from up(0)
    acc, sums = c.accumulators(), c.sums()
    for b in range(8):
        if b < 7:
            yield from up(b + 1)
        yield from c.add_rows(st, hid[b % 2], 4, acc, b == 0, b == 7)
        last_h[b % 2] = [c.last_mm]
    c.added(r, acc, gate, gt, sums, each)
    c.drop(h, c.last_mm)
    for i in range(2):
        c.drop(hid[i], last_h[i])
    mem.give(rl, last_r)


def layer(c, l, r, m, which, kv, streams, name, split, each=None, h=None):
    mem = c.mem
    own = which == 1

    def turn(seg, gain, h=None):
        a, sh, at = scale_shift(c, m, which, seg, seg + 1, column(c, gain, 8, 8 * l), name + "a")
        h = h or c.operand(name + "h", [8, 256], split)
        o, ot = r.rms or c.inverse(r, name + "o")
        if own:
            yield ot
        if not own and not r.banks:
            c.fill(1)
        c.turned_rows(r, o, ot, a, sh, h, at, fill=0 if own else 2)
        mem.give(a, h.all)
        mem.give(o, c.pe_last())
        if r.then:
            r.then()
        r.rms = r.then = None
        yield h.at(0)
        return h

    gates = {}

    def need(seg):
        while m["ct"][seg // 2] is None:
            c.fill(1, True)

    def gated(seg):
        need(seg)
        gate = mem.take(name + "g", [1024])
        gates[seg] = gate, c.gate(m, which, seg, gate)
        if not own:
            mem.give(m["sb"][seg // 2], gates[seg][1])
    while m["ct"][0] is None:
        yield
    yield r.all
    h = yield from turn(0, "n1_2", h)
    yield from mixers(c, l, h, own, kv, streams, name, split, lambda: gated(2))
    gate, gt = gates[2]
    c.added(r, c.acc, gate, gt, c.acc_sums)
    mem.give(gate, r.all)
    yield r.all
    gated(5)
    gate, gt = gates[5]
    h = yield from turn(3, "n2_2")
    yield from ffn(c, h, r, gate, gt, streams[2], name, split, each)
    mem.give(gate, r.all)


def context_keys(c, r, st):
    mem = c.mem
    m = c.mods["m3"]
    a, sh, at = scale_shift(c, m, 1, 0, 1, column(c, "n1_2", 8, 8), "c1a")
    h = c.operand("c1h", [8, 256], False)
    o, ot = c.inverse(r, "c1o")
    yield ot
    c.turned_rows(r, o, ot, a, sh, h, at)
    mem.give(o, c.pe_last())
    mem.give(r.buf, c.pe_last())
    mem.give(a, h.all)
    yield
    yield from last_keys(c, 1, h, c.kv[1], st, "c1")
    c.drop(h, c.last_mm)


def gains(c, name, spread=False):
    b, g = c.mem.take("gain", [1024]), c.group(name)
    if spread:
        row = c.mem.take("row", [1024])
        c.S.dma(g, row[0:1, :], c.d[name].rearrange("(o n) -> o n", o=1), row.w)
        t = [c.G(lambda e, h=h: e.partition_broadcast(b[:, h:h + 512], row[0:1, h:h + 512]), g.all, b.w) for h in (0, 512)]
        c.G(None, t)
        c.mem.give(row, t)
        return b, t
    c.S.dma(g, b[:, :], c.d[name].rearrange("(o n) -> o n", o=1).to_broadcast([128, 1024]), b.w)
    return b, g.all


def normed_twice(c, r, gain, gt, between, behind):
    V = c.V
    c.roots()
    y = Rows(c.mem.take("xb", [2, 1024]), [])
    junk = c.mem.take("ysq", [512])
    y.ss = c.mem.take("ss", [2, 2])
    for t in range(2):
        for h in range(2):
            s = slice(h * 512, h * 512 + 512)
            y.t[t, h] = [c.tt(V, y.buf[:, t, s], r.buf[:, t, s], gain[:, s], ALU.mult, r.t[t, h], gt, y.buf.w)]
    e = junk.w
    for t in range(2):
        e = c.squared_sum(junk[:, :], y.buf[:, t, 512:1024], y.ss[:, t, 1:2], y.t[t, 1], y.ss.w, e)
        y.st.append(e)
    c.mem.give(junk, e)
    between()
    c.turn(y)
    run(c.squares(r))
    for t in range(2):
        c.squared(y, t, 0)
    behind()
    m, n = c.mem.take("rms1", [2]), c.mem.take("rms2", [2])
    t1 = c.red(m[:, :], r.ss[:, :, :], ALU.add, r.st, m.w)
    c.mem.give(r.ss, t1)
    t1 = c.ts(V, m[:, :], m[:, :], 1.0 / 1024, EPS, ALU.mult, ALU.add, t1)
    t2 = c.red(n[:, :], y.ss[:, :, :], ALU.add, y.st, n.w)
    c.mem.give(y.ss, t2)
    t2 = c.stt(V, n[:, :], m[:, :], 1024.0 * EPS, n[:, :], ALU.mult, ALU.add, t1, t2)
    t2 = c.act(n[:, :], n[:, :], ACT.Sqrt, t2, scale=1.0 / 1024)
    t2 = c.recip(n[:, :], n[:, :], t2)
    y.rms = n, t2
    turned = [m for _, m in y.banks]

    def scaled():
        e = c.act(m[:, :], m[:, :], ACT.Sqrt, t1)
        e = c.recip(m[:, :], m[:, :], e)
        for t in range(2):
            y.t[t, 0] = y.t[t, 1] = [c.act(y.buf[:, t, :], y.buf[:, t, :], ACT.Identity, e, turned, y.t[t, 0], y.t[t, 1], scale=m[:, t:t + 1])]
        c.mem.give(m, y.all)
    y.then = scaled
    return y


def finish(c, r, gain, gt, out):
    V, A = c.V, c.A
    o = c.mem.take("fin", [2])
    made = [None, None]

    def product(t):
        made[t] = c.tt(V, r.buf[:, t, 512:1024], r.buf[:, t, 512:1024], gain[:, 512:1024], ALU.mult, r.t[t, 1], r.st, gt)

    def root(t):
        e = c.red(o[:, t:t + 1], r.ss[:, t, :], ALU.add, r.st, o.w)
        return c.act(o[:, t:t + 1], o[:, t:t + 1], ACT.Sqrt, e, bias=c.eps, scale=1.0 / 1024)

    def store(t, e):
        e = c.recip(o[:, t:t + 1], o[:, t:t + 1], e)
        a, b = r.buf[:, t, 0:512], r.buf[:, t, 512:1024]
        f = c.act(b, b, ACT.Identity, e, made[t], scale=o[:, t:t + 1])
        e = c.stt(V, a, a, o[:, t:t + 1], gain[:, 0:512], ALU.mult, ALU.mult, e, r.t[t, 0], r.st, gt)
        c.S.dma(c.outs, out[0, t * 128:t * 128 + 128, 512:1024], b, f)
        c.S.dma(c.outs, out[0, t * 128:t * 128 + 128, 0:512], a, e)
    first = []

    def each(t, h):
        if (t, h) == (0, 1):
            product(0)
        if (t, h) == (1, 0):
            first.append(root(0))
        if (t, h) == (1, 1):
            store(0, first[0])
            product(1)
            store(1, root(1))
    return each


def run(gen):
    for _ in gen:
        pass


def together(c, a, b, na, nb, after, left):
    jobs, todo, done = [Job(c, a), Job(c, b)], [na, nb], [0.0, 0.0]
    while not jobs[0].over:
        i = 1 if done[1] * todo[0] <= done[0] * todo[1] else 0
        if jobs[i].at > c.T.now + 0.2 and jobs[1 - i].at < jobs[i].at:
            i = 1 - i
        if c.link.now < c.T.now + 6.0 and jobs[0].at < c.T.now + 0.2:
            i = 0
        if jobs[1].over or c.left <= left:
            i = 0
        n = c.T.busy
        jobs[i].step()
        done[i] += c.T.busy - n
        if after and c.left <= 8:
            after = after()
    while c.left > left:
        jobs[1].step()
    if after:
        after()
    return jobs[1]


def program(nc, d, out):
    with ExitStack() as ctx:
        c = Core(nc, ctx, d)
        mem = c.mem
        c.hf_t, c.st_t, c.dm_t, c.cx_t, c.dk_made = [], [], [], [], False
        c.kv = [{}, {}]
        c.more_slots(5)
        c.more_pairs(3)
        setup(c)
        cond, ct = c.conds[0]
        ada1 = c.ada("m1", d["ada_w"][0], d["ada_b"][0], cond, ct)
        c.extra = 7
        c.early = Jobs(c)
        c.early.add(filters(c))
        c.early.list[0].step()
        x = c.rows_x = Rows(c.x, [])
        mod = Job(c, ada1)
        for i in range(10):
            if i < 8:
                c.early.ahead(mod.at)
            mod.step()
            if i == 0:
                c.early.list[0].step()
            if i == 1:
                x.t = Rows(c.x, load_rows(c, "x", c.x)).t
                g, c.dft = c.group("dft"), mem.take("dft", [6, 2, 128], top=True)
                c.S.dma(g, c.dft[:, :, :, :], d["k_dft"].rearrange("p (b k f) -> p b k f", b=6, k=2), c.dft.w)
                c.dft_t = g.all
            if i == 3:
                vectors(c)
            if i == 4:
                c.early.list[0].step()
                run(c.squares(x))
                rms = c.inverse(x, "rms")
                c.first = first_stream(c)
                c.scaled_x = c.scaled_rows(x, *rms)
                c.early.add(decays(c))
            if i == 5:
                c.turn(c.scaled_x)
                mem.give(c.scaled_x.buf, c.pe_last())
                c.first.preload(2)
            if i == 6:
                c.ctx_t = load_rows(c, "ctx", c.ctx_)
        cond, ct = c.conds[1]
        ada2 = c.ada("m2", d["ada_w_2"][0], d["ada_b_2"][0], cond, ct)
        ada3 = c.ada("m3", d["ada_w_2"][1], d["ada_b_2"][1], cond, ct)
        c.fillers = [Job(c, a) for a in (ada1, ada2, ada3)]

        def beside():
            cx, h = Rows(c.cx, c.cx_t), c.operand("c0h", [8, 256], False)
            for _ in c.squares(cx):
                yield
            yield from layer(c, 0, cx, c.mods["m2"], 1, c.kv[0], wc, "c0", False, h=h)
            yield from context_keys(c, cx, wk)
        wk = Stream(c, [by_cols(d["w_in_2"][1], c0) for c0 in (512, 768, 1792, 2048)], False, 0, 2)
        wc = layer_streams(c, 0, False, 0, 2, wk)
        work = experts_stream(c)
        work.deep += c.extra
        third = lambda: c.mods.get("m3", {"ct": [None]})["ct"][0]
        side, n = beside(), 0
        for _ in first_mix(c):
            n += bool(c.cx_t)
            for _ in range(dict(enumerate((0, 0, 1, 1, 1, 1, 2, 0, 1))).get(n, 0)):
                next(side)
            if n == 2:
                wc[0].preload(2)
            if n == 5:
                early = c.more_slots(3, True)
                work.preload(early)
            if n == 9:
                c.first.preload(2)
                early += c.more_slots(5 + c.extra - early, True)
                work.preload(early)
            while third() is None and c.fill():
                pass
        rest = c.fillers
        c.less_pairs(3)
        c.more_slots(5 - early + c.extra)

        m1 = c.mods["m1"]
        x = c.rows_x
        wc[0].preload(2)
        work.preload(8 + c.extra)
        c.fillers = [Job(c, side)]
        ax, sh, at = scale_shift(c, m1, 0, 3, 4, column(c, "n2", 8), "ax2")
        h2 = c.operand("h2", [8, 256], False)
        o, ot = c.inverse(x, "x2o")
        rows = Rows(mem.take("xn2", [2, 1024]), [])
        xn = rows.buf
        for h in range(2):
            s = slice(h * 512, h * 512 + 512)
            rows.t[0, h] = [c.ts(c.V, xn[:, 0, s], x.buf[:, 0, s], o[:, 0:1], None, ALU.mult, None, ot, x.t[0, h], xn.w)]
            rows.t[1, h] = [c.act(xn[:, 1, s], x.buf[:, 1, s], ACT.Identity, ot, x.t[1, h], xn.w, scale=o[:, 1:2])]
        xt = rows.all
        c.fill(1, True)
        c.turn(rows)
        c.moved_rows(rows, ax, sh, h2, at)
        mem.give(o, xt)
        gate = []

        def gated():
            gate.append(mem.take("gt2", [1024]))
            t = c.gate(m1, 0, 5, gate[0])
            mem.give(m1["sb"][2], t)
            return gate[0], t
        route(c, h2)
        c.drop(h2, c.pe_last())
        more = c.more_slots(1, True)
        c.extra += more
        work.deep += more
        work.preload(8 + c.extra)
        each = experts(c, work, x, xn, xt, ax, sh, at, gated)
        next(each)
        next(each)
        next(each)
        c.fillers = rest
        while third() is None:
            c.fill(1, True)
        c.fillers = []
        next(each)
        run(c.later)
        w1 = layer_streams(c, 1, True, 3, 1)
        w0 = layer_streams(c, 0, True, 3, 1, w1[0])
        gain = []

        def after():
            c.more_pairs(3)
            gain.extend(gains(c, "final_norm_g", True))
            work.then = w0[0]
        c.left = 99
        side = together(c, each, side, 300, 470, after, 2)
        c.less_slots(5)
        c.more_pairs(1)
        w0[0].preload(3)
        x = Rows(c.x, [beyond(c, xn, ax, sh, gate[0])])
        for b in (xn, gate[0], c.rk, c.wt, c.cnt, c.cnti, ax, m1["col"][0], m1["col"][1]):
            mem.give(b, x.all)
        c.fillers = [side] + rest
        mem.clock = lambda: c.T.now
        
        def between():
            w0[0].prime(2)
            c.fill(1, True)

        def behind():
            while not side.over:
                c.fill(1, True)
        y = normed_twice(c, x, *gain, between, behind)
        mem.give(c.x, x.st, *y.all)
        mem.give(gain[0], y.all)
        run(layer(c, 0, y, c.mods["m2"], 0, c.kv[0], w0, "x0", True))
        run(layer(c, 1, y, c.mods["m3"], 0, c.kv[1], w1, "x1", True, finish(c, y, *gains(c, "final_g_2"), out)))

        number([c.T, c.V, c.A, c.G, c.S])
        with nc.Block() as block:
            @block.tensor
            def _(e):
                c.T.play(e)

            @block.vector
            def _(e):
                c.V.play(e)

            @block.scalar
            def _(e):
                c.A.play(e)

            @block.gpsimd
            def _(e):
                c.G.play(e)

            @block.sync
            def _(e):
                c.S.play(e)
                e.wait_ge(c.outs.sem, c.outs.n)
    return c


_INS = ['x', 'c', 'ctx', 'c_ctx', 'ada_w', 'ada_b', 'norm1_g', 'norm2_g', 'w_in', 'b_in', 'ret_decay_logit', 'ret_w_o',
        'hy_conv_w', 'hy_conv_b', 'hy_ffn_w1', 'hy_ffn_b1', 'hy_ffn_freq', 'hy_ffn_w2', 'hy_ffn_b2', 'hy_ffn_w3', 'hy_skip',
        'hy_w_o', 'w_out', 'router_group_w', 'router_group_b', 'router_expert_w', 'router_expert_b', 'expert_w1', 'expert_w3',
        'expert_w2', 'final_norm_g', 'c_2', 'ctx_2', 'c_ctx_2', 'ada_w_2', 'ada_b_2', 'norm1_g_2', 'norm2_g_2', 'w_in_2',
        'w_out_2', 'na_rpb_2', 'sgu_ln_g_2', 'sgu_ln_b_2', 'sgu_w_2', 'sgu_b_2', 'diff_lq1_2', 'diff_lk1_2', 'diff_lq2_2',
        'diff_lk2_2', 'diff_subln_g_2', 'w_ff1_2', 'w_ff2_2', 'final_g_2']


_ROWS = ['c', 'c_ctx', 'c_2', 'c_ctx_2', 'norm1_g', 'norm2_g', 'b_in', 'hy_conv_w', 'hy_conv_b', 'hy_skip', 'norm1_g_2', 'norm2_g_2', 'sgu_b_2']


def arrays(inputs):
    a = {n: np.ascontiguousarray(inputs[n]) for n in _INS} | constants()
    feat, w1, w2, w3 = a["k_feat"], *(a[f"hy_ffn_w{i}"][0] for i in (1, 2, 3))
    pad = [np.zeros((31, n), np.float32) for n in (256, 64)]
    a["hyp"] = np.concatenate([np.concatenate([feat, pad[0]], 0), np.concatenate([w1, pad[1]], 0), w2, w3,
                               a["hy_ffn_b1"].T, a["hy_ffn_b2"].T, a["hy_ffn_freq"].T], 1)
    a["rows"] = np.concatenate([a[n].reshape(-1, 128) for n in _ROWS], 0)
    return a


def kernel(**inputs):
    import concourse.bacc as _bacc
    from concourse import mybir as _mybir
    from concourse.bass_utils import run_bass_kernel_spmd as _run

    nc = _bacc.Bacc("TRN2", target_bir_lowering=False, num_devices=1)
    named, d = {}, {}
    for name, a in arrays(inputs).items():
        named[f"in_{name}_dram"] = a
        d[name] = nc.dram_tensor(f"in_{name}_dram", a.shape, _mybir.dt.from_np(a.dtype), kind="ExternalInput").ap()
    out = nc.dram_tensor("out_0_dram", (1, 256, 1024), _mybir.dt.float32, kind="ExternalOutput").ap()
    program(nc, d, out)
    r = _run(nc, [named], core_ids=[0])
    return r.results[0]["out_0_dram"]
```
